# Optimizing a Trainium2 kernel written in Bass

```python
import math
import jax, jax.numpy as jnp
from jax import lax
import numpy as np

D_MODEL = 1024
BATCH = 1
SEQ = 256
DEPTH = 2

CHUNK = 64
N_META = 16
ROPE_THETA = 10000.0
EPS = 1e-6
A_HEADS = 4
A_DK = 128
A_DV = 128
A_CONV = 4
B_HEADS = 4
B_DH = 128
IDX_HEADS = 8
IDX_DIM = 64
TOPK_MAX = 256
TOPK_DIV = 4
Q_BLOCK = 64
D_FF = 2816
FFN_CONV = 3

A_WIDTH = A_HEADS * A_DV
B_WIDTH = B_HEADS * B_DH
IN_SPLITS = (A_HEADS * A_DK, A_HEADS * A_DK, A_WIDTH, A_WIDTH, A_HEADS, A_HEADS,
             B_WIDTH, B_DH, B_DH, IDX_HEADS * IDX_DIM, IDX_DIM, IDX_HEADS)
IN_COLS = sum(IN_SPLITS)
SPLIT_POINTS = tuple(int(c) for c in np.cumsum(IN_SPLITS)[:-1])


def rms_norm(x, g):
    xf = x.astype(jnp.float32)
    y = xf * lax.rsqrt(jnp.mean(xf * xf, axis=-1, keepdims=True) + EPS)
    return (y * g.astype(jnp.float32)).astype(x.dtype)

def l2_norm(x):
    xf = x.astype(jnp.float32)
    return xf * lax.rsqrt(jnp.sum(xf * xf, axis=-1, keepdims=True) + EPS)

def rope_tables(T, dim):
    inv_freq = 1.0 / (ROPE_THETA ** (jnp.arange(0, dim, 2, dtype=jnp.float32) / dim))
    ang = jnp.arange(T, dtype=jnp.float32)[:, None] * inv_freq[None, :]
    return jnp.cos(ang), jnp.sin(ang)

def apply_rope(x, cos, sin):
    xf = x.astype(jnp.float32)
    x1, x2 = jnp.split(xf, 2, axis=-1)
    c, s = cos[:, None, :], sin[:, None, :]
    return jnp.concatenate([x1 * c - x2 * s, x2 * c + x1 * s], axis=-1).astype(x.dtype)

def causal_dwconv(x, w):
    width = w.shape[0]
    T = x.shape[1]
    xp = jnp.pad(x, ((0, 0), (width - 1, 0), (0, 0)))
    out = xp[:, 0:T] * w[0]
    for i in range(1, width):
        out = out + xp[:, i:i + T] * w[i]
    return out

def gated_deltanet(q, k, v, z, a, b, conv_w, a_log, dt_bias, norm_g):
    f32 = jnp.float32
    Bsz, T, _ = q.shape
    qkv = jax.nn.silu(causal_dwconv(jnp.concatenate([q, k, v], axis=-1), conv_w))
    q, k, v = jnp.split(qkv, [A_HEADS * A_DK, 2 * A_HEADS * A_DK], axis=-1)
    q = l2_norm(q.reshape(Bsz, T, A_HEADS, A_DK)) * (A_DK ** -0.5)
    k = l2_norm(k.reshape(Bsz, T, A_HEADS, A_DK))
    v = v.reshape(Bsz, T, A_HEADS, A_DV).astype(f32)
    g = -jnp.exp(a_log.astype(f32)) * jax.nn.softplus(a.astype(f32) + dt_bias.astype(f32))
    beta = jax.nn.sigmoid(b.astype(f32))
    pad = (-T) % CHUNK
    Tp = T + pad
    N = Tp // CHUNK

    def chunks(t):
        t = jnp.pad(t, ((0, 0), (pad, 0)) + ((0, 0),) * (t.ndim - 2))
        t = t.reshape((Bsz, N, CHUNK) + t.shape[2:])
        return jnp.moveaxis(t, 3, 1)

    qc, kc, vc, gch, bc = chunks(q), chunks(k), chunks(v), chunks(g), chunks(beta)
    gcum = jnp.cumsum(gch, axis=-1)
    pos = jnp.arange(CHUNK)
    incl = pos[:, None] >= pos[None, :]
    strict = pos[:, None] > pos[None, :]
    decay = jnp.exp(jnp.where(incl, gcum[..., :, None] - gcum[..., None, :], -jnp.inf))
    kk = jnp.einsum('bhncd,bhnsd->bhncs', kc, kc)
    m = jnp.where(strict, bc[..., None] * kk * decay, 0.0)
    lhs = m + jnp.eye(CHUNK, dtype=f32)
    rhs = jnp.concatenate([vc * bc[..., None], kc * (bc * jnp.exp(gcum))[..., None]], axis=-1)
    sol = lax.linalg.triangular_solve(lhs, rhs, left_side=True, lower=True, unit_diagonal=True)
    u, w = sol[..., :A_DV], sol[..., A_DV:]
    qk = jnp.einsum('bhncd,bhnsd->bhncs', qc, kc) * decay

    def step(S, inp):
        q_c, k_c, u_c, w_c, g_c, qk_c = inp
        v_new = u_c - jnp.einsum('bhcd,bhde->bhce', w_c, S)
        o = (jnp.einsum('bhcd,bhde->bhce', q_c * jnp.exp(g_c)[..., None], S)
             + jnp.einsum('bhcs,bhse->bhce', qk_c, v_new))
        g_last = g_c[..., -1]
        S = (S * jnp.exp(g_last)[..., None, None]
             + jnp.einsum('bhcd,bhce->bhde', k_c * jnp.exp(g_last[..., None] - g_c)[..., None], v_new))
        return S, o

    xs = tuple(jnp.moveaxis(t, 2, 0) for t in (qc, kc, u, w, gcum, qk))
    S0 = jnp.zeros((Bsz, A_HEADS, A_DK, A_DV), f32)
    _, o = lax.scan(step, S0, xs)
    o = jnp.transpose(o, (1, 0, 3, 2, 4)).reshape(Bsz, Tp, A_HEADS, A_DV)[:, pad:]
    o = rms_norm(o, norm_g) * jax.nn.silu(z.reshape(Bsz, T, A_HEADS, A_DV).astype(f32))
    return o.reshape(Bsz, T, A_WIDTH).astype(z.dtype)

def dsa_attention(q, k, v, iq, ik, iw, q_norm, k_norm, kidx_norm, cos_a, sin_a, cos_i, sin_i):
    f32 = jnp.float32
    Bsz, T, _ = q.shape
    S = T - N_META
    topk = min(TOPK_MAX, S // TOPK_DIV)
    q = apply_rope(rms_norm(q.reshape(Bsz, T, B_HEADS, B_DH), q_norm), cos_a, sin_a)
    k = apply_rope(rms_norm(k.reshape(Bsz, T, 1, B_DH), k_norm), cos_a, sin_a)[:, :, 0]
    iq = apply_rope(iq.reshape(Bsz, T, IDX_HEADS, IDX_DIM), cos_i, sin_i)
    ik = apply_rope(rms_norm(ik.reshape(Bsz, T, 1, IDX_DIM), kidx_norm), cos_i, sin_i)[:, :, 0]
    iw = iw * (IDX_HEADS ** -0.5 * IDX_DIM ** -0.5)
    scale = B_DH ** -0.5

    q_m, k_m, v_m = q[:, :N_META], k[:, :N_META], v[:, :N_META]
    s_mm = jnp.einsum('bqhd,bkd->bhqk', q_m, k_m).astype(f32) * scale
    o_meta = jnp.einsum('bhqk,bkd->bqhd', jax.nn.softmax(s_mm, axis=-1).astype(v.dtype), v_m)

    nb = S // Q_BLOCK
    q_r = q[:, N_META:].reshape(Bsz, nb, Q_BLOCK, B_HEADS, B_DH).swapaxes(0, 1)
    iq_r = iq[:, N_META:].reshape(Bsz, nb, Q_BLOCK, IDX_HEADS, IDX_DIM).swapaxes(0, 1)
    iw_r = iw[:, N_META:].reshape(Bsz, nb, Q_BLOCK, IDX_HEADS).swapaxes(0, 1)
    ik_r = ik[:, N_META:]
    kv_r = jnp.concatenate([k[:, N_META:], v[:, N_META:]], axis=-1)
    key_pos = jnp.arange(S)

    def one_block(args):
        j, qb, iqb, iwb = args
        q_pos = j * Q_BLOCK + jnp.arange(Q_BLOCK)
        limit = (q_pos // CHUNK + 1) * CHUNK
        valid = key_pos[None, :] < limit[:, None]
        logit_i = jnp.einsum('bqhd,bsd->bhqs', iqb, ik_r)
        score = jnp.einsum('bhqs,bqh->bqs', jax.nn.relu(logit_i), iwb).astype(f32)
        score = jnp.where(valid[None], score, -jnp.inf)
        _, sel = lax.top_k(score, topk)
        sel_valid = sel < limit[None, :, None]
        kv_sel = jax.vmap(lambda arr, ix: arr[ix])(kv_r, sel)
        k_sel, v_sel = kv_sel[..., :B_DH], kv_sel[..., B_DH:]
        s_meta = jnp.einsum('bqhd,bmd->bhqm', qb, k_m).astype(f32)
        s_sel = jnp.einsum('bqhd,bqkd->bhqk', qb, k_sel).astype(f32)
        s_sel = jnp.where(sel_valid[:, None], s_sel, -jnp.inf)
        p = jax.nn.softmax(jnp.concatenate([s_meta, s_sel], axis=-1) * scale, axis=-1).astype(v.dtype)
        return (jnp.einsum('bhqm,bmd->bqhd', p[..., :N_META], v_m)
                + jnp.einsum('bhqk,bqkd->bqhd', p[..., N_META:], v_sel))

    o_r = lax.map(one_block, (jnp.arange(nb), q_r, iq_r, iw_r))
    o_r = o_r.swapaxes(0, 1).reshape(Bsz, S, B_HEADS, B_DH)
    return jnp.concatenate([o_meta, o_r], axis=1).reshape(Bsz, T, B_WIDTH)

def hybrid_mixer(n, w_in, conv_a, a_log, dt_bias, a_out_norm, q_norm, k_norm, kidx_norm,
                 w_branch_a, w_branch_b, w_gate, b_gate, w_out, cos_a, sin_a, cos_i, sin_i):
    Bsz, T, D = n.shape
    proj = n @ w_in
    aq, ak, av, az, aa, ab, bq, bk, bv, iq, ik, iw = jnp.split(proj, SPLIT_POINTS, axis=-1)
    o_a = gated_deltanet(aq, ak, av, az, aa, ab, conv_a, a_log, dt_bias, a_out_norm)
    o_b = dsa_attention(bq, bk, bv, iq, ik, iw, q_norm, k_norm, kidx_norm, cos_a, sin_a, cos_i, sin_i)
    gates = jax.nn.sigmoid(n @ w_gate + b_gate).reshape(Bsz, T, 2, D)
    y = gates[:, :, 0] * (o_a @ w_branch_a) + gates[:, :, 1] * (o_b @ w_branch_b)
    return y @ w_out

def conv_gated_mlp(n, w_up, conv_w, w_down):
    gate, up = jnp.split(n @ w_up, 2, axis=-1)
    gate = causal_dwconv(gate, conv_w)
    return (jax.nn.silu(gate) * up) @ w_down

def first_inputs(seed: int = 0) -> dict:
    key = jax.random.key(seed)
    ks = jax.random.split(key, 24)
    L, D = DEPTH, D_MODEL
    f32 = jnp.float32

    def nrm(k, shape, scale):
        return jax.random.normal(k, shape, f32) * scale

    def gain(k, shape):
        return 1.0 + nrm(k, shape, 0.02)

    a_init = jax.random.uniform(ks[5], (L, A_HEADS), f32, 1.0, 16.0)
    dt = jnp.exp(jax.random.uniform(ks[6], (L, A_HEADS), f32, math.log(1e-3), math.log(1e-1)))
    return {
        "x": nrm(ks[0], (BATCH, SEQ, D), 1.0),
        "meta_tokens": nrm(ks[1], (N_META, D), 0.5),
        "norm_mix": gain(ks[2], (L, D)),
        "w_in": nrm(ks[3], (L, D, IN_COLS), D ** -0.5),
        "conv_a": nrm(ks[4], (L, A_CONV, 2 * A_HEADS * A_DK + A_WIDTH), 0.5),
        "a_log": jnp.log(a_init),
        "dt_bias": dt + jnp.log(-jnp.expm1(-dt)),
        "a_out_norm": gain(ks[7], (L, A_DV)),
        "q_norm": gain(ks[8], (L, B_DH)),
        "k_norm": gain(ks[9], (L, B_DH)),
        "kidx_norm": gain(ks[10], (L, IDX_DIM)),
        "w_branch_a": nrm(ks[11], (L, A_WIDTH, D), A_WIDTH ** -0.5),
        "w_branch_b": nrm(ks[12], (L, B_WIDTH, D), B_WIDTH ** -0.5),
        "w_gate": nrm(ks[13], (L, D, 2 * D), D ** -0.5),
        "b_gate": nrm(ks[14], (L, 2 * D), 0.1),
        "w_out": nrm(ks[15], (L, D, D), D ** -0.5),
        "norm_ffn": gain(ks[16], (L, D)),
        "w_up": nrm(ks[17], (L, D, 2 * D_FF), D ** -0.5),
        "conv_ffn": nrm(ks[18], (L, FFN_CONV, D_FF), 0.5),
        "w_down": nrm(ks[19], (L, D_FF, D), D_FF ** -0.5),
    }

def first_block(x, meta_tokens, norm_mix, w_in, conv_a, a_log, dt_bias, a_out_norm, q_norm, k_norm,
              kidx_norm, w_branch_a, w_branch_b, w_gate, b_gate, w_out, norm_ffn, w_up, conv_ffn,
              w_down) -> jnp.ndarray:
    Bsz = x.shape[0]
    T = N_META + x.shape[1]
    cos_a, sin_a = rope_tables(T, B_DH)
    cos_i, sin_i = rope_tables(T, IDX_DIM)
    meta = jnp.broadcast_to(meta_tokens.astype(x.dtype)[None], (Bsz, N_META, x.shape[2]))
    h = jnp.concatenate([meta, x], axis=1)
    for l in range(DEPTH):
        n = rms_norm(h, norm_mix[l])
        h = h + hybrid_mixer(n, w_in[l], conv_a[l], a_log[l], dt_bias[l], a_out_norm[l], q_norm[l],
                             k_norm[l], kidx_norm[l], w_branch_a[l], w_branch_b[l], w_gate[l], b_gate[l],
                             w_out[l], cos_a, sin_a, cos_i, sin_i).astype(h.dtype)
        n = rms_norm(h, norm_ffn[l])
        h = h + conv_gated_mlp(n, w_up[l], conv_ffn[l], w_down[l]).astype(h.dtype)
    return h[:, N_META:]


BLOCK = 128
A_HEADS_2 = 8
A_HEAD_DIM = 64
A_WIDTH_2 = A_HEADS_2 * A_HEAD_DIM
DILATED = ((128, 1), (512, 4), (2048, 16))
B_WIDTH_2 = D_MODEL - A_WIDTH_2
SCONV_WIDTH = 3
IN_SPLITS_2 = (A_WIDTH_2, A_WIDTH_2, A_WIDTH_2, B_WIDTH_2, B_WIDTH_2, B_WIDTH_2)
IN_WIDTH = sum(IN_SPLITS_2)
RET_HEADS = 4
RET_KDIM = D_MODEL // RET_HEADS
RET_VDIM = 2 * D_MODEL // RET_HEADS
RET_CHUNK = 128
ROPE_BASE = 10000.0
FFN_CONV_WIDTH = 3
N_EVEN = (DEPTH + 1) // 2
N_ODD = DEPTH // 2


def rms_norm_2(x, g):
    xf = x.astype(jnp.float32)
    y = xf * lax.rsqrt(jnp.mean(xf * xf, axis=-1, keepdims=True) + EPS)
    return (y * g.astype(jnp.float32)).astype(x.dtype)

def causal_dwconv_2(x, w):
    K = w.shape[0]
    S = x.shape[1]
    xp = jnp.pad(x, ((0, 0), (K - 1, 0), (0, 0)))
    y = xp[:, 0:S] * w[0]
    for j in range(1, K):
        y = y + xp[:, j:j + S] * w[j]
    return y

def banded_causal_attention(q, k, v, reach):
    L, hd = q.shape[-2], q.shape[-1]
    lead = q.shape[:-2]
    nb = -(-L // BLOCK)
    pad_end = nb * BLOCK - L
    zp = [(0, 0)] * len(lead)
    qb = jnp.pad(q, zp + [(0, pad_end), (0, 0)]).reshape(*lead, nb, BLOCK, hd)
    kp = jnp.pad(k, zp + [(BLOCK, pad_end), (0, 0)]).reshape(*lead, nb + 1, BLOCK, hd)
    vp = jnp.pad(v, zp + [(BLOCK, pad_end), (0, 0)]).reshape(*lead, nb + 1, BLOCK, hd)
    kb = jnp.concatenate([kp[..., :-1, :, :], kp[..., 1:, :, :]], axis=-2)
    vb = jnp.concatenate([vp[..., :-1, :, :], vp[..., 1:, :, :]], axis=-2)
    s = jnp.einsum('...nqd,...nkd->...nqk', qb.astype(jnp.float32), kb.astype(jnp.float32)) * (hd ** -0.5)
    blk = jnp.arange(nb)[:, None, None]
    qi = jnp.arange(BLOCK)[None, :, None]
    kj = jnp.arange(2 * BLOCK)[None, None, :]
    rel = BLOCK + qi - kj
    kpos = blk * BLOCK - BLOCK + kj
    mask = (rel >= 0) & (rel <= reach) & (kpos >= 0)
    s = jnp.where(mask, s, -jnp.inf)
    m = jnp.max(s, axis=-1, keepdims=True)
    p = jnp.exp(s - m)
    den = jnp.sum(p, axis=-1, keepdims=True)
    o = jnp.einsum('...nqk,...nkd->...nqd', p, vb.astype(jnp.float32)) / den
    lse = (m + jnp.log(den))[..., 0]
    o = o.reshape(*lead, nb * BLOCK, hd)[..., :L, :]
    lse = lse.reshape(*lead, nb * BLOCK)[..., :L]
    return o, lse

def dilated_attention(q, k, v):
    Bn, H, S, hd = q.shape
    outs, lses = [], []
    for window, dil in DILATED:
        L = S // dil
        split = lambda t: t.reshape(Bn, H, L, dil, hd).swapaxes(2, 3)
        o, lse = banded_causal_attention(split(q), split(k), split(v), window // dil)
        outs.append(o.swapaxes(2, 3).reshape(Bn, H, S, hd))
        lses.append(lse.swapaxes(2, 3).reshape(Bn, H, S))
    wts = jax.nn.softmax(jnp.stack(lses), axis=0)
    return jnp.sum(wts[..., None] * jnp.stack(outs), axis=0)

def even_mixer(xn, w_in, q_gain, k_gain, sconv_w, w_out):
    Bn, S, _ = xn.shape
    proj = xn @ w_in
    q, k, v, gate_b, gate_c, h = jnp.split(proj, np.cumsum(IN_SPLITS_2)[:-1].tolist(), axis=-1)
    heads = lambda t: t.reshape(Bn, S, A_HEADS_2, A_HEAD_DIM)
    q = rms_norm_2(heads(q), q_gain).transpose(0, 2, 1, 3)
    k = rms_norm_2(heads(k), k_gain).transpose(0, 2, 1, 3)
    v = heads(v).transpose(0, 2, 1, 3)
    a = dilated_attention(q, k, v).astype(xn.dtype).transpose(0, 2, 1, 3).reshape(Bn, S, A_WIDTH_2)
    b = gate_b * causal_dwconv_2(gate_c * h, sconv_w)
    return jnp.concatenate([a, b], axis=-1) @ w_out

def rotary(x, pos):
    half = x.shape[-1] // 2
    inv = ROPE_BASE ** (-jnp.arange(half, dtype=jnp.float32) / half)
    ang = pos[:, None] * inv[None, :]
    cos = jnp.cos(ang)[None, :, None, :]
    sin = jnp.sin(ang)[None, :, None, :]
    x1, x2 = x[..., :half], x[..., half:]
    return jnp.concatenate([x1 * cos - x2 * sin, x1 * sin + x2 * cos], axis=-1)

def chunkwise_retention(q, k, v):
    Bn, S, H, dk = q.shape
    dv = v.shape[-1]
    nc = S // RET_CHUNK
    log_g = jnp.log1p(-(2.0 ** (-5.0 - jnp.arange(H, dtype=jnp.float32))))
    i = jnp.arange(RET_CHUNK, dtype=jnp.float32)
    diff = i[:, None] - i[None, :]
    inner_decay = jnp.where(diff >= 0, jnp.exp(log_g[:, None, None] * jnp.maximum(diff, 0.0)), 0.0)
    q_decay = jnp.exp(log_g[:, None] * (i + 1.0))
    k_decay = jnp.exp(log_g[:, None] * (RET_CHUNK - 1.0 - i))
    chunk_decay = jnp.exp(log_g * RET_CHUNK)
    to_chunks = lambda t: t.reshape(Bn, nc, RET_CHUNK, H, t.shape[-1]).transpose(1, 0, 3, 2, 4)

    def step(state, qkv):
        qc, kc, vc = qkv
        scores = jnp.einsum('bhqd,bhkd->bhqk', qc, kc) * inner_decay
        o = (jnp.einsum('bhqk,bhke->bhqe', scores, vc)
             + jnp.einsum('bhqd,bhde->bhqe', qc, state) * q_decay[..., None])
        state = (state * chunk_decay[:, None, None]
                 + jnp.einsum('bhkd,bhke->bhde', kc * k_decay[..., None], vc))
        return state, o

    state0 = jnp.zeros((Bn, H, dk, dv), jnp.float32)
    _, o = lax.scan(step, state0, (to_chunks(q), to_chunks(k), to_chunks(v)))
    return o.transpose(1, 0, 3, 2, 4).reshape(Bn, S, H, dv)

def retention_mixer(xn, wq, wk, wv, wg, gn_gain, wo):
    Bn, S, _ = xn.shape
    pos = jnp.arange(S, dtype=jnp.float32)
    q = (xn @ wq).reshape(Bn, S, RET_HEADS, RET_KDIM).astype(jnp.float32)
    k = (xn @ wk).reshape(Bn, S, RET_HEADS, RET_KDIM).astype(jnp.float32) * (RET_KDIM ** -0.5)
    v = (xn @ wv).reshape(Bn, S, RET_HEADS, RET_VDIM).astype(jnp.float32)
    o = chunkwise_retention(rotary(q, pos), rotary(k, pos), v)
    mu = jnp.mean(o, axis=-1, keepdims=True)
    var = jnp.mean(jnp.square(o - mu), axis=-1, keepdims=True)
    o = (o - mu) * lax.rsqrt(var + EPS) * gn_gain.astype(jnp.float32)
    o = o.reshape(Bn, S, RET_HEADS * RET_VDIM).astype(xn.dtype)
    return (jax.nn.silu(xn @ wg) * o) @ wo

def conv_glu_ffn(xn, w_up, conv_w, w_down):
    u = causal_dwconv_2(xn @ w_up, conv_w)
    g, val = jnp.split(u, 2, axis=-1)
    return (jax.nn.silu(g) * val) @ w_down

def second_inputs(seed: int = 0) -> dict:
    key = jax.random.key(seed)
    ks = jax.random.split(key, 24)
    nrm = lambda k, shape, s: jax.random.normal(k, shape, jnp.float32) * s
    gain = lambda k, shape: 1.0 + 0.02 * jax.random.normal(k, shape, jnp.float32)
    D = D_MODEL
    return {
        "x": jax.random.normal(ks[0], (BATCH, SEQ, D), jnp.float32),
        "even_norm": gain(ks[1], (N_EVEN, D)),
        "even_w_in": nrm(ks[2], (N_EVEN, D, IN_WIDTH), D ** -0.5),
        "even_q_gain": gain(ks[3], (N_EVEN, A_HEAD_DIM)),
        "even_k_gain": gain(ks[4], (N_EVEN, A_HEAD_DIM)),
        "even_sconv_w": nrm(ks[5], (N_EVEN, SCONV_WIDTH, B_WIDTH_2), SCONV_WIDTH ** -0.5),
        "even_w_out": nrm(ks[6], (N_EVEN, A_WIDTH_2 + B_WIDTH_2, D), (A_WIDTH_2 + B_WIDTH_2) ** -0.5),
        "odd_norm": gain(ks[7], (N_ODD, D)),
        "ret_wq": nrm(ks[8], (N_ODD, D, RET_HEADS * RET_KDIM), D ** -0.5),
        "ret_wk": nrm(ks[9], (N_ODD, D, RET_HEADS * RET_KDIM), D ** -0.5),
        "ret_wv": nrm(ks[10], (N_ODD, D, RET_HEADS * RET_VDIM), D ** -0.5),
        "ret_wg": nrm(ks[11], (N_ODD, D, RET_HEADS * RET_VDIM), D ** -0.5),
        "ret_gn_gain": gain(ks[12], (N_ODD, RET_HEADS, RET_VDIM)),
        "ret_wo": nrm(ks[13], (N_ODD, RET_HEADS * RET_VDIM, D), (RET_HEADS * RET_VDIM) ** -0.5),
        "ffn_norm": gain(ks[14], (DEPTH, D)),
        "ffn_w_up": nrm(ks[15], (DEPTH, D, 2 * D_FF), D ** -0.5),
        "ffn_conv_w": nrm(ks[16], (DEPTH, FFN_CONV_WIDTH, 2 * D_FF), FFN_CONV_WIDTH ** -0.5),
        "ffn_w_down": nrm(ks[17], (DEPTH, D_FF, D), D_FF ** -0.5),
    }

def second_block(x, even_norm, even_w_in, even_q_gain, even_k_gain, even_sconv_w, even_w_out,
              odd_norm, ret_wq, ret_wk, ret_wv, ret_wg, ret_gn_gain, ret_wo,
              ffn_norm, ffn_w_up, ffn_conv_w, ffn_w_down):
    for l in range(DEPTH):
        if l % 2 == 0:
            e = l // 2
            x = x + even_mixer(rms_norm_2(x, even_norm[e]), even_w_in[e], even_q_gain[e],
                               even_k_gain[e], even_sconv_w[e], even_w_out[e])
        else:
            o = l // 2
            x = x + retention_mixer(rms_norm_2(x, odd_norm[o]), ret_wq[o], ret_wk[o], ret_wv[o],
                                    ret_wg[o], ret_gn_gain[o], ret_wo[o])
        x = x + conv_glu_ffn(rms_norm_2(x, ffn_norm[l]), ffn_w_up[l], ffn_conv_w[l], ffn_w_down[l])
    return x


def setup_inputs(seed=0):
    out = dict(first_inputs(seed))
    for name, value in second_inputs(seed + 1).items():
        if name != "x":
            out[name + "_2"] = value
    return out


def reference(
    x, meta_tokens, norm_mix, w_in, conv_a, a_log, dt_bias, a_out_norm, q_norm, k_norm,
    kidx_norm, w_branch_a, w_branch_b, w_gate, b_gate, w_out, norm_ffn, w_up, conv_ffn, w_down,
    even_norm_2, even_w_in_2, even_q_gain_2, even_k_gain_2, even_sconv_w_2, even_w_out_2,
    odd_norm_2, ret_wq_2, ret_wk_2, ret_wv_2, ret_wg_2, ret_gn_gain_2, ret_wo_2, ffn_norm_2,
    ffn_w_up_2, ffn_conv_w_2, ffn_w_down_2,
):
    x = first_block(
        x, meta_tokens, norm_mix, w_in, conv_a, a_log, dt_bias, a_out_norm, q_norm, k_norm,
        kidx_norm, w_branch_a, w_branch_b, w_gate, b_gate, w_out, norm_ffn, w_up, conv_ffn,
        w_down,
    )
    return second_block(
        x, even_norm_2, even_w_in_2, even_q_gain_2, even_k_gain_2, even_sconv_w_2, even_w_out_2,
        odd_norm_2, ret_wq_2, ret_wk_2, ret_wv_2, ret_wg_2, ret_gn_gain_2, ret_wo_2, ffn_norm_2,
        ffn_w_up_2, ffn_conv_w_2, ffn_w_down_2,
    )


_drawn_inputs = setup_inputs


def setup_inputs(seed=0):
    import zlib

    import numpy as np

    out = dict(_drawn_inputs(seed))
    spreads = {}
    factors = {'a_out_norm': 3.113,
     'q_norm': 5.896,
     'k_norm': 7.864,
     'even_q_gain_2': 8.0,
     'even_k_gain_2': 8.0,
     'odd_norm_2': 3.732,
     'ret_gn_gain_2': 7.271,
     'ffn_norm_2': 3.486}
    for name, (base, spread) in spreads.items():
        noise = np.random.default_rng([zlib.crc32(name.encode()), seed]).standard_normal(out[name].shape)
        drawn = base * np.exp(spread * noise) if base else spread * noise
        out[name] = __import__('jax').numpy.asarray(drawn.astype(out[name].dtype))
    for name, factor in factors.items():
        out[name] = (out[name] * factor).astype(out[name].dtype)
    return out
```

```python
import math
from contextlib import ExitStack

import numpy as np

import concourse.bass as bass
from concourse import mybir

F32 = mybir.dt.float32
F32R = mybir.dt.float32r
ACT = mybir.ActivationFunctionType
ALU = mybir.AluOpType
AX = mybir.AxisListType.X
ds = bass.ds

P = 128
D = 1024
DC = D // P
DEPTH = 2
SEQ = 256
META = 16
T = META + SEQ
EPS = 1e-6
HEADS = 4
IDX_HEADS, IDX_DIM, TOPK = 8, 64, 64
FF = 2816
FC = FF // P
CHUNK = 64
INPUTS = (
    "x", "meta_tokens", "norm_mix", "w_in", "conv_a", "a_log", "dt_bias", "a_out_norm", "q_norm", "k_norm", "kidx_norm",
    "w_branch_a", "w_branch_b", "w_gate", "b_gate", "w_out", "norm_ffn", "w_up", "conv_ffn", "w_down", "even_norm_2",
    "even_w_in_2", "even_q_gain_2", "even_k_gain_2", "even_sconv_w_2", "even_w_out_2", "odd_norm_2", "ret_wq_2", "ret_wk_2",
    "ret_wv_2", "ret_wg_2", "ret_gn_gain_2", "ret_wo_2", "ffn_norm_2", "ffn_w_up_2", "ffn_conv_w_2", "ffn_w_down_2",
)
TB = [(0, META), (META, P), (META + P, P)]
LEVELS = 7
PANEL = 256
C_AB, C_BQ, C_BK, C_IQ, C_IK = 2048, 2056, 2568, 2824, 3336
IN_COLS = 3408
S_IK, S_BK, S_BV, S_AB, S_ALL = 0, 128, 256, 384, 400

M_IN, M_GATE, M_BRANCH, M_OUT, M_UP, M_DOWN, M_LAYER = 0, 6, 10, 12, 14, 25, 31
R_IN, R_GATE, R_BRANCH, R_OUT, R_UP, R_DOWN, R_LAYER = 0, 6, 10, 14, 16, 27, 29
M_E, R_E = DEPTH * M_LAYER, DEPTH * R_LAYER
E_OUT, E_UP, E_DOWN, M_EVEN, R_EVEN = 6, 8, 19, 25, 21
M_O, R_O = M_E + M_EVEN, R_E + R_EVEN
O_K, O_V, O_G, O_OUT, O_UP, O_DOWN = 2, 4, 8, 12, 16, 27
RO_OUT, RO_UP, RO_DOWN, M_ODD, R_ODD = 12, 14, 25, 33, 27
M_ALL, R_ALL = M_O + M_ODD, R_O + R_ODD
DOWN_K = [(0, 8), (8, 8), (16, FC - 16)]

BIG = 1e30
INVALID = -3.0e38
TAKEN = -3.4e38


def constants():
    f = np.float32
    p = np.arange(P)
    parts, at = [], {}

    def put(name, a):
        at[name] = sum(x.shape[1] for x in parts)
        parts.append(np.ascontiguousarray(a, dtype=f).reshape(P, -1))

    put("ident", np.eye(P))
    put("ones", np.ones((P, P)))
    put("half", (p[:, None] // 64 == p[None, :] // 64))

    def turn(dim):
        r = np.zeros((P, P))
        for i in range(P):
            if i % dim < dim // 2:
                r[i + dim // 2, i] = -1.0
            else:
                r[i - dim // 2, i] = 1.0
        return r

    put("turn_a", turn(P))
    put("turn_i", turn(IDX_DIM))

    def angles(dim, n_tok):
        inv = (1.0 / (f(10000.0) ** (np.arange(0, dim, 2, dtype=f) / f(dim)))).astype(f)
        return (np.arange(n_tok, dtype=f)[:, None] * inv[None, :]).astype(f)

    for name, dim in (("a", P), ("i", IDX_DIM)):
        ang = angles(dim, T)
        rows = p % (dim // 2)
        put("cos_" + name, np.cos(ang).T[rows])
        put("sin_" + name, np.sin(ang).T[rows])
    for l in range(LEVELS):
        s, c = p[:, None], p[None, :]
        put(f"level{l}", (s >> (l + 1) == c >> (l + 1)) & ((c >> l) % 2 == 1) & ((s >> l) % 2 == 0))
    put("upto", p[:, None] <= p[None, :])
    q = np.arange(SEQ).reshape(2, P).T
    limit = (q // CHUNK + 1) * CHUNK
    put("barred", np.where(np.arange(SEQ)[None, None, :] < limit[:, :, None], 0.0, INVALID))
    col = np.zeros((P, 4))
    col[:, 0] = EPS
    col[:, 1] = math.log(P ** -0.5)
    col[:, 2] = 1.0
    put("cols", col)
    first, first_at = np.concatenate(parts, 1), dict(at)
    parts.clear()
    at.clear()
    t, s = np.arange(SEQ)[:, None], np.arange(SEQ)[None, :]
    back = t - s
    count = sum(((back >= 0) & (back % d == 0) & (back // d <= w // d)).astype(f) for w, d in ((128, 1), (512, 4), (2048, 16)))
    put("count", count.reshape(2, P, SEQ).transpose(1, 0, 2))
    put("unseen", np.where(count > 0, 0.0, -BIG).reshape(2, P, SEQ).transpose(1, 0, 2))
    half = P
    inv = (f(10000.0) ** (-np.arange(half, dtype=f) / f(half))).astype(f)
    ang = (np.arange(SEQ, dtype=f)[:, None] * inv[None, :]).astype(f)
    put("cos_r", np.cos(ang).T)
    put("sin_r", np.sin(ang).T)
    for h in range(4):
        log_g = np.log1p(-(2.0 ** (-5.0 - h)))
        dec = np.where(back >= 0, np.exp(log_g * np.maximum(back, 0)), 0.0) * 256 ** -0.5
        dec = dec.T.reshape(2, P, SEQ)
        put(f"decay{h}", np.concatenate([dec[0], dec[1][:, P:]], 1))
    second = np.concatenate(parts, 1)
    return {"arrays": {"c1": first, "c2": second}, "places": (first_at, at, first.shape[1], second.shape[1])}


def plan_aux(jobs):
    place, used, q = {}, [0] * 4, 0
    for job in jobs:
        if isinstance(job, tuple):
            _, n, names = job
            for name in names:
                used[q % 4] += 1
                place[name] = (q % 4, used[q % 4])
                q += 1
            for b in range(4):
                used[b] += (n - 1) * len(names) // 4
        else:
            used[q % 4] += 1
            place[job] = (q % 4, used[q % 4])
            q += 1
    return place, used


class Own:

    def __init__(self, eng, sem):
        self.eng, self.sem, self.base, self.n = eng, sem, 0, 0

    def done(self, ins):
        ins.then_inc(self.sem, 1)
        self.n += 1
        return self.n

    def wait(self, n=None):
        self.eng.wait_ge(self.sem, self.base + (self.n if n is None else n))


JOBS = (
    ["ms1", "ik", "bk", "bv", "ab"]
    + [f"ssq{h}" for h in range(4)] + [f"ssk{h}" for h in range(4)] + [f"sbq{h}" for h in range(4)] + ["sbk", "sik"]
    + ["gc"] + [x for b in range(3) for x in (f"gb{b}", f"bb{b}")]
    + [x for b in range(3) for x in (f"kk{b}", f"qk{b}")] + [x for b in range(3) for x in (f"kt{b}", f"vt{b}")]
    + [f"rq{h}" for h in range(4)] + [f"ri{c}" for c in range(4)] + ["rk", "rik"]
    + [f"ix{j}{e}" for j in range(2) for e in range(4)]
    + [("loop", LEVELS, ["Y0", "Y1", "Y2", "XA0", "X1", "A1", "X2", "A2"])]
    + ["vn0", "o0", "dS0", "kS1", "vn1", "o1", "dS1", "kS2", "vn2", "o2"]
    + ["s0", "pt0", "pv0"] + [f"{x}{j}" for j in (1, 2) for x in ("sa", "sb", "sc", "sd", "pt0_", "pt1_", "pt2_", "pv")]
    + [f"so{h}" for h in range(4)] + ["ms2"]
)
PLACE, AUX_PER = plan_aux(JOBS)
JOBS2 = (
    ["ems"] + [f"eq{c}" for c in range(4)] + ["e00", "e01"] + [f"et0{g}" for g in range(2)] + ["ev0"]
    + [f"e1{e}" for e in range(4)] + [f"et1{g}{b}" for g in range(2) for b in range(2)] + ["ev1", "emf", "oms"]
    + [f"os{h}" for h in range(4)] + [f"oo{h}{e}" for h in range(4) for e in range(2)] + [f"om{h}" for h in range(4)]
    + [f"ow{h}" for h in range(4)] + ["omf"]
)
PLACE.update(plan_aux(JOBS2)[0])

PER = {
    "panel_in": 2 * 16 * M_LAYER, "whi": 2 * M_LAYER, "wlo": 2 * M_LAYER, "whi_used": 2 * M_LAYER, "panel_done": 2 * M_LAYER,
    "lin_read": R_LAYER, "small_in": 5 * 16,
    "sq": 2, "rstd": 2, "n": 2 * DC, "nh": 4, "nl": 4,
    "conv": 12, "silu": 4, "sq_heads": 1, "sq_att": 1, "rn": 4, "qk_unit": 2, "att_unit": 3,
    "sp_in": 1, "sp_ln": 1, "gt": 7, "eg": 4, "dec": 3, "kdx": 1, "qe": 1,
    "rope": 4, "score": 8, "ml": 3 * LEVELS, "ab_ready": 3,
    "nmx": 3, "soft": 2, "pn": 3, "ob_h": 3, "sqo": 1, "rno": 1, "oa": 1, "oa_h": 1, "oa_l": 1,
    "gates": 1, "y": 8, "yh": 4, "yl": 4,
    "tap": 2 * 11, "gate_silu": 2 * 11, "ah": 2 * 11, "al": 2 * 11,
    "act_own": 0, "dve_own": 0,
}
PER["act_own"] = 4
PER["dve_own"] = 134


SECOND = ("c2_in", "sq2", "rstd2", "n2", "nh2", "nl2", "raw2", "esq", "ern", "eunit", "enmx", "esoft", "epn", "eob_h", "egh", "econv",
          "eb", "eb_h", "eb_l", "oraw", "orot", "osc", "osq", "omean", "ovar", "ogate", "og_h", "og_l", "tap2", "silu2", "conv2", "ah2", "al2")


def bf(ap, axis, shape):
    return ap.unsqueeze(axis).to_broadcast(shape)


def build(nc, a, places, out):
    ctx = ExitStack()
    consts_at1, consts_at2, n1, n2 = places
    with ctx:
        sem = {name: ctx.enter_context(nc.semaphore(name)) for name in PER if name not in ("panel_in", "lin_read")}
        for name in ("start_in", "h0", "rows", "stored", "turned", "turned_back", "out_ready", "cleared", "pe_stood", "dve_stood", *SECOND):
            sem[name] = ctx.enter_context(nc.semaphore(name))
        panel_in = [ctx.enter_context(nc.semaphore(f"panel_in{i}")) for i in range(2)]
        lin_read = [ctx.enter_context(nc.semaphore(f"lin_read{i}")) for i in range(4)]
        aux_full = [ctx.enter_context(nc.semaphore(f"aux_full{i}")) for i in range(4)]
        aux_read = [ctx.enter_context(nc.semaphore(f"aux_read{i}")) for i in range(4)]
        lin = [ctx.enter_context(nc.psum_tensor(f"lin{i}", [P, 512], F32)) for i in range(4)]
        aux = [ctx.enter_context(nc.psum_tensor(f"aux{i}", [P, 512], F32)) for i in range(4)]

        base = nc.sbuf_usable_end - nc.sbuf_bytes_remaining
        base = (base + 63) // 64 * 64

        def tile(name, shape, at, dt=F32):
            size = 4 * int(np.prod(shape[1:]))
            assert at % 32 == 0 and at + size <= nc.sbuf_usable_end, (name, at + size - nc.sbuf_usable_end)
            return nc.alloc_sbuf_tensor_at(name, shape, dt, offset=at), (at + size + 31) // 32 * 32

        hT, o = tile("hT", [P, DC, T], base)
        nH, o = tile("nH", [P, DC, T], o, F32R)
        nL, o = tile("nL", [P, DC, T], o, F32R)
        stage, o = tile("stage", [P, 2, DC, PANEL], o)
        wH, o = tile("wH", [P, 2, DC, PANEL], o, F32R)
        wL, o = tile("wL", [P, 2, DC, PANEL], o, F32R)
        c1, o = tile("c1", [P, n1], o)
        par, o = tile("par", [P, 2 * DEPTH, 2 * P], o)
        rates, o = tile("rates", [P, DEPTH, 8], o)
        parL, o = tile("parL", [P, 2 * P + 24], o)
        o = (o + 63) // 64 * 64
        arena = o

        def const(name, n, parts=P):
            return c1[0:parts, consts_at1[name]:consts_at1[name] + n]

        ident, ones = const("ident", P), const("ones", P)
        eps_col, lnq_col = const("cols", 1), c1[:, consts_at1["cols"] + 1:consts_at1["cols"] + 2]

        rawT, o = tile("rawT", [P, 24, T], arena)
        cT, o = tile("cT", [P, 12, T], o)
        zT, o = tile("zT", [P, 4, T], o)
        kd_at = o
        kd, o = tile("kd", [P, 3, 4, P], o)
        vt, o = tile("vt", [P, 3, 4, P], o)
        mixer_tail = o
        nT, o = tile("nT", [P, DC, T], o)
        oH, o = tile("oH", [P, DC, T], o, F32R)
        oL, o2 = tile("oL", [P, DC, T], o, F32R)
        wS, _ = tile("wS", [P, DC, S_ALL], o - 4 * DC * T)
        o = o2

        def blocks(name, at):
            big, at = tile(name, [P, 2, 4, P], at)
            small, at = tile(name + "0", [META, 4, META], at)
            return [small[:, :, :], big[:, 0], big[:, 1]], at

        MT, q_at = blocks("MT", o)
        QD, x_at = blocks("QD", q_at)
        X, a_at = blocks("X", x_at)
        A, ml_at = blocks("A", a_at)
        ML, y_at = blocks("ML", ml_at)
        Y, o2 = blocks("Y", y_at)
        mt_at, o = o, o2
        sq8, _ = tile("sq8", [P, DC, T], x_at)
        gtri, _ = blocks("gtri", x_at)
        bdiag, _ = blocks("bdiag", a_at)
        decay, _ = blocks("decay", ml_at)
        sq_att, _ = tile("sq_att", [P, 6, T], ml_at)
        rnq, _ = tile("rnq", [P, 4, T], mt_at)
        rnk, _ = tile("rnk", [P, 4, T], q_at)
        rnb, _ = tile("rnb", [P, 5, T], kd_at)
        rni, _ = tile("rni", [P, T], kd_at + 4 * 3 * 4 * P)
        tmp4, _ = tile("tmp4", [P, 4, T], y_at)
        R, vn_at = tile("R", [P, 4, P], ml_at)
        vn, _ = tile("vn", [P, 4, P], vn_at)
        S, _ = tile("S", [P, 4, P], y_at)
        Pm, _ = tile("Pm", [P, 4, T], mt_at)
        PT, _ = tile("PT", [P, 3, 4 * P], arena + 4 * 24 * T + 4 * 4 * T)
        sqo, _ = tile("sqo", [P, 4, T], x_at)
        rno, _ = tile("rno", [P, 4, T], a_at)
        yT, _ = tile("yT", [P, DC, T], mixer_tail)
        ytmp, _ = tile("ytmp", [P, 2, T], x_at)
        rl, r_at = tile("rl", [P, 2, 2 * SEQ], mixer_tail)
        score, r_at = tile("score", [P, 2, SEQ], r_at)
        work, r_at = tile("work", [P, 2, SEQ], r_at)
        assert r_at <= mixer_tail + 4 * DC * T
        eg, o2 = tile("eg", [P, 4, T], o)
        oA, _ = tile("oA", [P, 4, T], o)
        o = o2
        bkr, o = tile("bkr", [P, T], o)
        ikr, o = tile("ikr", [P, T], o)
        vtok, o = tile("vtok", [P, 3, P], o)
        bias, o = tile("bias", [P, 2, T], o)
        rs, _ = tile("rs", [P, T], y_at)
        P0, s_at = tile("P0", [META, 4, META], y_at + 4 * 4 * P)
        ab, o = tile("ab", [P, 3, 16], o)
        iw, o = tile("iw", [P, 3, 8], o)
        gx, o = tile("gx", [P, 3, 4], o)
        gm, o = tile("gm", [P, 3, 4], o)
        gl, o = tile("gl", [P, 3, 4], o)
        gg, o = tile("gg", [P, 3, 4], o)
        bt, o = tile("bt", [P, 3, 4], o)
        beta, o = tile("beta", [P, 3, 4], o)
        gcs, o = tile("gcs", [P, 3, 4], o)
        egt, o = tile("egt", [P, 3, 4], o)
        kdx, o = tile("kdx", [P, 3, 4], o)
        sdec, o = tile("sdec", [P, 3, 4], o)
        m8, s_at = tile("m8", [P, 2, 8], s_at)
        mx, s_at = tile("mx", [P, 4], s_at)
        nmx, s_at = tile("nmx", [P, 4], s_at)
        sm, s_at = tile("sm", [P, 4], s_at)
        rsm, s_at = tile("rsm", [P, 4], s_at)
        aH, f_at = tile("aH", [P, FC, T], arena, F32R)
        aL, f_at = tile("aL", [P, FC, T], f_at, F32R)
        assert f_at <= mixer_tail
        u, f_at = tile("u", [P, 2, T], mt_at)
        sg, f_at = tile("sg", [P, 2, T], f_at)
        av, f_at = tile("av", [P, 2, T], f_at)
        xin, s_at = tile("xin", [P, 2, D], arena)
        metain, s_at = tile("metain", [META, D], s_at)
        rows, s_at = tile("rows", [P, 2 * DEPTH, 2, P], s_at)
        outT, _ = tile("outT", [P, 2, D], arena)

        n_tok, KB = SEQ, 4 * SEQ
        c2, _ = tile("c2", [P, n2], x_at)
        assert x_at + 4 * n2 <= y_at
        nT2, top = tile("nT2", [P, DC, SEQ], arena + 78 * KB)
        assert top <= x_at
        raw8, e_at = tile("raw8", [P, 8, SEQ], arena)
        vtk, e_at = tile("vtk", [P, 2, 512], e_at)
        gbt, e_at = tile("gbt", [P, 4, SEQ], e_at)
        gct, e_at = tile("gct", [P, 4, SEQ], e_at)
        ght, e_at = tile("ght", [P, 4, SEQ], e_at)
        cvt, e_at = tile("cvt", [P, 4, SEQ], e_at)
        Pe, e_at = tile("Pe", [P, 8, SEQ], e_at)
        PTe, e_at = tile("PTe", [P, 2, 8 * P], e_at)
        sqe, e_at = tile("sqe", [P, 8, SEQ], e_at)
        rne, e_at = tile("rne", [P, 8, SEQ], e_at)
        eH, e_at = tile("eH", [P, 8, SEQ], e_at, F32R)
        eL, e_at = tile("eL", [P, 8, SEQ], e_at, F32R)
        assert e_at <= arena + 78 * KB
        qk2, o_at = tile("qk2", [P, 2, 4, 2, SEQ], arena)
        vtk2, o_at2 = tile("vtk2", [P, 2, 2048], o_at)
        gH, _ = tile("gH", [P, 16, SEQ], arena, F32R)
        gL, _ = tile("gL", [P, 16, SEQ], o_at, F32R)
        tsin, o_at3 = tile("tsin", [P, 2, 4, SEQ], o_at2)
        sq4, o_at = tile("sq4", [P, 4, SEQ], o_at2)
        rn4, _ = tile("rn4", [P, 4, SEQ], o_at)
        sgT, o_at = tile("sgT", [P, 16, SEQ], o_at3)
        sc, o_at = tile("sc", [P, 4, 384], o_at)
        oR, o_at4 = tile("oR", [P, 16, SEQ], o_at)
        sqo2, _ = tile("sqo2", [P, 8, SEQ], o_at)
        assert o_at4 <= arena + 78 * KB
        aH2, f_at = tile("aH2", [P, FC, SEQ], arena, F32R)
        aL2, f_at = tile("aL2", [P, FC, SEQ], f_at, F32R)
        u2, f_at = tile("u2", [P, 4, SEQ], f_at)
        sg2, f_at = tile("sg2", [P, 2, SEQ], f_at)
        av2, f_at = tile("av2", [P, 2, SEQ], f_at)
        sqf, f_at = tile("sqf", [P, 8, SEQ], f_at)
        assert f_at <= arena + 78 * KB
        mx8, s_at = tile("mx8", [P, 8], y_at + 4 * 4 * P)
        nmx8, s_at = tile("nmx8", [P, 8], s_at)
        sm8, s_at = tile("sm8", [P, 8], s_at)
        rsm8, s_at = tile("rsm8", [P, 8], s_at)
        KE_QG, KE_KG, KE_SC, KE_FN, KE_T2 = 8, 9, 10, 22, 30
        KO_GN, KO_FN, KO_T2 = 8, 24, 32

        def p2(j, k):
            return par[:, DEPTH + j, k:k + 1]

        def table2(name, n):
            return c2[:, consts_at2[name]:consts_at2[name] + n]

        K_CONV, K_NORM1, K_NORM2, K_ANORM, K_QN, K_KN, K_IN, K_BG, K_FCONV, K_NB = 0, 48, 56, 64, 65, 66, 67, 68, P, 2 * P
        K_DT, K_NA = 2 * P + 16, 2 * P + 20

        def pc(k, n=1):
            return parL[:, k:k + n]

        def at(name, l, n):
            return l * PER[name] + n

        def tok(b):
            return slice(TB[b][0], TB[b][0] + TB[b][1])

        def cdyn(x, width=1):
            return ds(x, width)

        def full(name, l, it=0):
            b, n = PLACE[name]
            return aux_full[b], l * AUX_PER[b] + n + it * 2

        def read(name, l, it=0):
            b, n = PLACE[name]
            return aux_read[b], l * AUX_PER[b] + n + it * 2

        def bank(name):
            return aux[PLACE[name][0]]

        def emptied(name):
            return aux_read[PLACE[name][0]]

        def filled(name):
            return aux_full[PLACE[name][0]]

        def stand(eng, name):
            eng.sem_inc(sem[name], 1)

        def load(sp, m, s, pieces):
            sp.wait_ge(sem["wlo"], 2 * m + s + 1)
            for k0, k1, src in pieces:
                sp.dma_start(stage[:, s, k0:k1, :], src).then_inc(panel_in[s], 16)

        def split_hi(act, m, s):
            act.wait_ge(panel_in[s], 32 * m + 32)
            act.wait_ge(sem["whi_used"], 2 * m + s + 1)
            nc.scalar.activation(wH[:, s], stage[:, s], ACT.Copy).then_inc(sem["whi"], 1)

        def split_lo(dve, m, s):
            dve.wait_ge(sem["whi"], 2 * m + s + 1)
            dve.wait_ge(sem["panel_done"], 2 * m + s + 1)
            nc.vector.tensor_tensor(wL[:, s], stage[:, s], wH[:, s].bitcast(F32), ALU.subtract).then_inc(sem["wlo"], 1)

        def multiply(pe, m, s, rnd, groups, width, start=True, stop=True):
            pe.wait_ge(sem["whi"], 2 * m + s + 1)
            for b, _, _ in groups:
                if start:
                    pe.wait_ge(lin_read[b], rnd)
            for b, cols, ks in groups:
                for n, (k, xh, xl) in enumerate(ks):
                    nc.tensor.matmul(lin[b][:, 0:width], wH[:, s, k, cols], xh, start=start and n == 0, stop=False)
                    mm = nc.tensor.matmul(lin[b][:, 0:width], wH[:, s, k, cols], xl, start=False, stop=False)
            mm.then_inc(sem["whi_used"], 1)
            pe.wait_ge(sem["wlo"], 2 * m + s + 3)
            for b, cols, ks in groups:
                for n, (k, xh, _) in enumerate(ks):
                    mm = nc.tensor.matmul(lin[b][:, 0:width], wL[:, s, k, cols], xh, start=False, stop=stop and n == len(ks) - 1)
            mm.then_inc(sem["panel_done"], 1)

        def halves(s, x_hi, x_lo, n=DC, k0=0):
            return [(2 * s + c, slice(c * P, c * P + P), [(k, x_hi[:, k0 + k, :], x_lo[:, k0 + k, :]) for k in range(n)])
                    for c in range(2)]

        block = ctx.enter_context(nc.Block())

        def w_rows(name, k_all):
            return a[name].rearrange("l (k p) n -> p (l k) n", p=P), k_all

        @block.sync
        def _(sp):
            sp.dma_start(c1[:, :], a["c1"]).then_inc(sem["start_in"], 16)
            sp.dma_start(xin[:, :, :], a["x"].rearrange("b (j p) d -> p (b j) d", p=P)).then_inc(sem["start_in"], 16)
            sp.dma_start(metain[:, :], a["meta_tokens"]).then_inc(sem["start_in"], 16)

            sp.wait_ge(sem["cleared"], 1)

            def row(l, t, r, src, n, cols=slice(0, P)):
                sp.dma_start(rows[r:r + n, l, t, cols], src).then_inc(sem["rows"], 16)

            for l in range(DEPTH):
                row(l, 0, K_CONV, a["conv_a"][l].rearrange("k (c p) -> (k c) p", p=P), 48)
                row(l, 0, K_NORM1, a["norm_mix"][l].rearrange("(c p) -> c p", p=P), DC)
                row(l, 0, K_NORM2, a["norm_ffn"][l].rearrange("(c p) -> c p", p=P), DC)
                row(l, 0, K_ANORM, a["a_out_norm"][l:l + 1, :], 1)
                row(l, 0, K_QN, a["q_norm"][l:l + 1, :], 1)
                row(l, 0, K_KN, a["k_norm"][l:l + 1, :], 1)
                row(l, 0, K_IN, a["kidx_norm"][l:l + 1, :], 1, slice(0, 64))
                row(l, 0, K_IN, a["kidx_norm"][l:l + 1, :], 1, slice(64, P))
                row(l, 0, K_BG, a["b_gate"][l].rearrange("(c p) -> c p", p=P), 16)
                row(l, 1, 0, a["conv_ffn"][l].rearrange("k (c p) -> (k c) p", p=P), 66)
                sp.dma_start(rates[:, l, 0:4], a["dt_bias"][l:l + 1, :].to_broadcast([P, 4])).then_inc(sem["rows"], 16)
                sp.dma_start(rates[:, l, 4:8], a["a_log"][l:l + 1, :].to_broadcast([P, 4])).then_inc(sem["rows"], 16)

            l = DEPTH
            row(l, 0, 0, a["even_norm_2"].rearrange("l (c p) -> (l c) p", p=P), DC)
            for r, name in ((KE_QG, "even_q_gain_2"), (KE_KG, "even_k_gain_2")):
                for h in range(2):
                    row(l, 0, r, a[name], 1, slice(64 * h, 64 * h + 64))
            row(l, 0, KE_SC, a["even_sconv_w_2"].rearrange("l k (c p) -> (l k c) p", p=P), 12)
            row(l + 1, 0, 0, a["odd_norm_2"].rearrange("l (c p) -> (l c) p", p=P), DC)
            row(l + 1, 0, KO_GN, a["ret_gn_gain_2"].rearrange("l h (c p) -> (l h c) p", p=P), 16)
            for j, fn, t2 in ((0, KE_FN, KE_T2), (1, KO_FN, KO_T2)):
                row(l + j, 0, fn, a["ffn_norm_2"][j].rearrange("(c p) -> c p", p=P), DC)
                row(l + j, 0, t2, a["ffn_conv_w_2"][j, 2:3].rearrange("k (c p) -> (k c) p", p=P), 2 * FC)
                row(l + j, 1, 0, a["ffn_conv_w_2"][j, 0:2].rearrange("k (c p) -> (k c) p", p=P), 4 * FC)

            def whole(w, l, kd_, col):
                return [(k0, k0 + 4, w[:, ds(l * kd_ + k0, 4), ds(col, PANEL)]) for k0 in (0, 4)]

            w_in, _ = w_rows("w_in", DC)
            w_gate, _ = w_rows("w_gate", DC)
            w_a, _ = w_rows("w_branch_a", 4)
            w_b, _ = w_rows("w_branch_b", 4)
            w_out, _ = w_rows("w_out", DC)
            w_up, _ = w_rows("w_up", DC)
            w_down, _ = w_rows("w_down", FC)

            def layer(l):
                m0 = l * M_LAYER
                with sp.Fori(0, 4) as i:
                    for s in range(2):
                        load(sp, m0 + i, s, whole(w_in, l, DC, i * 512 + s * PANEL))
                for i, col in ((4, C_BQ), (5, C_IQ)):
                    for s in range(2):
                        load(sp, m0 + i, s, whole(w_in, l, DC, col + s * PANEL))
                with sp.Fori(0, 4) as i:
                    for s in range(2):
                        load(sp, m0 + M_GATE + i, s, whole(w_gate, l, DC, i * 512 + s * PANEL))
                with sp.Fori(0, 2) as i:
                    for s in range(2):
                        cols = ds(i * 512 + s * PANEL, PANEL)
                        load(sp, m0 + M_BRANCH + i, s, [(0, 4, w_a[:, ds(l * 4, 4), cols]), (4, 8, w_b[:, ds(l * 4, 4), cols])])
                with sp.Fori(0, 2) as i:
                    for s in range(2):
                        load(sp, m0 + M_OUT + i, s, whole(w_out, l, DC, i * 512 + s * PANEL))
                with sp.Fori(0, 11) as i:
                    for s in range(2):
                        load(sp, m0 + M_UP + i, s, whole(w_up, l, DC, i * PANEL + s * FF))
                with sp.Fori(0, 2) as i:
                    for p in range(6):
                        k0, n = DOWN_K[p % 3]
                        cols = ds(i * 512 + (p // 3) * PANEL, PANEL)
                        load(sp, m0 + M_DOWN + 3 * i + p // 2, p % 2,
                             [(h, h + n // 2, w_down[:, ds(l * FC + k0 + h, n // 2), cols]) for h in (0, n // 2)])

            with sp.Fori(0, DEPTH) as l:
                layer(l)

            def mlp2(j, m):
                up = a["ffn_w_up_2"].rearrange("l (k p) n -> p (l k) n", p=P)
                down = a["ffn_w_down_2"].rearrange("l (k p) n -> p (l k) n", p=P)
                with sp.Fori(0, 11) as i:
                    for s in range(2):
                        load(sp, m + i, s, whole(up, j, DC, i * PANEL + s * FF))
                with sp.Fori(0, 2) as i:
                    for p in range(6):
                        k0, n = DOWN_K[p % 3]
                        cols = ds(i * 512 + (p // 3) * PANEL, PANEL)
                        load(sp, m + 11 + 3 * i + p // 2, p % 2,
                             [(h, h + n // 2, down[:, j * FC + k0 + h:j * FC + k0 + h + n // 2, cols]) for h in (0, n // 2)])

            def columns(name, m, pairs):
                w = a[name].rearrange("l (k p) n -> p (l k) n", p=P)
                with sp.Fori(0, pairs) as i:
                    for s in range(2):
                        load(sp, m + i, s, whole(w, 0, DC, i * 512 + s * PANEL))

            columns("even_w_in_2", M_E, 6)
            columns("even_w_out_2", M_E + E_OUT, 2)
            mlp2(0, M_E + E_UP)
            columns("ret_wq_2", M_O, 2)
            columns("ret_wk_2", M_O + O_K, 2)
            columns("ret_wv_2", M_O + O_V, 4)
            columns("ret_wg_2", M_O + O_G, 4)
            w_o = a["ret_wo_2"].rearrange("l (k p) n -> p (l k) n", p=P)
            with sp.Fori(0, 4) as i:
                for s in range(2):
                    load(sp, M_O + O_OUT + i, s, [(k0, k0 + 4, w_o[:, 8 * s + k0:8 * s + k0 + 4, ds(i * PANEL, PANEL)]) for k0 in (0, 4)])
            mlp2(1, M_O + O_UP)
            sp.wait_ge(sem["out_ready"], 4)
            sp.dma_start(out.rearrange("(j p) d -> p j d", p=P), outT[:, :, :]).then_inc(sem["stored"], 16)
            sp.wait_ge(sem["stored"], 16)

        @block.gpsimd
        def _(pool):
            w = a["w_in"].rearrange("l (k p) n -> p (l k) n", p=P)
            for l in range(DEPTH):
                if l:
                    pool.wait_ge(sem["panel_done"], at("panel_done", l - 1, 2 * M_OUT + 2))
                for to, of, n in ((S_IK, C_IK, 64), (S_IK + 64, C_IK, 64), (S_BK, C_BK, 2 * P), (S_AB, C_AB, 8), (S_AB + 8, C_IK + 64, 8)):
                    pool.dma_start(wS[:, :, to:to + n], w[:, l * DC:(l + 1) * DC, of:of + n]).then_inc(sem["small_in"], 16)
            pool.wait_ge(sem["small_in"], DEPTH * 80)
            pool.wait_ge(sem["nl"], DEPTH * PER["nl"])
            pool.dma_start(c2[:, :], a["c2"]).then_inc(sem["c2_in"], 16)
            pool.wait_ge(sem["c2_in"], 16)

        @block.tensor
        def _(pe):
            def begin(name, l, it=0):
                b, n = PLACE[name]
                pe.wait_ge(aux_read[b], l * AUX_PER[b] + n + it * 2 - 1)
                return aux[b]

            def mm(o_, l_, r_, start=True, stop=True):
                return nc.tensor.matmul(o_, l_, r_, start=start, stop=stop)

            pe.sem_inc(sem["whi_used"], 2)
            pe.sem_inc(sem["panel_done"], 2)
            pe.wait_ge(sem["start_in"], 48)
            for c in range(DC):
                if c >= 4:
                    pe.wait_ge(sem["h0"], c - 3)
                cols = slice(c * P, c * P + P)
                nc.tensor.transpose(lin[c % 4][:, 0:META], metain[:, cols], ident[0:META, 0:META])
                for j in range(2):
                    t = nc.tensor.transpose(lin[c % 4][:, META + j * P:META + (j + 1) * P], xin[:, j, cols], ident)
                t.then_inc(sem["turned"], 1)
            pe.wait_ge(sem["rows"], (DEPTH * 12 + 14) * 16)
            for l in range(2 * DEPTH):
                pe.wait_ge(sem["h0"], 5 + l)
                nc.tensor.transpose(lin[l][:, 0:P], rows[:, l, 0, :], ident)
                nc.tensor.transpose(lin[l][:, P:2 * P], rows[:, l, 1, :], ident).then_inc(sem["turned"], 1)

            def mean_square(name, l, which):
                pe.wait_ge(sem["sq"], at("sq", l, which))
                ps = begin(name, l)
                for c in range(DC):
                    t = mm(ps[:, 0:T], ones, sq8[:, c, :], c == 0, c == DC - 1)
                t.then_inc(filled(name), 1)

            def layer(l):
                m0, r0 = l * M_LAYER, l * R_LAYER
                mean_square("ms1", l, 1)
                pe.wait_ge(sem["n"], at("n", l, DC))
                pe.wait_ge(sem["small_in"], at("small_in", l, 80))
                for name, col in (("ik", S_IK), ("bk", S_BK)):
                    ps = begin(name, l)
                    for k in range(DC):
                        t = mm(ps[:, 0:T], wS[:, k, col:col + P], nT[:, k, :], k == 0, k == DC - 1)
                    t.then_inc(filled(name), 1)
                for name, col, n in (("bv", S_BV, P), ("ab", S_AB, 16)):
                    ps = begin(name, l)
                    for b in range(3):
                        for k in range(DC):
                            t = mm(ps[0:TB[b][1], b * n:(b + 1) * n], nT[:, k, tok(b)], wS[:, k, col:col + n], k == 0, k == DC - 1)
                    t.then_inc(filled(name), 1)
                pe.wait_ge(sem["nl"], at("nl", l, 2))
                stand(pe, "pe_stood")
                with pe.Fori(0, 6) as i:
                    for s in range(2):
                        multiply(pe, m0 + i, s, r0 + i, halves(s, nH, nL), T)

                pe.wait_ge(sem["sq_heads"], at("sq_heads", l, 1))
                for h in range(8):
                    name = f"ss{'qk'[h // 4]}{h % 4}"
                    mm(begin(name, l)[:, 0:T], ones, sq8[:, h, :]).then_inc(filled(name), 1)
                pe.wait_ge(sem["sq_att"], at("sq_att", l, 1))
                for h, name in enumerate([f"sbq{h}" for h in range(4)] + ["sbk", "sik"]):
                    mm(begin(name, l)[:, 0:T], ones, sq_att[:, h, :]).then_inc(filled(name), 1)

                def gate(i):
                    for s in range(2):
                        multiply(pe, m0 + M_GATE + i, s, r0 + R_GATE + i, halves(s, nH, nL), T)

                gate(0)
                pe.wait_ge(sem["gt"], at("gt", l, 1))
                ps = begin("gc", l)
                for b in (1, 2, 0):
                    n = TB[b][1]
                    t = mm(ps[0:n, 4 * b:4 * b + 4], const("upto", n, n), gg[0:n, b, :])
                t.then_inc(filled("gc"), 1)
                for b in range(3):
                    n = TB[b][1]
                    for name, src, count in ((f"gb{b}", gtri, 2 + b), (f"bb{b}", bdiag, 5 + b)):
                        pe.wait_ge(sem["gt"], at("gt", l, count))
                        mm(begin(name, l)[:, 0:4 * n], ones[0:n, :], src[b].rearrange("p h c -> p (h c)")).then_inc(filled(name), 1)
                pe.wait_ge(sem["qk_unit"], at("qk_unit", l, 2))
                for b in range(3):
                    n = TB[b][1]
                    for name, off in ((f"kk{b}", 4), (f"qk{b}", 0)):
                        ps = begin(name, l)
                        for h in range(4):
                            t = mm(ps[0:n, h * n:(h + 1) * n], cT[:, 4 + h, tok(b)], cT[:, off + h, tok(b)])
                        t.then_inc(filled(name), 1)
                for b in range(3):
                    n = TB[b][1]
                    for name, off in ((f"kt{b}", 4), (f"vt{b}", 8)):
                        ps = begin(name, l)
                        if off == 8 and b == 0:
                            pe.wait_ge(sem["silu"], at("silu", l, 3))
                        for h in range(4):
                            t = nc.tensor.transpose(ps[0:n, h * P:(h + 1) * P], cT[:, off + h, tok(b)], ident)
                        t.then_inc(filled(name), 1)
                gate(1)
                pe.wait_ge(sem["att_unit"], at("att_unit", l, 3))
                for h in range(4):
                    mm(begin(f"rq{h}", l)[:, 0:T], const("turn_a", P), rawT[:, 16 + h, :]).then_inc(filled(f"rq{h}"), 1)
                pe.wait_ge(lin_read[3], r0 + 6)
                for c in range(4):
                    mm(begin(f"ri{c}", l)[:, 0:T], const("turn_i", P), rawT[:, 20 + c, :]).then_inc(filled(f"ri{c}"), 1)
                mm(begin("rk", l)[:, 0:T], const("turn_a", P), bkr[:, :]).then_inc(filled("rk"), 1)
                mm(begin("rik", l)[:, 0:T], const("turn_i", P), ikr[:, :]).then_inc(filled("rik"), 1)
                gate(2)
                pe.wait_ge(sem["rope"], at("rope", l, 4))
                for j in range(2):
                    for e in range(4):
                        name = f"ix{j}{e}"
                        ps = begin(name, l)
                        for n in range(2):
                            h = 4 * (e // 2) + e % 2 + 2 * n
                            r = 64 * (h % 2)
                            t = mm(ps[:, n * SEQ:(n + 1) * SEQ], rawT[r:r + 64, 20 + h // 2, tok(j + 1)], ikr[r:r + 64, META:T])
                        t.then_inc(filled(name), 1)
                with pe.Fori(0, LEVELS) as it:
                    for b in range(3):
                        n = TB[b][1]
                        pe.wait_ge(sem["ml"], at("ml", l, it * 3 + b + 1))
                        ps = begin(f"Y{b}", l, it)
                        if b == 0:
                            stand(pe, "pe_stood")
                        for h in range(4):
                            t = mm(ps[0:n, h * n:(h + 1) * n], ML[b][:, h, :], X[b][:, h, :])
                        t.then_inc(filled(f"Y{b}"), 1)
                    pe.wait_ge(*read("Y0", l, it))
                    ps = begin("XA0", l, it)
                    stand(pe, "pe_stood")
                    for h in range(4):
                        mm(ps[0:META, h * META:(h + 1) * META], A[0][:, h, :], Y[0][:, h, :])
                        t = mm(ps[0:META, (4 + h) * META:(5 + h) * META], Y[0][:, h, :], A[0][:, h, :])
                    t.then_inc(filled("XA0"), 1)
                    for b in (1, 2):
                        pe.wait_ge(*read(f"Y{b}", l, it))
                        for name, lhs, rhs in ((f"X{b}", A, Y), (f"A{b}", Y, A)):
                            ps = begin(name, l, it)
                            for h in range(4):
                                t = mm(ps[:, h * P:(h + 1) * P], lhs[b][:, h, :], rhs[b][:, h, :])
                            t.then_inc(filled(name), 1)
                gate(3)
                for b in range(3):
                    n = TB[b][1]
                    rhs = vt[0:n, 0] if b == 0 else R
                    if b:
                        pe.wait_ge(*read(f"dS{b - 1}", l))
                        ps = begin(f"kS{b}", l)
                        for h in range(4):
                            t = mm(ps[:, h * P:(h + 1) * P], cT[:, 4 + h, tok(b)], S[:, h, :])
                        t.then_inc(filled(f"kS{b}"), 1)
                        pe.wait_ge(*read(f"kS{b}", l))
                    pe.wait_ge(sem["ab_ready"], at("ab_ready", l, b + 1))
                    ps = begin(f"vn{b}", l)
                    if b == 0:
                        stand(pe, "pe_stood")
                    for h in range(4):
                        t = mm(ps[0:n, h * P:(h + 1) * P], A[b][:, h, :], rhs[:, h, :])
                    t.then_inc(filled(f"vn{b}"), 1)
                    pe.wait_ge(*read(f"vn{b}", l))
                    pe.wait_ge(sem["qe"], at("qe", l, 1))
                    ps = begin(f"o{b}", l)
                    for h in range(4):
                        if b:
                            mm(ps[:, h * n:(h + 1) * n], S[:, h, :], cT[:, h, tok(b)], True, False)
                        t = mm(ps[:, h * n:(h + 1) * n], vn[0:n, h, :], QD[b][:, h, :], b == 0, True)
                    t.then_inc(filled(f"o{b}"), 1)
                    if b < 2:
                        ps = begin(f"dS{b}", l)
                        for h in range(4):
                            t = mm(ps[:, h * P:(h + 1) * P], kd[0:n, b, h, :], vn[0:n, h, :])
                        t.then_inc(filled(f"dS{b}"), 1)
                ps = begin("s0", l)
                for h in range(4):
                    t = mm(ps[0:META, h * META:(h + 1) * META], rawT[:, 16 + h, 0:META], bkr[:, 0:META])
                t.then_inc(filled("s0"), 1)
                pe.wait_ge(sem["pn"], at("pn", l, 1))
                ps = begin("pt0", l)
                stand(pe, "pe_stood")
                for h in range(4):
                    t = nc.tensor.transpose(ps[0:META, h * META:(h + 1) * META], P0[:, h, :], ident[0:META, 0:META])
                t.then_inc(filled("pt0"), 1)
                pe.wait_ge(*read("pt0", l))
                mm(begin("pv0", l)[:, 0:4 * META], vtok[0:META, 0, :], PT[0:META, 0, 0:4 * META]).then_inc(filled("pv0"), 1)
                for j in (1, 2):
                    for h in range(4):
                        name = f"s{'abcd'[h]}{j}"
                        mm(begin(name, l)[:, 0:T], rawT[:, 16 + h, tok(j)], bkr[:, :]).then_inc(filled(name), 1)
                    pe.wait_ge(sem["pn"], at("pn", l, 1 + j))
                    for b in range(3):
                        name = f"pt{b}_{j}"
                        ps = begin(name, l)
                        for h in range(4):
                            t = nc.tensor.transpose(ps[0:TB[b][1], h * P:(h + 1) * P], Pm[:, h, tok(b)], ident)
                        t.then_inc(filled(name), 1)
                    ps = begin(f"pv{j}", l)
                    for b in range(3):
                        n = TB[b][1]
                        pe.wait_ge(*read(f"pt{b}_{j}", l))
                        t = mm(ps[:, :], vtok[0:n, b, :], PT[0:n, b, :], b == 0, b == 2)
                    t.then_inc(filled(f"pv{j}"), 1)
                pe.wait_ge(sem["sqo"], at("sqo", l, 1))
                for h in range(4):
                    mm(begin(f"so{h}", l)[:, 0:T], ones, sqo[:, h, :]).then_inc(filled(f"so{h}"), 1)
                pe.wait_ge(sem["oa_l"], at("oa_l", l, 1))
                pe.wait_ge(*read("pv2", l))
                stand(pe, "pe_stood")
                with pe.Fori(0, 2) as i:
                    for s in range(2):
                        multiply(pe, m0 + M_BRANCH + i, s, r0 + R_BRANCH + 2 * i + s,
                                 [(2 * br + c, slice(c * P, c * P + P), [(4 * br + k, oH[:, 4 * br + k, :], oL[:, 4 * br + k, :]) for k in range(4)])
                                  for br in range(2) for c in range(2)], T)
                pe.wait_ge(sem["yl"], at("yl", l, 4))
                stand(pe, "pe_stood")
                with pe.Fori(0, 2) as i:
                    for s in range(2):
                        multiply(pe, m0 + M_OUT + i, s, r0 + R_OUT + i, halves(s, nH, nL), T)
                mean_square("ms2", l, 2)
                pe.wait_ge(sem["nl"], at("nl", l, 4))
                stand(pe, "pe_stood")
                with pe.Fori(0, 11) as i:
                    for s in range(2):
                        multiply(pe, m0 + M_UP + i, s, r0 + R_UP + i, halves(s, nH, nL), T)
                pe.wait_ge(sem["al"], at("al", l, FC))
                stand(pe, "pe_stood")
                with pe.Fori(0, 2) as i:
                    for p in range(6):
                        k0, n = DOWN_K[p % 3]
                        multiply(pe, m0 + M_DOWN + 3 * i + p // 2, p % 2, r0 + R_DOWN + i, 
                                 [(2 * (p // 3) + c, slice(c * P, c * P + P), [(k, aH[:, k0 + k, :], aL[:, k0 + k, :]) for k in range(n)])
                                  for c in range(2)], T, start=p % 3 == 0, stop=p % 3 == 2)

            with pe.Fori(0, DEPTH) as l:
                layer(l)

            L = DEPTH

            def multiply_tok(m, s, rnd):
                pe.wait_ge(sem["whi"], 2 * m + s + 1)
                for j in range(2):
                    pe.wait_ge(lin_read[2 * s + j], rnd)
                    to, rows_ = lin[2 * s + j][:, 0:PANEL], slice(j * P, j * P + P)
                    for k in range(DC):
                        mm(to, nH[:, k, rows_], wH[:, s, k, :], k == 0, False)
                        t = mm(to, nL[:, k, rows_], wH[:, s, k, :], False, False)
                t.then_inc(sem["whi_used"], 1)
                pe.wait_ge(sem["wlo"], 2 * m + s + 3)
                for j in range(2):
                    for k in range(DC):
                        t = mm(lin[2 * s + j][:, 0:PANEL], nH[:, k, j * P:j * P + P], wL[:, s, k, :], False, k == DC - 1)
                t.then_inc(sem["panel_done"], 1)

            nH2, nL2 = nH[:, :, 0:SEQ], nL[:, :, 0:SEQ]

            def mean_square2(name, which, sq):
                pe.wait_ge(sem["sq2"], which)
                ps = begin(name, L)
                for c in range(DC):
                    t = mm(ps[:, 0:SEQ], ones, sq[:, c, :], c == 0, c == DC - 1)
                t.then_inc(filled(name), 1)

            def mlp2(name, which, m, r):
                mean_square2(name, which, sqf)
                pe.wait_ge(sem["nl2"], 2 * which)
                with pe.Fori(0, 11) as i:
                    for s in range(2):
                        multiply(pe, m + i, s, r + i, halves(s, nH2, nL2), SEQ)
                pe.wait_ge(sem["al2"], FC * which // 2)
                with pe.Fori(0, 2) as i:
                    for p in range(6):
                        k0, n = DOWN_K[p % 3]
                        multiply(pe, m + 11 + 3 * i + p // 2, p % 2, r + 11 + i,
                                 [(2 * (p // 3) + c, slice(c * P, c * P + P), [(k, aH2[:, k0 + k, :], aL2[:, k0 + k, :]) for k in range(n)])
                                  for c in range(2)], SEQ, start=p % 3 == 0, stop=p % 3 == 2)

            mean_square2("ems", 1, sqe)
            pe.wait_ge(sem["nl2"], 2)
            with pe.Fori(0, 2) as i:
                for s in range(2):
                    multiply(pe, M_E + i, s, R_E + i, halves(s, nH2, nL2), SEQ)
            for s in range(2):
                multiply_tok(M_E + 2, s, R_E + 2)
            with pe.Fori(3, 6) as i:
                for s in range(2):
                    multiply(pe, M_E + i, s, R_E + i, halves(s, nH2, nL2), SEQ)
            pe.wait_ge(sem["esq"], 1)
            for c in range(4):
                mm(begin(f"eq{c}", L)[:, :], const("half", P), sqe[:, 2 * c:2 * c + 2, :].rearrange("p c t -> p (c t)")).then_inc(filled(f"eq{c}"), 1)
            pe.wait_ge(sem["eunit"], 2)
            pe.wait_ge(lin_read[3], R_E + 3)
            for j in range(2):
                keys = (j + 1) * P
                for e, heads in enumerate([(0, 2, 4, 6), (1, 3, 5, 7)] if j == 0 else [(0, 2), (1, 3), (4, 6), (5, 7)]):
                    name = f"e{j}{e}"
                    ps = begin(name, L)
                    for n, h in enumerate(heads):
                        r = 64 * (h % 2)
                        t = mm(ps[:, n * keys:(n + 1) * keys], raw8[r:r + 64, h // 2, j * P:j * P + P], raw8[r:r + 64, 4 + h // 2, 0:keys])
                    t.then_inc(filled(name), 1)
                pe.wait_ge(sem["epn"], 1 + j)
                for g in range(2):
                    for b in range(j + 1):
                        name = f"et{j}{g}" + (str(b) if j else "")
                        ps = begin(name, L)
                        for h in range(4):
                            t = nc.tensor.transpose(ps[:, h * P:(h + 1) * P], Pe[:, 4 * g + h, b * P:b * P + P], ident)
                        t.then_inc(filled(name), 1)
                name = f"et{j}1" + ("1" if j else "")
                pe.wait_ge(*read(name, L))
                if j:
                    pe.wait_ge(*read("et101", L))
                    pe.wait_ge(*read("et100", L))
                    pe.wait_ge(*read("et110", L))
                else:
                    pe.wait_ge(*read("et00", L))
                ps = begin(f"ev{j}", L)
                for h in range(8):
                    r = 64 * (h % 2)
                    for b in range(j + 1):
                        t = mm(ps[r:r + 64, (h // 2) * P:(h // 2 + 1) * P], vtk[:, b, h * 64:h * 64 + 64], PTe[:, b, h * P:(h + 1) * P], b == 0, b == j)
                t.then_inc(filled(f"ev{j}"), 1)
            pe.wait_ge(*read("ev1", L))
            pe.wait_ge(sem["eb_l"], 1)
            with pe.Fori(0, 2) as i:
                for s in range(2):
                    multiply(pe, M_E + E_OUT + i, s, R_E + E_OUT + i, halves(s, eH, eL), SEQ)
            mlp2("emf", 2, M_E + E_UP, R_E + E_UP)

            mean_square2("oms", 3, sqo2)
            pe.wait_ge(sem["nl2"], 6)
            with pe.Fori(0, 4) as i:
                for s in range(2):
                    multiply(pe, M_O + i, s, R_O + i, halves(s, nH2, nL2), SEQ)
            with pe.Fori(O_V, O_G) as i:
                for s in range(2):
                    multiply_tok(M_O + i, s, R_O + i)
            pe.wait_ge(sem["orot"], 4)
            for h in range(4):
                ps = begin(f"os{h}", L)
                for b in range(2):
                    to = ps[:, 0:SEQ] if b == 0 else ps[:, SEQ:SEQ + P]
                    for d in range(2):
                        t = mm(to, qk2[:, 1, h, d, b * P:b * P + P], qk2[:, 0, h, d, b * P:SEQ], d == 0, d == 1)
                t.then_inc(filled(f"os{h}"), 1)
            with pe.Fori(O_G, O_OUT) as i:
                for s in range(2):
                    multiply(pe, M_O + i, s, R_O + i, halves(s, nH2, nL2), SEQ)
            for h in range(4):
                pe.wait_ge(*read(f"os{h}", L))
                if h == 0:
                    pe.wait_ge(lin_read[3], R_O + O_G)
                for e in range(2):
                    name = f"oo{h}{e}"
                    ps = begin(name, L)
                    for n in range(2):
                        cols = slice(h * 512 + (2 * e + n) * P, h * 512 + (2 * e + n + 1) * P)
                        mm(ps[:, n * SEQ:(n + 1) * SEQ], vtk2[:, 0, cols], sc[:, h, 0:SEQ], True, False)
                        t = mm(ps[:, n * SEQ + P:(n + 1) * SEQ], vtk2[:, 1, cols], sc[:, h, SEQ:SEQ + P], False, True)
                    t.then_inc(filled(name), 1)
            for h in range(4):
                pe.wait_ge(*read(f"oo{h}0", L))
                pe.wait_ge(*read(f"oo{h}1", L))
                ps = begin(f"om{h}", L)
                for e in range(4):
                    t = mm(ps[:, 0:SEQ], ones, oR[:, 4 * h + e, :], e == 0, e == 3)
                t.then_inc(filled(f"om{h}"), 1)
            for h in range(4):
                pe.wait_ge(sem["osq"], h + 1)
                ps = begin(f"ow{h}", L)
                for e in range(4):
                    t = mm(ps[:, 0:SEQ], ones, sq4[:, e, :], e == 0, e == 3)
                t.then_inc(filled(f"ow{h}"), 1)
            pe.wait_ge(sem["og_l"], 4)
            with pe.Fori(0, 2) as i:
                for q in range(2):
                    for s in range(2):
                        multiply(pe, M_O + O_OUT + 2 * i + q, s, R_O + RO_OUT + i,
                                 [(2 * q + c, slice(c * P, c * P + P), [(k, gH[:, 8 * s + k, :], gL[:, 8 * s + k, :]) for k in range(DC)])
                                  for c in range(2)], SEQ, start=s == 0, stop=s == 1)
            mlp2("omf", 4, M_O + O_UP, R_O + RO_UP)
            for j in range(2):
                for q in range(2):
                    b = 2 * j + q
                    pe.wait_ge(lin_read[3], R_ALL)
                    for c in range(4):
                        t = nc.tensor.transpose(lin[b][:, c * P:(c + 1) * P], hT[:, 4 * q + c, META + j * P:META + (j + 1) * P], ident)
                    t.then_inc(sem["turned_back"], 1)

        @block.scalar
        def _(act):
            own = Own(act, sem["act_own"])
            Exp, Ln, Copy, Square, Silu, Relu = ACT.Exp, ACT.Ln, ACT.Copy, ACT.Square, ACT.Silu, ACT.Relu
            f = nc.scalar.activation

            for c in range(DC):
                act.wait_ge(sem["turned"], c + 1)
                f(hT[:, c, :], lin[c % 4][:, 0:T], Copy).then_inc(sem["h0"], 1)
            for l in range(2 * DEPTH):
                act.wait_ge(sem["turned"], DC + 1 + l)
                f(par[:, l, :], lin[l][:, 0:2 * P], Copy).then_inc(sem["h0"], 1)
            f(rates[:, :, 4:8], rates[:, :, 4:8], Exp).then_inc(sem["h0"], 1)
            act.wait_ge(sem["h0"], DC)
            for s in range(2):
                split_hi(act, 0, s)

            def norm(l, which, name, h_round):
                act.wait_ge(lin_read[3], h_round)
                f(sq8[:, :, :], hT[:, :, :], Square).then_inc(sem["sq"], 1)
                act.wait_ge(*full(name, l))
                f(rs[:, :], bank(name)[:, 0:T], Ln, bias=eps_col, scale=1.0 / D).then_inc(emptied(name), 1)
                act.wait_ge(*read(name, l))
                f(rs[:, :], rs[:, :], Exp, scale=-0.5).then_inc(sem["rstd"], 1)
                for g in range(2):
                    act.wait_ge(sem["n"], at("n", l, DC * (which - 1) + 4 * g + 4))
                    f(nH[:, 4 * g:4 * g + 4, :], nT[:, 4 * g:4 * g + 4, :], Copy).then_inc(sem["nh"], 1)

            def layer(l):
                own.base, own.n = l * PER["act_own"], 0
                m0, r0 = l * M_LAYER, l * R_LAYER
                norm(l, 1, "ms1", r0)
                for name, to in (("ik", ikr), ("bk", bkr)):
                    act.wait_ge(*full(name, l))
                    f(to[:, :], bank(name)[:, 0:T], Copy).then_inc(emptied(name), 1)
                for name, to, n in (("bv", vtok, P), ("ab", ab, 16)):
                    act.wait_ge(*full(name, l))
                    own.done(f(to[0:META, 0, :], bank(name)[0:META, 0:n], Copy))
                    f(to[:, 1:3, :], bank(name)[:, n:3 * n].rearrange("p (b n) -> p b n", b=2), Copy).then_inc(emptied(name), 1)
                with act.Fori(0, 6) as i:
                    for s in range(2):
                        split_hi(act, m0 + i + 1, s)
                        act.wait_ge(sem["panel_done"], 2 * (m0 + i) + s + 3)
                        for c in range(2):
                            b = 2 * s + c
                            f(rawT[:, ds(4 * i + b, 1), :], lin[b][:, 0:T].unsqueeze(1), Copy).then_inc(lin_read[b], 1)
                for g in range(3):
                    act.wait_ge(sem["conv"], at("conv", l, 4 * g + 4))
                    f(cT[:, 4 * g:4 * g + 4, :], cT[:, 4 * g:4 * g + 4, :], Silu).then_inc(sem["silu"], 1)
                act.wait_ge(lin_read[3], r0 + 6)
                f(zT[:, :, :], rawT[:, 12:16, :], Silu).then_inc(sem["silu"], 1)
                act.wait_ge(sem["silu"], at("silu", l, 2))
                f(sq8[:, :, :], cT[:, 0:8, :], Square).then_inc(sem["sq_heads"], 1)
                f(sq_att[:, 0:4, :], rawT[:, 16:20, :], Square)
                act.wait_ge(*read("bk", l))
                f(sq_att[:, 4, :], bkr[:, :], Square)
                f(sq_att[:, 5, :], ikr[:, :], Square).then_inc(sem["sq_att"], 1)
                act.wait_ge(sem["sp_in"], at("sp_in", l, 1))
                own.done(f(gl[:, :, :], gm[:, :, :], Exp))
                own.wait()
                f(gl[:, :, :], gl[:, :, :], Ln, bias=c1[:, consts_at1["cols"] + 2:consts_at1["cols"] + 3])
                f(bt[:, :, :], ab[:, :, 4:8], Exp, scale=-1.0).then_inc(sem["sp_ln"], 1)
                for names, to, scale, bias_ in (
                    ([f"ssq{h}" for h in range(4)], rnq, 1.0, lnq_col),
                    ([f"ssk{h}" for h in range(4)], rnk, 1.0, 0.0),
                    ([f"sbq{h}" for h in range(4)] + ["sbk"], rnb, 1.0 / P, 0.0),
                ):
                    for h, name in enumerate(names):
                        act.wait_ge(*full(name, l))
                        f(to[:, h, :], bank(name)[:, 0:T], Ln, bias=eps_col, scale=scale).then_inc(emptied(name), 1)
                    act.wait_ge(*read(names[-1], l))
                    f(to[:, :, :], to[:, :, :], Exp, scale=-0.5, bias=bias_).then_inc(sem["rn"], 1)
                act.wait_ge(*full("sik", l))
                f(rni[:, :], bank("sik")[:, 0:T], Ln, bias=eps_col, scale=1.0 / P).then_inc(emptied("sik"), 1)
                act.wait_ge(*read("sik", l))
                f(rni[:, :], rni[:, :], Exp, scale=-0.5).then_inc(sem["rn"], 1)

                def gate(i):
                    for s in range(2):
                        split_hi(act, m0 + M_GATE + i + 1, s)
                        act.wait_ge(sem["panel_done"], 2 * (m0 + M_GATE + i) + s + 3)
                        for c in range(2):
                            b = 2 * s + c
                            f(rawT[:, 4 * i + b, :], lin[b][:, 0:T], Exp, scale=-1.0, bias=pc(K_NB + 4 * i + b)).then_inc(lin_read[b], 1)

                gate(0)
                act.wait_ge(*full("gc", l))
                own.done(f(gcs[0:META, 0, :], bank("gc")[0:META, 0:4], Copy))
                f(gcs[:, 1:3, :], bank("gc")[:, 4:12].rearrange("p (b h) -> p b h", b=2), Copy).then_inc(emptied("gc"), 1)
                act.wait_ge(*read("gc", l))
                f(egt[:, :, :], gcs[:, :, :], Exp).then_inc(sem["eg"], 1)
                for b in range(3):
                    n = TB[b][1]
                    act.wait_ge(*full(f"gb{b}", l))
                    f(eg[:, :, tok(b)], bank(f"gb{b}")[:, 0:4 * n].rearrange("p (h c) -> p h c", h=4), Exp).then_inc(sem["eg"], 1)
                    act.wait_ge(*read(f"gb{b}", l))
                    f(decay[b], decay[b], Exp).then_inc(sem["dec"], 1)
                f(kdx[:, :, :], kdx[:, :, :], Exp).then_inc(sem["kdx"], 1)
                for b in range(3):
                    n = TB[b][1]
                    act.wait_ge(*full(f"vt{b}", l))
                    f(vt[0:n, b], bank(f"vt{b}")[0:n, :].rearrange("p (h d) -> p h d", h=4), Copy).then_inc(emptied(f"vt{b}"), 1)
                gate(1)
                gate(2)
                for j in range(2):
                    for e in range(4):
                        name = f"ix{j}{e}"
                        act.wait_ge(*full(name, l))
                        if 4 * j + e >= 2:
                            act.wait_ge(sem["score"], at("score", l, 4 * j + e - 1))
                        f(rl[:, e % 2, :], bank(name)[:, :], Relu).then_inc(emptied(name), 1)
                with act.Fori(0, LEVELS) as it:
                    for b in range(3):
                        n = TB[b][1]
                        act.wait_ge(*full(f"Y{b}", l, it))
                        f(Y[b], bank(f"Y{b}")[0:n, 0:4 * n].rearrange("p (h c) -> p h c", h=4), Copy).then_inc(emptied(f"Y{b}"), 1)
                gate(3)
                for b in range(3):
                    n = TB[b][1]
                    act.wait_ge(*full(f"vn{b}", l))
                    f(vn[0:n], bank(f"vn{b}")[0:n, :].rearrange("p (h d) -> p h d", h=4), Copy).then_inc(emptied(f"vn{b}"), 1)
                    act.wait_ge(sem["qe"], at("qe", l, 1))
                    act.wait_ge(*full(f"o{b}", l))
                    f(oA[:, :, tok(b)], bank(f"o{b}")[:, 0:4 * n].rearrange("p (h c) -> p h c", h=4), Copy).then_inc(emptied(f"o{b}"), 1)
                act.wait_ge(*read("o2", l))
                f(sqo[:, :, :], oA[:, :, :], Square).then_inc(sem["sqo"], 1)
                act.wait_ge(sem["nmx"], at("nmx", l, 1))
                for h in range(4):
                    e = f(P0[:, h, :], bank("s0")[0:META, h * META:(h + 1) * META], Exp, scale=P ** -0.5, bias=nmx[0:META, h:h + 1], accum_out=sm[0:META, h:h + 1])
                e.then_inc(emptied("s0"), 1)
                act.wait_ge(*full("pt0", l))
                f(PT[0:META, 0, 0:4 * META], bank("pt0")[0:META, 0:4 * META], Copy).then_inc(emptied("pt0"), 1)
                act.wait_ge(*full("pv0", l))
                f(oH[:, 4:8, tok(0)], bank("pv0")[:, 0:4 * META].rearrange("p (h c) -> p h c", h=4), Copy).then_inc(sem["ob_h"], 1)
                for j in (1, 2):
                    act.wait_ge(sem["nmx"], at("nmx", l, 1 + j))
                    for h in range(4):
                        e = f(Pm[:, h, :], Pm[:, h, :], Exp, scale=P ** -0.5, bias=nmx[:, h:h + 1], accum_out=sm[:, h:h + 1])
                    e.then_inc(sem["soft"], 1)
                    for b in range(3):
                        n = TB[b][1]
                        act.wait_ge(*full(f"pt{b}_{j}", l))
                        f(PT[0:n, b, :], bank(f"pt{b}_{j}")[0:n, :], Copy).then_inc(emptied(f"pt{b}_{j}"), 1)
                    act.wait_ge(*full(f"pv{j}", l))
                    f(oH[:, 4:8, tok(j)], bank(f"pv{j}")[:, :].rearrange("p (h c) -> p h c", h=4), Copy).then_inc(sem["ob_h"], 1)
                for h in range(4):
                    act.wait_ge(*full(f"so{h}", l))
                    f(rno[:, h, :], bank(f"so{h}")[:, 0:T], Ln, bias=eps_col, scale=1.0 / P).then_inc(emptied(f"so{h}"), 1)
                act.wait_ge(*read("so3", l))
                f(rno[:, :, :], rno[:, :, :], Exp, scale=-0.5).then_inc(sem["rno"], 1)
                act.wait_ge(sem["oa"], at("oa", l, 1))
                f(oH[:, 0:4, :], oA[:, :, :], Copy).then_inc(sem["oa_h"], 1)
                with act.Fori(0, 2) as i:
                    for s in range(2):
                        split_hi(act, m0 + M_BRANCH + i + 1, s)
                        act.wait_ge(sem["y"], at("y", l, 4 * i + 2 * s + 2))
                        two = ds(4 * i + 2 * s, 2)
                        f(nH[:, two, :], yT[:, two, :], Copy).then_inc(sem["yh"], 1)
                with act.Fori(0, 2) as i:
                    for s in range(2):
                        split_hi(act, m0 + M_OUT + i + 1, s)
                norm(l, 2, "ms2", r0 + R_UP)
                with act.Fori(0, 11) as i:
                    m, r = m0 + M_UP + i, r0 + R_UP + i
                    split_hi(act, m + 1, 0)
                    act.wait_ge(sem["panel_done"], 2 * m + 3)
                    for c in range(2):
                        f(u[:, c, :], lin[c][:, 0:T], Copy, scale=parL[:, ds(K_FCONV + 2 * FC + 2 * i + c, 1)]).then_inc(sem["tap"], 1)
                    split_hi(act, m + 1, 1)
                    for c in range(2):
                        act.wait_ge(lin_read[c], r + 1)
                        f(sg[:, c, :], u[:, c, :], Silu).then_inc(sem["gate_silu"], 1)
                    for c in range(2):
                        act.wait_ge(lin_read[2 + c], r + 1)
                        f(aH[:, ds(2 * i + c, 1), :], av[:, c, :].unsqueeze(1), Copy).then_inc(sem["ah"], 1)
                with act.Fori(0, 2) as i:
                    for p in range(6):
                        split_hi(act, m0 + M_DOWN + 3 * i + p // 2 + 1, p % 2)
                assert own.n == PER["act_own"], own.n

            with act.Fori(0, DEPTH) as l:
                layer(l)

            L = DEPTH
            own.base, own.n = L * PER["act_own"], 0
            h2 = hT[:, :, META:T]

            def norm2(which, name, h_round, sq):
                act.wait_ge(lin_read[3], h_round)
                f(sq[:, :, :], h2, Square).then_inc(sem["sq2"], 1)
                act.wait_ge(*full(name, L))
                f(rs[:, 0:SEQ], bank(name)[:, 0:SEQ], Ln, bias=eps_col, scale=1.0 / D).then_inc(emptied(name), 1)
                act.wait_ge(*read(name, L))
                f(rs[:, 0:SEQ], rs[:, 0:SEQ], Exp, scale=-0.5).then_inc(sem["rstd2"], 1)
                for g in range(2):
                    act.wait_ge(sem["n2"], DC * (which - 1) + 4 * g + 4)
                    f(nH[:, 4 * g:4 * g + 4, 0:SEQ], nT2[:, 4 * g:4 * g + 4, :], Copy).then_inc(sem["nh2"], 1)

            def take(m, s, to, func=Copy):
                split_hi(act, m + 1, s)
                act.wait_ge(sem["panel_done"], 2 * m + s + 3)
                for c in range(2):
                    f(to(c), lin[2 * s + c][:, 0:SEQ].unsqueeze(1), func).then_inc(lin_read[2 * s + c], 1)

            def mlp2(j, m, r, last):
                which = 2 * j + 2
                norm2(which, ("emf", "omf")[j], r, sqf)
                t2 = (KE_T2, KO_T2)[j]
                with act.Fori(0, 11) as i:
                    for s in range(2):
                        split_hi(act, m + i + 1, s)
                        act.wait_ge(sem["panel_done"], 2 * (m + i) + s + 3)
                        for c in range(2):
                            f(u2[:, 2 * s + c, :], lin[2 * s + c][:, 0:SEQ], Copy,
                              scale=par[:, DEPTH + j, ds(t2 + s * FC + 2 * i + c, 1)]).then_inc(sem["tap2"], 1)
                    for c in range(2):
                        act.wait_ge(lin_read[c], r + i + 1)
                        f(sg2[:, c, :], u2[:, c, :], Silu).then_inc(sem["silu2"], 1)
                    for c in range(2):
                        act.wait_ge(sem["conv2"], j * FC + 2 * i + c + 1)
                        f(aH2[:, ds(2 * i + c, 1), :], av2[:, c, :].unsqueeze(1), Copy).then_inc(sem["ah2"], 1)
                if last:
                    for p in range(10):
                        split_hi(act, m + 11 + p // 2 + 1, p % 2)
                else:
                    with act.Fori(0, 2) as i:
                        for p in range(6):
                            split_hi(act, m + 11 + 3 * i + p // 2 + 1, p % 2)

            norm2(1, "ems", R_E, sqe)
            with act.Fori(0, 2) as i:
                for s in range(2):
                    take(M_E + i, s, lambda c: raw8[:, ds(4 * i + 2 * s + c, 1), :])
            for s in range(2):
                take(M_E + 2, s, lambda c: vtk[:, c:c + 1, s * PANEL:(s + 1) * PANEL])
            f(sqe[:, :, :], raw8[:, :, :], Square).then_inc(sem["esq"], 1)
            for s in range(2):
                take(M_E + 3, s, lambda c: gbt[:, 2 * s + c, :].unsqueeze(1))
            for s in range(2):
                take(M_E + 4, s, lambda c: gct[:, 2 * s + c, :].unsqueeze(1))
            for s in range(2):
                split_hi(act, M_E + 6, s)
            for c in range(4):
                act.wait_ge(*full(f"eq{c}", L))
                f(rne[:, 2 * c:2 * c + 2, :], bank(f"eq{c}")[:, :].rearrange("p (c t) -> p c t", c=2), Ln, bias=eps_col, scale=1.0 / 64).then_inc(emptied(f"eq{c}"), 1)
            act.wait_ge(*read("eq2", L))
            act.wait_ge(*read("eq3", L))
            f(rne[:, :, :], rne[:, :, :], Exp, scale=-0.5).then_inc(sem["ern"], 1)
            for j in range(2):
                keys = (j + 1) * P
                act.wait_ge(sem["enmx"], 1 + j)
                for h in range(8):
                    e = f(Pe[:, h, 0:keys], Pe[:, h, 0:keys], Exp, scale=0.125, bias=nmx8[:, h:h + 1])
                e.then_inc(sem["esoft"], 1)
                for g in range(2):
                    for b in range(j + 1):
                        name = f"et{j}{g}" + (str(b) if j else "")
                        act.wait_ge(*full(name, L))
                        f(PTe[:, b, g * 512:(g + 1) * 512], bank(name)[:, :], Copy).then_inc(emptied(name), 1)
                act.wait_ge(*full(f"ev{j}", L))
                f(eH[:, 0:4, j * P:j * P + P], bank(f"ev{j}")[:, :].rearrange("p (c t) -> p c t", c=4), Copy).then_inc(sem["eob_h"], 1)
            act.wait_ge(sem["eb"], 1)
            f(eH[:, 4:8, :], cvt[:, :, :], Copy).then_inc(sem["eb_h"], 1)
            with act.Fori(0, 2) as i:
                for s in range(2):
                    split_hi(act, M_E + E_OUT + i + 1, s)
            mlp2(0, M_E + E_UP, R_E + E_UP, False)

            norm2(3, "oms", R_O, sqo2)
            with act.Fori(0, 2) as i:
                for s in range(2):
                    take(M_O + i, s, lambda c: qk2[:, 0, ds(2 * i + s, 1), c, :])
            with act.Fori(0, 2) as i:
                for s in range(2):
                    take(M_O + O_K + i, s, lambda c: qk2[:, 1, ds(2 * i + s, 1), c, :])
            with act.Fori(0, 4) as i:
                for s in range(2):
                    take(M_O + O_V + i, s, lambda c: vtk2[:, c:c + 1, ds(i * 512 + s * PANEL, PANEL)])
            with act.Fori(0, 4) as i:
                for s in range(2):
                    take(M_O + O_G + i, s, lambda c: sgT[:, ds(4 * i + 2 * s + c, 1), :], Silu)
            for h in range(4):
                for e in range(2):
                    name = f"oo{h}{e}"
                    act.wait_ge(*full(name, L))
                    f(oR[:, 4 * h + 2 * e:4 * h + 2 * e + 2, :], bank(name)[:, :].rearrange("p (c t) -> p c t", c=2), Copy).then_inc(emptied(name), 1)
            for h in range(4):
                act.wait_ge(*read(f"om{h}", L))
                if h:
                    act.wait_ge(*full(f"ow{h - 1}", L))
                f(sq4[:, :, :], oR[:, 4 * h:4 * h + 4, :], Square).then_inc(sem["osq"], 1)
                act.wait_ge(*full(f"ow{h}", L))
                f(rn4[:, h, :], bank(f"ow{h}")[:, 0:SEQ], Ln, bias=eps_col, scale=1.0 / 512).then_inc(emptied(f"ow{h}"), 1)
                act.wait_ge(*read(f"ow{h}", L))
                f(rn4[:, h, :], rn4[:, h, :], Exp, scale=-0.5).then_inc(sem["ovar"], 1)
            for h in range(4):
                act.wait_ge(sem["ogate"], h + 1)
                f(gH[:, 4 * h:4 * h + 4, :], oR[:, 4 * h:4 * h + 4, :], Copy).then_inc(sem["og_h"], 1)
            with act.Fori(0, 4) as i:
                for s in range(2):
                    split_hi(act, M_O + O_OUT + i + 1, s)
            mlp2(1, M_O + O_UP, R_O + RO_UP, True)
            for b in range(4):
                act.wait_ge(sem["turned_back"], b + 1)
                f(outT[:, b // 2, (b % 2) * 512:(b % 2) * 512 + 512], lin[b][:, :], Copy).then_inc(sem["out_ready"], 1)

        @block.vector
        def _(dve):
            own = Own(dve, sem["dve_own"])
            v = nc.vector
            dve.sem_inc(sem["wlo"], 2)
            v.memset(rows[:, :, :, :], 0.0).then_inc(sem["cleared"], 1)
            for x in (ab, gcs, kdx):
                v.memset(x[:, 0:1, :], 0.0)
            v.memset(bias[:, :, 0:META], 0.0).then_inc(sem["cleared"], 1)
            dve.wait_ge(sem["h0"], DC + 2 * DEPTH + 1)
            v.tensor_scalar(rates[:, :, 4:8], rates[:, :, 4:8], -1.0, None, ALU.mult).then_inc(sem["cleared"], 1)
            dve.wait_ge(sem["cleared"], 3)
            for s in range(2):
                split_lo(dve, 0, s)

            def norm(l, which, gain):
                dve.wait_ge(sem["rstd"], at("rstd", l, which))
                for c in range(DC):
                    v.scalar_tensor_tensor(nT[:, c, :], hT[:, c, :], pc(gain + c), rs[:, :], ALU.mult, ALU.mult).then_inc(sem["n"], 1)
                for g in range(2):
                    dve.wait_ge(sem["nh"], at("nh", l, 2 * which - 1 + g))
                    gs = slice(4 * g, 4 * g + 4)
                    v.tensor_tensor(nL[:, gs, :], nT[:, gs, :], nH[:, gs, :].bitcast(F32), ALU.subtract).then_inc(sem["nl"], 1)

            def layer(l):
                own.base, own.n = l * PER["dve_own"], 0
                m0, r0 = l * M_LAYER, l * R_LAYER
                own.done(v.tensor_copy(parL[:, 0:2 * P].unsqueeze(1), par[:, ds(l, 1), :]))
                own.done(v.tensor_scalar(parL[:, K_NB:K_NB + 16].unsqueeze(1), par[:, ds(l, 1), K_BG:K_BG + 16], -1.0, None, ALU.mult))
                own.done(v.tensor_copy(parL[:, K_DT:K_DT + 8].unsqueeze(1), rates[:, ds(l, 1), :]))
                own.wait()
                norm(l, 1, K_NORM1)
                start = own.n
                with dve.Fori(0, 3) as i:
                    own.base, own.n = l * PER["dve_own"] + i * 12, start
                    for s in range(2):
                        split_lo(dve, m0 + i + 1, s)
                    for tap in range(4):
                        for c in range(4):
                            raw, acc = rawT[:, ds(4 * i + c, 1), :], cT[:, ds(4 * i + c, 1), :]
                            w = parL[:, ds(K_CONV + (3 - tap) * 12 + 4 * i + c, 1)]
                            if tap == 0:
                                dve.wait_ge(lin_read[c], r0 + i + 1)
                                own.done(v.tensor_scalar(acc, raw, w, None, ALU.mult))
                                continue
                            own.wait(own.n - 3 if tap < 3 else start + 9 + c)
                            ins = v.scalar_tensor_tensor(acc[:, :, tap:T], raw[:, :, 0:T - tap], w, acc[:, :, tap:T], ALU.mult, ALU.add)
                            if tap < 3:
                                own.done(ins)
                            else:
                                ins.then_inc(sem["conv"], 1)
                own.base, own.n = l * PER["dve_own"], start + 36
                with dve.Fori(3, 6) as i:
                    for s in range(2):
                        split_lo(dve, m0 + i + 1, s)
                dve.wait_ge(*read("ab", l))
                own.done(v.tensor_tensor(gx[:, :, :], ab[:, :, 0:4], bf(pc(K_DT, 4), 1, [P, 3, 4]), ALU.add))
                own.wait()
                v.scalar_tensor_tensor(gm[:, :, :], gx[:, :, :], -1.0, gx[:, :, :], ALU.mult, ALU.min).then_inc(sem["sp_in"], 1)
                own.done(v.tensor_scalar(iw[:, :, :], ab[:, :, 8:16], IDX_HEADS ** -0.5 * IDX_DIM ** -0.5, None, ALU.mult))
                dve.wait_ge(sem["sp_ln"], at("sp_ln", l, 1))
                own.done(v.scalar_tensor_tensor(gm[:, :, :], gx[:, :, :], 0.0, gl[:, :, :], ALU.max, ALU.add))
                own.wait()
                v.tensor_tensor(gg[:, :, :], gm[:, :, :], bf(pc(K_NA, 4), 1, [P, 3, 4]), ALU.mult).then_inc(sem["gt"], 1)
                own.done(v.tensor_scalar(bt[:, :, :], bt[:, :, :], 1.0, None, ALU.add))
                own.wait()
                own.done(v.reciprocal(beta[:, :, :], bt[:, :, :]))
                dve.wait_ge(sem["rn"], at("rn", l, 1))
                v.tensor_tensor(cT[:, 0:4, :], cT[:, 0:4, :], rnq[:, :, :], ALU.mult).then_inc(sem["qk_unit"], 1)
                dve.wait_ge(sem["rn"], at("rn", l, 2))
                v.tensor_tensor(cT[:, 4:8, :], cT[:, 4:8, :], rnk[:, :, :], ALU.mult).then_inc(sem["qk_unit"], 1)
                dve.wait_ge(sem["gt"], at("gt", l, 1))
                own.wait()
                for src, spread in ((gg, gtri), (beta, bdiag)):
                    for b in range(3):
                        n = TB[b][1]
                        mask = const("upto", n, n) if src is gg else ident[0:n, 0:n]
                        v.tensor_tensor(spread[b], bf(mask, 1, [n, 4, n]), bf(src[0:n, b, :], 2, [n, 4, n]), ALU.mult).then_inc(sem["gt"], 1)
                dve.wait_ge(sem["rn"], at("rn", l, 4))
                v.scalar_tensor_tensor(rawT[:, 16:20, :], rawT[:, 16:20, :], pc(K_QN), rnb[:, 0:4, :], ALU.mult, ALU.mult).then_inc(sem["att_unit"], 1)
                v.scalar_tensor_tensor(bkr[:, :], bkr[:, :], pc(K_KN), rnb[:, 4, :], ALU.mult, ALU.mult).then_inc(sem["att_unit"], 1)
                v.scalar_tensor_tensor(ikr[:, :], ikr[:, :], pc(K_IN), rni[:, :], ALU.mult, ALU.mult).then_inc(sem["att_unit"], 1)

                def gate_lo(i):
                    for s in range(2):
                        split_lo(dve, m0 + M_GATE + i + 1, s)

                gate_lo(0)
                dve.wait_ge(sem["eg"], at("eg", l, 1))
                own.done(v.tensor_scalar(egt[:, :, :], egt[:, :, :], -1.0, None, ALU.mult))
                dve.wait_ge(*read("gc", l))
                for b in range(3):
                    n = TB[b][1]
                    ps = bank(f"gb{b}")
                    dve.wait_ge(*full(f"gb{b}", l))
                    dve.wait_ge(sem["eg"], at("eg", l, 2 + b))
                    for h in range(4):
                        v.tensor_scalar(decay[b][:, h, :], ps[0:n, h * n:(h + 1) * n], gcs[0:n, b, h:h + 1], 0.0, ALU.subtract, ALU.min)
                    v.tensor_tensor(kdx[0:n, b, :], ps[0:n, n - 1:4 * n:n], gcs[0:n, b, :], ALU.subtract).then_inc(emptied(f"gb{b}"), 1)
                    dve.wait_ge(sem["dec"], at("dec", l, b + 1))
                    own.done(v.tensor_tensor(decay[b], decay[b], bf(const("upto", n, n), 1, [n, 4, n]), ALU.mult))
                    own.wait()
                    dve.wait_ge(*full(f"bb{b}", l))
                    v.tensor_tensor(MT[b], bank(f"bb{b}")[0:n, 0:4 * n].rearrange("p (h c) -> p h c", h=4), decay[b], ALU.mult).then_inc(emptied(f"bb{b}"), 1)
                for b in range(3):
                    n = TB[b][1]
                    dve.wait_ge(*full(f"kk{b}", l))
                    dve.wait_ge(*read(f"bb{b}", l))
                    v.tensor_tensor(MT[b], bank(f"kk{b}")[0:n, 0:4 * n].rearrange("p (h c) -> p h c", h=4), MT[b], ALU.mult).then_inc(emptied(f"kk{b}"), 1)
                    dve.wait_ge(*full(f"qk{b}", l))
                    v.tensor_tensor(QD[b], bank(f"qk{b}")[0:n, 0:4 * n].rearrange("p (h c) -> p h c", h=4), decay[b], ALU.mult).then_inc(emptied(f"qk{b}"), 1)
                for b in range(3):
                    own.done(v.tensor_copy(sdec[:, b, :], eg[:, :, TB[b][0] + TB[b][1] - 1]))
                v.tensor_tensor(cT[:, 0:4, :], cT[:, 0:4, :], eg[:, :, :], ALU.mult).then_inc(sem["qe"], 1)
                dve.wait_ge(sem["kdx"], at("kdx", l, 1))
                for b in range(3):
                    n = TB[b][1]
                    dve.wait_ge(*full(f"kt{b}", l))
                    v.tensor_tensor(kd[0:n, b], bank(f"kt{b}")[0:n, :].rearrange("p (h d) -> p h d", h=4), bf(kdx[0:n, b, :], 2, [n, 4, P]), ALU.mult).then_inc(emptied(f"kt{b}"), 1)
                gate_lo(1)
                for n, (names, kind, x) in enumerate((
                    ([f"rq{h}" for h in range(4)], "a", rawT[:, 16:20, :]), ([f"ri{c}" for c in range(4)], "i", rawT[:, 20:24, :]),
                    (["rk"], "a", bkr[:, :].unsqueeze(1)), (["rik"], "i", ikr[:, :].unsqueeze(1)),
                )):
                    if n:
                        dve.wait_ge(sem["rope"], at("rope", l, n))
                    for c, name in enumerate(names):
                        dve.wait_ge(*full(name, l))
                        v.tensor_tensor(tmp4[:, c, :], bank(name)[:, 0:T], const("sin_" + kind, T), ALU.mult).then_inc(emptied(name), 1)
                    own.done(v.tensor_tensor(x, x, bf(const("cos_" + kind, T), 1, [P, len(names), T]), ALU.mult))
                    own.wait()
                    dve.wait_ge(*read(names[-1], l))
                    v.tensor_tensor(x, x, tmp4[:, 0:len(names), :], ALU.add).then_inc(sem["rope"], 1)
                gate_lo(2)
                for j in range(2):
                    for e in range(4):
                        dve.wait_ge(*read(f"ix{j}{e}", l))
                        for n in range(2):
                            h = 4 * (e // 2) + e % 2 + 2 * n
                            r, w = rl[:, e % 2, n * SEQ:(n + 1) * SEQ], iw[:, j + 1, h:h + 1]
                            if e + n == 0:
                                ins = v.tensor_scalar(score[:, j, :], r, w, None, ALU.mult)
                            else:
                                if n == 0:
                                    dve.wait_ge(sem["score"], at("score", l, 4 * j + e))
                                else:
                                    own.wait()
                                ins = v.scalar_tensor_tensor(score[:, j, :], r, w, score[:, j, :], ALU.mult, ALU.add)
                            if n == 0:
                                own.done(ins)
                            else:
                                ins.then_inc(sem["score"], 1)
                    dve.wait_ge(sem["score"], at("score", l, 4 * j + 4))
                    own.done(v.tensor_tensor(score[:, j, :], score[:, j, :], c1[:, consts_at1["barred"] + j * SEQ:consts_at1["barred"] + (j + 1) * SEQ], ALU.add))
                for b in range(3):
                    n = TB[b][1]
                    for m in (X, A):
                        own.done(v.tensor_copy(m[b], bf(ident[0:n, 0:n], 1, [n, 4, n])))
                with dve.Fori(0, LEVELS) as it:
                    for b in range(3):
                        n = TB[b][1]
                        level = c1[0:n, ds(consts_at1["level0"] + it * P, n)]
                        v.tensor_tensor(ML[b], MT[b], bf(level, 1, [n, 4, n]), ALU.mult).then_inc(sem["ml"], 1)
                    dve.wait_ge(*full("XA0", l, it))
                    v.tensor_tensor(X[0], X[0], bank("XA0")[0:META, 0:4 * META].rearrange("p (h c) -> p h c", h=4), ALU.subtract)
                    v.tensor_tensor(A[0], A[0], bank("XA0")[0:META, 4 * META:8 * META].rearrange("p (h c) -> p h c", h=4), ALU.subtract).then_inc(emptied("XA0"), 1)
                    for b in (1, 2):
                        for name, m in ((f"X{b}", X), (f"A{b}", A)):
                            if name[0] == "X":
                                dve.wait_ge(*full(f"A{b}", l, it))
                            v.tensor_tensor(m[b], m[b], bank(name)[:, :].rearrange("p (h c) -> p h c", h=4), ALU.subtract).then_inc(emptied(name), 1)
                dve.wait_ge(*read("A2", l, LEVELS - 1))
                for b in range(3):
                    n = TB[b][1]
                    v.tensor_tensor(A[b], A[b], bf(beta[0:n, b, :], 2, [n, 4, n]), ALU.mult).then_inc(sem["ab_ready"], 1)
                gate_lo(3)
                for turn in range(TOPK // 8):
                    for j in range(2):
                        src = score if turn == 0 else work
                        own.wait(own.n - 1 if turn else None)
                        stand(dve, "dve_stood")
                        own.done(v.max(m8[:, j, :], src[:, j, :]))
                    for j in range(2):
                        src = score if turn == 0 else work
                        own.wait(own.n - 1)
                        stand(dve, "dve_stood")
                        own.done(v.match_replace(work[:, j, :], m8[:, j, :], src[:, j, :], TAKEN))
                own.wait()
                own.done(v.tensor_scalar(bias[:, :, META:T], work[:, :, :], 0.5 * (INVALID + TAKEN), -BIG, ALU.is_gt, ALU.mult))
                own.wait()
                for b in range(3):
                    if b:
                        ps = bank(f"kS{b}")
                        dve.wait_ge(*full(f"kS{b}", l))
                        for h in range(4):
                            ins = v.scalar_tensor_tensor(R[:, h, :], ps[:, h * P:(h + 1) * P], egt[:, b, h:h + 1], vt[:, b, h, :], ALU.mult, ALU.add)
                        ins.then_inc(emptied(f"kS{b}"), 1)
                    if b < 2:
                        ps = bank(f"dS{b}")
                        dve.wait_ge(*full(f"dS{b}", l))
                        if b == 0:
                            v.tensor_copy(S[:, :, :], ps[:, :].rearrange("p (h d) -> p h d", h=4)).then_inc(emptied("dS0"), 1)
                        else:
                            for h in range(4):
                                ins = v.scalar_tensor_tensor(S[:, h, :], S[:, h, :], sdec[:, b, h:h + 1], ps[:, h * P:(h + 1) * P], ALU.mult, ALU.add)
                            ins.then_inc(emptied(f"dS{b}"), 1)
                dve.wait_ge(*full("s0", l))
                own.done(v.tensor_reduce(mx[0:META, :], bank("s0")[0:META, 0:4 * META].rearrange("p (h k) -> p h k", h=4), AX, ALU.max))
                own.wait()
                v.tensor_scalar(nmx[0:META, :], mx[0:META, :], -(P ** -0.5), None, ALU.mult).then_inc(sem["nmx"], 1)
                dve.wait_ge(*read("s0", l))
                own.done(v.reciprocal(rsm[0:META, :], sm[0:META, :]))
                own.wait()
                v.tensor_tensor(P0[:, :, :], P0[:, :, :], bf(rsm[0:META, :], 2, [META, 4, META]), ALU.mult).then_inc(sem["pn"], 1)

                def out_lo(j):
                    dve.wait_ge(sem["ob_h"], at("ob_h", l, 1 + j))
                    v.tensor_tensor(oL[:, 4:8, tok(j)], bank(f"pv{j}")[:, 0:4 * TB[j][1]].rearrange("p (h c) -> p h c", h=4),
                                    oH[:, 4:8, tok(j)].bitcast(F32), ALU.subtract).then_inc(emptied(f"pv{j}"), 1)

                out_lo(0)
                for j in (1, 2):
                    for h in range(4):
                        name = f"s{'abcd'[h]}{j}"
                        dve.wait_ge(*full(name, l))
                        v.tensor_tensor(Pm[:, h, :], bank(name)[:, 0:T], bias[:, j - 1, :], ALU.add).then_inc(emptied(name), 1)
                    dve.wait_ge(*read(f"sd{j}", l))
                    own.done(v.tensor_reduce(mx[:, :], Pm[:, :, :], AX, ALU.max))
                    own.wait()
                    v.tensor_scalar(nmx[:, :], mx[:, :], -(P ** -0.5), None, ALU.mult).then_inc(sem["nmx"], 1)
                    dve.wait_ge(sem["soft"], at("soft", l, j))
                    own.done(v.reciprocal(rsm[:, :], sm[:, :]))
                    own.wait()
                    v.tensor_tensor(Pm[:, :, :], Pm[:, :, :], bf(rsm[:, :], 2, [P, 4, T]), ALU.mult).then_inc(sem["pn"], 1)
                    out_lo(j)
                dve.wait_ge(lin_read[3], r0 + R_BRANCH)
                own.done(v.tensor_scalar(rawT[:, 0:16, :], rawT[:, 0:16, :], 1.0, None, ALU.add))
                own.wait()
                v.reciprocal(rawT[:, 0:16, :], rawT[:, 0:16, :]).then_inc(sem["gates"], 1)
                dve.wait_ge(sem["rno"], at("rno", l, 1))
                own.done(v.scalar_tensor_tensor(oA[:, :, :], oA[:, :, :], pc(K_ANORM), rno[:, :, :], ALU.mult, ALU.mult))
                own.wait()
                v.tensor_tensor(oA[:, :, :], oA[:, :, :], zT[:, :, :], ALU.mult).then_inc(sem["oa"], 1)
                dve.wait_ge(sem["oa_h"], at("oa_h", l, 1))
                v.tensor_tensor(oL[:, 0:4, :], oA[:, :, :], oH[:, 0:4, :].bitcast(F32), ALU.subtract).then_inc(sem["oa_l"], 1)
                dve.wait_ge(sem["gates"], at("gates", l, 1))
                stand(dve, "dve_stood")
                with dve.Fori(0, 2) as i:
                    for s in range(2):
                        split_lo(dve, m0 + M_BRANCH + i + 1, s)
                        r = r0 + R_BRANCH + 2 * i + s
                        dve.wait_ge(sem["panel_done"], 2 * (m0 + M_BRANCH + i) + s + 3)
                        for c in range(2):
                            q = 4 * i + 2 * s + c
                            v.tensor_tensor(yT[:, ds(q, 1), :], lin[c][:, 0:T].unsqueeze(1), rawT[:, ds(q, 1), :], ALU.mult).then_inc(lin_read[c], 1)
                            v.tensor_tensor(ytmp[:, c, :].unsqueeze(1), lin[2 + c][:, 0:T].unsqueeze(1), rawT[:, ds(8 + q, 1), :], ALU.mult).then_inc(lin_read[2 + c], 1)
                        for c in range(2):
                            q = 4 * i + 2 * s + c
                            dve.wait_ge(lin_read[2 + c], r + 1)
                            v.tensor_tensor(yT[:, ds(q, 1), :], yT[:, ds(q, 1), :], ytmp[:, c, :].unsqueeze(1), ALU.add).then_inc(sem["y"], 1)
                        two = ds(4 * i + 2 * s, 2)
                        dve.wait_ge(sem["yh"], at("yh", l, 2 * i + s + 1))
                        v.tensor_tensor(nL[:, two, :], yT[:, two, :], nH[:, two, :].bitcast(F32), ALU.subtract).then_inc(sem["yl"], 1)
                with dve.Fori(0, 2) as i:
                    for s in range(2):
                        split_lo(dve, m0 + M_OUT + i + 1, s)
                        dve.wait_ge(sem["panel_done"], 2 * (m0 + M_OUT + i) + s + 3)
                        for c in range(2):
                            x = hT[:, ds(4 * i + 2 * s + c, 1), :]
                            v.tensor_tensor(x, x, lin[2 * s + c][:, 0:T].unsqueeze(1), ALU.add).then_inc(lin_read[2 * s + c], 1)
                norm(l, 2, K_NORM2)
                with dve.Fori(0, 11) as i:
                    m, r = m0 + M_UP + i, r0 + R_UP + i
                    own.base = l * PER["dve_own"] + i * 2
                    n0 = own.n
                    split_lo(dve, m + 1, 0)
                    for c in range(2):
                        dve.wait_ge(sem["tap"], at("tap", l, 2 * i + c + 1))
                        own.done(v.scalar_tensor_tensor(u[:, c, 1:T], lin[c][:, 0:T - 1], parL[:, ds(K_FCONV + FC + 2 * i + c, 1)], u[:, c, 1:T], ALU.mult, ALU.add))
                    for c in range(2):
                        own.wait(n0 + c + 1)
                        v.scalar_tensor_tensor(u[:, c, 2:T], lin[c][:, 0:T - 2], parL[:, ds(K_FCONV + 2 * i + c, 1)], u[:, c, 2:T], ALU.mult, ALU.add).then_inc(lin_read[c], 1)
                    split_lo(dve, m + 1, 1)
                    dve.wait_ge(sem["panel_done"], 2 * m + 4)
                    for c in range(2):
                        dve.wait_ge(sem["gate_silu"], at("gate_silu", l, 2 * i + c + 1))
                        v.tensor_tensor(av[:, c, :], lin[2 + c][:, 0:T], sg[:, c, :], ALU.mult).then_inc(lin_read[2 + c], 1)
                    for c in range(2):
                        dve.wait_ge(sem["ah"], at("ah", l, 2 * i + c + 1))
                        q = ds(2 * i + c, 1)
                        v.tensor_tensor(aL[:, q, :], av[:, c, :].unsqueeze(1), aH[:, q, :].bitcast(F32), ALU.subtract).then_inc(sem["al"], 1)
                own.base, own.n = l * PER["dve_own"], n0 + 22
                with dve.Fori(0, 2) as i:
                    for p in range(6):
                        m = m0 + M_DOWN + 3 * i + p // 2
                        split_lo(dve, m + 1, p % 2)
                        if p % 3 == 2:
                            dve.wait_ge(sem["panel_done"], 2 * m + p % 2 + 3)
                            for c in range(2):
                                b = 2 * (p // 3) + c
                                x = hT[:, ds(4 * i + b, 1), :]
                                v.tensor_tensor(x, x, lin[b][:, 0:T].unsqueeze(1), ALU.add).then_inc(lin_read[b], 1)
                assert own.n == PER["dve_own"], own.n

            with dve.Fori(0, DEPTH) as l:
                layer(l)

            L = DEPTH
            own.base, own.n = L * PER["dve_own"], 0
            h2 = hT[:, :, META:T]

            def norm2(which, gains):
                dve.wait_ge(sem["rstd2"], which)
                for c in range(DC):
                    v.scalar_tensor_tensor(nT2[:, c, :], h2[:, c, :], gains(c), rs[:, 0:SEQ], ALU.mult, ALU.mult).then_inc(sem["n2"], 1)
                for g in range(2):
                    dve.wait_ge(sem["nh2"], 2 * which - 1 + g)
                    gs = slice(4 * g, 4 * g + 4)
                    v.tensor_tensor(nL[:, gs, 0:SEQ], nT2[:, gs, :], nH[:, gs, 0:SEQ].bitcast(F32), ALU.subtract).then_inc(sem["nl2"], 1)

            def los(m, pairs):
                with dve.Fori(0, pairs) as i:
                    for s in range(2):
                        split_lo(dve, m + i + 1, s)

            def add_h(chunk, b):
                x = hT[:, ds(chunk, 1), META:T]
                v.tensor_tensor(x, x, lin[b][:, 0:SEQ].unsqueeze(1), ALU.add).then_inc(lin_read[b], 1)

            def mlp2(j, m, r, last):
                norm2(2 * j + 2, lambda c: p2(j, (KE_FN, KO_FN)[j] + c))
                n0 = own.n
                with dve.Fori(0, 11) as i:
                    own.base = L * PER["dve_own"] + i * 4
                    own.n = n0
                    for s in range(2):
                        split_lo(dve, m + i + 1, s)
                        for c in range(2):
                            q = 2 * s + c
                            w = par[:, DEPTH + j, ds(P + 2 * FC + s * FC + 2 * i + c, 1)]
                            dve.wait_ge(sem["tap2"], j * 2 * FC + 4 * i + q + 1)
                            own.done(v.scalar_tensor_tensor(u2[:, q, 1:SEQ], lin[q][:, 0:SEQ - 1], w, u2[:, q, 1:SEQ], ALU.mult, ALU.add))
                        for c in range(2):
                            q = 2 * s + c
                            w = par[:, DEPTH + j, ds(P + s * FC + 2 * i + c, 1)]
                            own.wait(n0 + q + 1)
                            v.scalar_tensor_tensor(u2[:, q, 2:SEQ], lin[q][:, 0:SEQ - 2], w, u2[:, q, 2:SEQ], ALU.mult, ALU.add).then_inc(lin_read[q], 1)
                    for c in range(2):
                        dve.wait_ge(sem["silu2"], j * FC + 2 * i + c + 1)
                        dve.wait_ge(lin_read[2 + c], r + i + 1)
                        v.tensor_tensor(av2[:, c, :], u2[:, 2 + c, :], sg2[:, c, :], ALU.mult).then_inc(sem["conv2"], 1)
                    for c in range(2):
                        dve.wait_ge(sem["ah2"], j * FC + 2 * i + c + 1)
                        q = ds(2 * i + c, 1)
                        v.tensor_tensor(aL2[:, q, :], av2[:, c, :].unsqueeze(1), aH2[:, q, :].bitcast(F32), ALU.subtract).then_inc(sem["al2"], 1)
                own.base, own.n = L * PER["dve_own"], n0 + 44

                def down(i, last):
                    for p in range(6):
                        mp = m + 11 + 3 * i + p // 2
                        if not (last and p >= 4):
                            split_lo(dve, mp + 1, p % 2)
                        if p % 3 == 2:
                            dve.wait_ge(sem["panel_done"], 2 * mp + p % 2 + 3)
                            for c in range(2):
                                add_h(4 * i + 2 * (p // 3) + c, 2 * (p // 3) + c)

                if last:
                    for i in range(2):
                        down(i, i == 1)
                else:
                    with dve.Fori(0, 2) as i:
                        down(i, False)

            norm2(1, lambda c: p2(0, c))
            los(M_E, 5)
            for s in range(2):
                split_lo(dve, M_E + 6, s)
                dve.wait_ge(sem["panel_done"], 2 * (M_E + 5) + s + 3)
                for c in range(2):
                    b = 2 * s + c
                    dve.wait_ge(lin_read[b], R_E + 5)
                    v.tensor_tensor(ght[:, b, :], lin[b][:, 0:SEQ], gct[:, b, :], ALU.mult).then_inc(lin_read[b], 1)
            dve.wait_ge(sem["ern"], 1)
            v.scalar_tensor_tensor(raw8[:, 0:4, :], raw8[:, 0:4, :], p2(0, KE_QG), rne[:, 0:4, :], ALU.mult, ALU.mult).then_inc(sem["eunit"], 1)
            v.scalar_tensor_tensor(raw8[:, 4:8, :], raw8[:, 4:8, :], p2(0, KE_KG), rne[:, 4:8, :], ALU.mult, ALU.mult).then_inc(sem["eunit"], 1)
            for tap in range(3):
                for c in range(4):
                    w = p2(0, KE_SC + (2 - tap) * 4 + c)
                    if tap == 0:
                        dve.wait_ge(lin_read[c], R_E + 6)
                        own.done(v.tensor_scalar(cvt[:, c, :], ght[:, c, :], w, None, ALU.mult))
                    else:
                        own.wait(own.n - 3)
                        own.done(v.scalar_tensor_tensor(cvt[:, c, tap:SEQ], ght[:, c, 0:SEQ - tap], w, cvt[:, c, tap:SEQ], ALU.mult, ALU.add))
            own.wait()
            v.tensor_tensor(cvt[:, :, :], cvt[:, :, :], gbt[:, :, :], ALU.mult).then_inc(sem["eb"], 1)
            dve.wait_ge(sem["c2_in"], 16)
            for j in range(2):
                keys = (j + 1) * P
                unseen = c2[:, consts_at2["unseen"] + j * SEQ:consts_at2["unseen"] + j * SEQ + keys]
                count = c2[:, consts_at2["count"] + j * SEQ:consts_at2["count"] + j * SEQ + keys]
                for e, heads in enumerate([(0, 2, 4, 6), (1, 3, 5, 7)] if j == 0 else [(0, 2), (1, 3), (4, 6), (5, 7)]):
                    name, n = f"e{j}{e}", len(heads)
                    dve.wait_ge(*full(name, L))
                    v.tensor_tensor(Pe[:, heads[0]:heads[-1] + 1:2, 0:keys], bank(name)[:, 0:n * keys].rearrange("p (h k) -> p h k", h=n),
                                    bf(unseen, 1, [P, n, keys]), ALU.add).then_inc(emptied(name), 1)
                dve.wait_ge(*read(name, L))
                own.done(v.tensor_reduce(mx8[:, :], Pe[:, :, 0:keys], AX, ALU.max))
                own.wait()
                v.tensor_scalar(nmx8[:, :], mx8[:, :], -0.125, None, ALU.mult).then_inc(sem["enmx"], 1)
                dve.wait_ge(sem["esoft"], 1 + j)
                own.done(v.tensor_tensor(Pe[:, :, 0:keys], Pe[:, :, 0:keys], bf(count, 1, [P, 8, keys]), ALU.mult))
                own.wait()
                own.done(v.tensor_reduce(sm8[:, :], Pe[:, :, 0:keys], AX, ALU.add))
                own.wait()
                own.done(v.reciprocal(rsm8[:, :], sm8[:, :]))
                own.wait()
                v.tensor_tensor(Pe[:, :, 0:keys], Pe[:, :, 0:keys], bf(rsm8[:, :], 2, [P, 8, keys]), ALU.mult).then_inc(sem["epn"], 1)
                dve.wait_ge(sem["eob_h"], 1 + j)
                ts = slice(j * P, j * P + P)
                v.tensor_tensor(eL[:, 0:4, ts], bank(f"ev{j}")[:, :].rearrange("p (c t) -> p c t", c=4), eH[:, 0:4, ts].bitcast(F32),
                                ALU.subtract).then_inc(emptied(f"ev{j}"), 1)
            dve.wait_ge(sem["eb_h"], 1)
            v.tensor_tensor(eL[:, 4:8, :], cvt[:, :, :], eH[:, 4:8, :].bitcast(F32), ALU.subtract).then_inc(sem["eb_l"], 1)
            with dve.Fori(0, 2) as i:
                for s in range(2):
                    split_lo(dve, M_E + E_OUT + i + 1, s)
                    dve.wait_ge(sem["panel_done"], 2 * (M_E + E_OUT + i) + s + 3)
                    for c in range(2):
                        add_h(4 * i + 2 * s + c, 2 * s + c)
            mlp2(0, M_E + E_UP, R_E + E_UP, False)

            norm2(3, lambda c: p2(1, c))

            def rotate(n, rnd):
                x = [qk2[:, n, :, d, :] for d in range(2)]
                cos, sin = (bf(table2(name, SEQ), 1, [P, 4, SEQ]) for name in ("cos_r", "sin_r"))
                for b in range(4):
                    dve.wait_ge(lin_read[b], rnd)
                if n:
                    dve.wait_ge(sem["orot"], 2)
                for d in range(2):
                    own.done(v.tensor_tensor(tsin[:, d], x[d], sin, ALU.mult))
                own.wait()
                for d in range(2):
                    own.done(v.tensor_tensor(x[d], x[d], cos, ALU.mult))
                own.wait()
                v.tensor_tensor(x[0], x[0], tsin[:, 1], ALU.subtract).then_inc(sem["orot"], 1)
                v.tensor_tensor(x[1], x[1], tsin[:, 0], ALU.add).then_inc(sem["orot"], 1)

            los(M_O, 2)
            los(M_O + O_K, 1)
            rotate(0, R_O + O_K)
            los(M_O + O_K + 1, 2)
            rotate(1, R_O + O_V)
            los(M_O + O_V + 1, 3)
            for h in range(4):
                dve.wait_ge(*full(f"os{h}", L))
                v.tensor_tensor(sc[:, h, :], bank(f"os{h}")[:, 0:384], table2(f"decay{h}", 384), ALU.mult).then_inc(emptied(f"os{h}"), 1)
            los(M_O + O_G, 4)
            for h in range(4):
                x = oR[:, 4 * h:4 * h + 4, :]
                dve.wait_ge(*full(f"om{h}", L))
                v.scalar_tensor_tensor(x, bf(bank(f"om{h}")[:, 0:SEQ], 1, [P, 4, SEQ]), -1.0 / 512, x, ALU.mult, ALU.add).then_inc(emptied(f"om{h}"), 1)
            for h in range(4):
                dve.wait_ge(sem["ovar"], h + 1)
                for e in range(4):
                    c = 4 * h + e
                    own.done(v.scalar_tensor_tensor(oR[:, c, :], oR[:, c, :], p2(1, KO_GN + c), rn4[:, h, :], ALU.mult, ALU.mult))
                own.wait()
                cs = slice(4 * h, 4 * h + 4)
                v.tensor_tensor(oR[:, cs, :], oR[:, cs, :], sgT[:, cs, :], ALU.mult).then_inc(sem["ogate"], 1)
            for h in range(4):
                cs = slice(4 * h, 4 * h + 4)
                dve.wait_ge(sem["og_h"], h + 1)
                v.tensor_tensor(gL[:, cs, :], oR[:, cs, :], gH[:, cs, :].bitcast(F32), ALU.subtract).then_inc(sem["og_l"], 1)
            with dve.Fori(0, 2) as i:
                for q in range(2):
                    m = M_O + O_OUT + 2 * i + q
                    for s in range(2):
                        split_lo(dve, m + 1, s)
                    dve.wait_ge(sem["panel_done"], 2 * m + 4)
                    for c in range(2):
                        add_h(4 * i + 2 * q + c, 2 * q + c)
            mlp2(1, M_O + O_UP, R_O + RO_UP, True)


def kernel(**inputs):
    import numpy as _np
    import concourse.bacc as _bacc
    from concourse import mybir as _mybir
    from concourse.bass_utils import run_bass_kernel_spmd as _run

    nc = _bacc.Bacc("TRN2", target_bir_lowering=False, num_devices=1)
    arrays, a = {}, {}
    tables = constants()
    given = {name: _np.ascontiguousarray(inputs[name]) for name in INPUTS}
    for name, x in (*given.items(), *tables["arrays"].items()):
        arrays[f"in_{name}"] = x
        a[name] = nc.dram_tensor(f"in_{name}", x.shape, _mybir.dt.from_np(x.dtype), kind="ExternalInput").ap()
    out = nc.dram_tensor("out", (1, SEQ, D), _mybir.dt.float32, kind="ExternalOutput").ap()
    build(nc, a, tables["places"], out.rearrange("b t d -> (b t) d"))
    r = _run(nc, [arrays], core_ids=[0])
    return r.results[0]["out"]
```

```python
import math
from contextlib import ExitStack

import numpy as np

import concourse.bass as bass
from concourse import mybir

F32 = mybir.dt.float32
F32R = mybir.dt.float32r
ACT = mybir.ActivationFunctionType
ALU = mybir.AluOpType
AX = mybir.AxisListType.X
ds = bass.ds

P = 128
D = 1024
DC = D // P
DEPTH = 2
SEQ = 256
META = 16
T = META + SEQ
EPS = 1e-6
HEADS = 4
IDX_HEADS, IDX_DIM, TOPK = 8, 64, 64
FF = 2816
FC = FF // P
CHUNK = 64
INPUTS = (
    "x", "meta_tokens", "norm_mix", "w_in", "conv_a", "a_log", "dt_bias", "a_out_norm", "q_norm", "k_norm", "kidx_norm",
    "w_branch_a", "w_branch_b", "w_gate", "b_gate", "w_out", "norm_ffn", "w_up", "conv_ffn", "w_down", "even_norm_2",
    "even_w_in_2", "even_q_gain_2", "even_k_gain_2", "even_sconv_w_2", "even_w_out_2", "odd_norm_2", "ret_wq_2", "ret_wk_2",
    "ret_wv_2", "ret_wg_2", "ret_gn_gain_2", "ret_wo_2", "ffn_norm_2", "ffn_w_up_2", "ffn_conv_w_2", "ffn_w_down_2",
)
TB = [(0, META), (META, P), (META + P, P)]
LEVELS = 7
PANEL = 256
C_AB, C_BQ, C_BK, C_IQ, C_IK = 2048, 2056, 2568, 2824, 3336
IN_COLS = 3408
S_IK, S_BK, S_BV, S_AB, S_ALL = 0, 128, 256, 384, 400

M_IN, M_GATE, M_BRANCH, M_OUT, M_UP, M_DOWN, M_LAYER = 0, 6, 10, 12, 14, 25, 31
R_IN, R_GATE, R_BRANCH, R_OUT, R_UP, R_DOWN, R_LAYER = 0, 6, 10, 12, 14, 25, 27
M_E, R_E = DEPTH * M_LAYER, DEPTH * R_LAYER
E_OUT, E_UP, E_DOWN, M_EVEN, R_EVEN = 6, 8, 19, 25, 21
M_O, R_O = M_E + M_EVEN, R_E + R_EVEN
O_K, O_V, O_G, O_OUT, O_UP, O_DOWN = 2, 4, 8, 12, 16, 27
RO_OUT, RO_UP, RO_DOWN, M_ODD, R_ODD = 12, 14, 25, 33, 27
M_ALL, R_ALL = M_O + M_ODD, R_O + R_ODD
DOWN_K = [(0, 8), (8, 8), (16, FC - 16)]

BIG = 1e30
INVALID = -3.0e38
TAKEN = -3.4e38
GATE_LEAST = -40.0


def constants():
    f = np.float32
    p = np.arange(P)
    parts, at = [], {}

    def put(name, a):
        at[name] = sum(x.shape[1] for x in parts)
        parts.append(np.ascontiguousarray(a, dtype=f).reshape(P, -1))

    put("ident", np.eye(P))
    put("ones", np.ones((P, P)))
    col = np.zeros((P, 4))
    col[:, 0] = EPS
    col[:, 1] = math.log(P ** -0.5)
    col[:, 2] = 1.0
    put("cols", col)
    put("half", (p[:, None] // 64 == p[None, :] // 64))

    def turn(dim):
        r = np.zeros((P, P))
        for i in range(P):
            if i % dim < dim // 2:
                r[i + dim // 2, i] = -1.0
            else:
                r[i - dim // 2, i] = 1.0
        return r

    put("turn_a", turn(P))
    put("turn_i", turn(IDX_DIM))

    def angles(dim, n_tok):
        inv = (1.0 / (f(10000.0) ** (np.arange(0, dim, 2, dtype=f) / f(dim)))).astype(f)
        return (np.arange(n_tok, dtype=f)[:, None] * inv[None, :]).astype(f)

    for name, dim in (("a", P), ("i", IDX_DIM)):
        ang = angles(dim, T)
        rows = p % (dim // 2)
        put("cos_" + name, np.cos(ang).T[rows])
        put("sin_" + name, np.sin(ang).T[rows])
    for l in range(LEVELS):
        s, c = p[:, None], p[None, :]
        put(f"level{l}", (s >> (l + 1) == c >> (l + 1)) & ((c >> l) % 2 == 1) & ((s >> l) % 2 == 0))
    put("upto", p[:, None] <= p[None, :])
    q = np.arange(SEQ).reshape(2, P).T
    limit = (q // CHUNK + 1) * CHUNK
    put("barred", np.where(np.arange(SEQ)[None, None, :] < limit[:, :, None], 0.0, INVALID))
    first, first_at = np.concatenate(parts, 1), dict(at)
    parts.clear()
    at.clear()
    t, s = np.arange(SEQ)[:, None], np.arange(SEQ)[None, :]
    back = t - s
    count = sum(((back >= 0) & (back % d == 0) & (back // d <= w // d)).astype(f) for w, d in ((128, 1), (512, 4), (2048, 16)))
    put("count", count.reshape(2, P, SEQ).transpose(1, 0, 2))
    put("unseen", np.where(count > 0, 0.0, -BIG).reshape(2, P, SEQ).transpose(1, 0, 2))
    half = P
    inv = (f(10000.0) ** (-np.arange(half, dtype=f) / f(half))).astype(f)
    ang = (np.arange(SEQ, dtype=f)[:, None] * inv[None, :]).astype(f)
    put("cos_r", np.cos(ang).T)
    put("sin_r", np.sin(ang).T)
    for h in range(4):
        log_g = np.log1p(-(2.0 ** (-5.0 - h)))
        dec = np.where(back >= 0, np.exp(log_g * np.maximum(back, 0)), 0.0) * 256 ** -0.5
        dec = dec.T.reshape(2, P, SEQ)
        put(f"decay{h}", np.concatenate([dec[0], dec[1][:, P:]], 1))
    second = np.concatenate(parts, 1)
    return {"arrays": {"c1": first, "c2": second}, "places": (first_at, at, first.shape[1], second.shape[1])}


def plan_aux(jobs):
    place, used, q = {}, [0] * 4, 0
    for job in jobs:
        n, names = job[1:] if isinstance(job, tuple) else (1, [job])
        step = len(names) // 4
        for name in names:
            used[q % 4] += 1
            place[name] = (q % 4, used[q % 4], step)
            q += 1
        for b in range(4):
            used[b] += (n - 1) * step
    return place, used


class Own:

    def __init__(self, eng, sem):
        self.eng, self.sem, self.base, self.n = eng, sem, 0, 0

    def done(self, ins):
        ins.then_inc(self.sem, 1)
        self.n += 1
        return self.n

    def wait(self, n=None):
        self.eng.wait_ge(self.sem, self.base + (self.n if n is None else n))


JOBS = (
    ["ms1", "ik", "bk", "tk"]
    + [f"ssq{h}" for h in range(4)] + [f"ssk{h}" for h in range(4)] + [f"sbq{h}" for h in range(4)] + ["sbk", "sik"]
    + ["gc"] + [x for b in range(3) for x in (f"gb{b}", f"bb{b}")]
    + [x for b in range(3) for x in (f"kk{b}", f"qk{b}")] + [x for b in range(3) for x in (f"kt{b}", f"vt{b}")]
    + [f"rq{h}" for h in range(4)] + [f"ri{c}" for c in range(4)] + ["rk", "rik"]
    + [f"ix{j}{e}" for j in range(2) for e in range(4)]
    + [("loop", LEVELS, ["Y0", "Y1", "Y2", "XA0", "X1", "A1", "X2", "A2"])]
    + ["vn0", "s0"] + [f"s{h}1" for h in "abcd"] + ["o0", "dS0", "pt0", "kS1", "pv0"] + [f"pt{b}_1" for b in range(3)] + ["vn1"]
    + [f"s{h}2" for h in "abcd"] + ["o1", "dS1", "pv1", "kS2"] + [f"pt{b}_2" for b in range(3)] + ["vn2", "pv2", "o2"]
    + [f"so{h}" for h in range(4)] + [("loop", 2, [f"br{b}" for b in range(4)])] + ["ms2"]
)
PLACE, AUX_PER = plan_aux(JOBS)
JOBS2 = (
    ["ems"] + [f"eq{c}" for c in range(4)] + ["e00", "e01"] + [f"e1{e}" for e in range(4)] + [f"et0{g}" for g in range(2)] + ["ev0"]
    + [f"et1{g}{b}" for g in range(2) for b in range(2)] + ["ev1", "emf", "oms"]
    + [f"os{h}" for h in range(4)] + [f"oo{h}{e}" for h in range(4) for e in range(2)] + [f"om{h}" for h in range(4)]
    + [f"ow{h}" for h in range(4)] + ["omf"]
)
PLACE.update(plan_aux(JOBS2)[0])

PER = {
    "panel_in": 16 * M_LAYER, "whi": 4 * M_LAYER, "wlo": 4 * M_LAYER, "whi_used": 2 * M_LAYER, "panel_done": 2 * M_LAYER,
    "lin_read": R_LAYER, "small_in": 5 * 16,
    "sq": DC, "rstd": 2, "n": 2 * DC, "nh": DC, "nl": DC,
    "conv": 12, "silu": 3, "sq_heads": 2, "sq_att": 1, "rn": 4, "qk_unit": 2, "att_unit": 3,
    "sp_in": 1, "sp_ln": 1, "gt": 7, "eg": 4, "dec": 3, "kdx": 1, "qe": 1,
    "rope": 4, "score": 8, "ml": 3 * LEVELS, "ab_ready": 3,
    "nmx": 3, "soft": 2, "pn": 3, "ob_h": 3, "sqo": 3, "rno": 4, "oa": 4, "oa_h": 4, "oa_l": 4,
    "gates": 12, "y": 8, "yh": 4, "yl": 4,
    "tap": 2 * 11, "gate_silu": 2 * 11, "ah": 2 * 11, "al": 2 * 11,
    "act_own": 0, "dve_own": 0,
}
PER["act_own"] = 4
PER["dve_own"] = 134


SECOND = ("c2_in", "sq2", "rstd2", "n2", "nh2", "nl2", "raw2", "esq", "ern", "eunit", "enmx", "esoft", "epn", "eob_h", "egh", "econv",
          "eb_h", "eb_l", "oraw", "orot", "osc", "osq", "omean", "ovar", "ogate", "og_h", "og_l", "tap2", "silu2", "conv2", "ah2", "al2")


def bf(ap, axis, shape):
    return ap.unsqueeze(axis).to_broadcast(shape)


def build(nc, a, places, out):
    ctx = ExitStack()
    consts_at1, consts_at2, n1, n2 = places
    with ctx:
        sem = {name: ctx.enter_context(nc.semaphore(name)) for name in PER if name not in ("panel_in", "lin_read")}
        for name in ("start_in", "tables_in", "h0", "rows", "rows2", "stored", "turned", "turned_back", "out_ready", "cleared", "pe_stood", "dve_stood", *SECOND):
            sem[name] = ctx.enter_context(nc.semaphore(name))
        panel_in = [ctx.enter_context(nc.semaphore(f"panel_in{i}")) for i in range(4)]
        lin_read = [ctx.enter_context(nc.semaphore(f"lin_read{i}")) for i in range(4)]
        aux_full = [ctx.enter_context(nc.semaphore(f"aux_full{i}")) for i in range(4)]
        aux_read = [ctx.enter_context(nc.semaphore(f"aux_read{i}")) for i in range(4)]
        lin = [ctx.enter_context(nc.psum_tensor(f"lin{i}", [P, 512], F32)) for i in range(4)]
        aux = [ctx.enter_context(nc.psum_tensor(f"aux{i}", [P, 512], F32)) for i in range(4)]

        base = nc.sbuf_usable_end - nc.sbuf_bytes_remaining
        base = (base + 63) // 64 * 64

        def tile(name, shape, at, dt=F32):
            size = 4 * int(np.prod(shape[1:]))
            assert at % 32 == 0 and at + size <= nc.sbuf_usable_end, (name, at + size - nc.sbuf_usable_end)
            return nc.alloc_sbuf_tensor_at(name, shape, dt, offset=at), (at + size + 31) // 32 * 32

        hT, o = tile("hT", [P, DC, T], base)
        nH, o = tile("nH", [P, DC, T], o, F32R)
        nL, o = tile("nL", [P, DC, T], o, F32R)
        stage, o = tile("stage", [P, 2, DC, PANEL], o)
        wH, o = tile("wH", [P, 2, DC, PANEL], o, F32R)
        wL, o = tile("wL", [P, 2, DC, PANEL], o, F32R)
        c1, o = tile("c1", [P, n1], o)
        par, o = tile("par", [P, 2 * DEPTH, 2 * P], o)
        rates, o = tile("rates", [P, DEPTH, 8], o)
        parL, o = tile("parL", [P, 2 * P + 8], o)
        o = (o + 63) // 64 * 64
        arena = o

        def const(name, n, parts=P):
            return c1[0:parts, consts_at1[name]:consts_at1[name] + n]

        ident, ones = const("ident", P), const("ones", P)
        eps_col, lnq_col = const("cols", 1), c1[:, consts_at1["cols"] + 1:consts_at1["cols"] + 2]
        one_col = c1[:, consts_at1["cols"] + 2:consts_at1["cols"] + 3]

        rawT, o = tile("rawT", [P, 24, T], arena)
        cT, o = tile("cT", [P, 12, T], o)
        zT, o = tile("zT", [P, 4, T], o)
        kd_at = o
        kd, o = tile("kd", [P, 3, 4, P], o)
        vt, o = tile("vt", [P, 3, 4, P], o)
        mixer_tail = o
        nT, o = tile("nT", [P, DC, T], o)
        oH, o = tile("oH", [P, DC, T], o, F32R)
        oL, o2 = tile("oL", [P, DC, T], o, F32R)
        wS, _ = tile("wS", [P, DC, S_ALL], o - 4 * DC * T)
        o = o2

        def blocks(name, at):
            big, at = tile(name, [P, 2, 4, P], at)
            small, at = tile(name + "0", [META, 4, META], at)
            return [small[:, :, :], big[:, 0], big[:, 1]], at

        MT, q_at = blocks("MT", o)
        QD, x_at = blocks("QD", q_at)
        X, a_at = blocks("X", x_at)
        A, ml_at = blocks("A", a_at)
        ML, y_at = blocks("ML", ml_at)
        Y, o2 = blocks("Y", y_at)
        mt_at, o = o, o2
        sqh, _ = tile("sqh", [P, DC, T], x_at)
        gtri, _ = blocks("gtri", x_at)
        bdiag, _ = blocks("bdiag", a_at)
        decay, _ = blocks("decay", ml_at)
        sq_att, _ = tile("sq_att", [P, 6, T], ml_at)
        rnq, _ = tile("rnq", [P, 4, T], mt_at)
        rnk, _ = tile("rnk", [P, 4, T], q_at)
        rnb, _ = tile("rnb", [P, 5, T], kd_at)
        rni, _ = tile("rni", [P, T], kd_at + 4 * 3 * 4 * P)
        tmp4, _ = tile("tmp4", [P, 4, T], y_at)
        R, vn_at = tile("R", [P, 4, P], ml_at)
        vn, _ = tile("vn", [P, 4, P], vn_at)
        S, _ = tile("S", [P, 4, P], y_at)
        Pm, _ = tile("Pm", [P, 4, T], mt_at)
        sqo, _ = tile("sqo", [P, 4, T], x_at)
        rno, _ = tile("rno", [P, 4, T], a_at)
        yT, _ = tile("yT", [P, DC, T], mixer_tail)
        sq8, _ = tile("sq8", [P, DC, T], mixer_tail)
        ytmp, _ = tile("ytmp", [P, 2, T], x_at)
        rl, r_at = tile("rl", [P, 2, 2 * SEQ], mixer_tail)
        score, r_at = tile("score", [P, 2, SEQ], r_at)
        PT, pt_end = tile("PT", [P, 3, 4 * P], mixer_tail)
        assert pt_end <= r_at
        work, r_at = tile("work", [P, 2, SEQ], r_at)
        assert r_at <= mixer_tail + 4 * DC * T
        eg, o2 = tile("eg", [P, 4, T], o)
        oA, _ = tile("oA", [P, 4, T], o)
        o = o2
        bkr, o = tile("bkr", [P, T], o)
        ikr, o = tile("ikr", [P, T], o)
        vtok, o = tile("vtok", [P, 3, P], o)
        bias, o = tile("bias", [P, 2, T], o)
        rs, _ = tile("rs", [P, T], y_at)
        P0, s_at = tile("P0", [META, 4, META], y_at + 4 * 4 * P)
        ab, o = tile("ab", [P, 3, 16], o)
        iw, o = tile("iw", [P, 3, 8], o)
        gx, o = tile("gx", [P, 3, 4], o)
        gm, o = tile("gm", [P, 3, 4], o)
        gl, o = tile("gl", [P, 3, 4], o)
        gg, o = tile("gg", [P, 3, 4], o)
        bt, o = tile("bt", [P, 3, 4], o)
        beta, o = tile("beta", [P, 3, 4], o)
        gcs, o = tile("gcs", [P, 3, 4], o)
        egt, o = tile("egt", [P, 3, 4], o)
        kdx, o = tile("kdx", [P, 3, 4], o)
        sdec, o = tile("sdec", [P, 3, 4], o)
        m8, o = tile("m8", [P, 2, 8], o)
        mx, s_at = tile("mx", [P, 3, 4], s_at)
        nmx, s_at = tile("nmx", [P, 3, 4], s_at)
        sm, s_at = tile("sm", [P, 3, 4], s_at)
        rsm, s_at = tile("rsm", [P, 3, 4], s_at)
        aH, f_at = tile("aH", [P, FC, T], arena, F32R)
        aL, f_at = tile("aL", [P, FC, T], f_at, F32R)
        assert f_at <= mixer_tail
        u, f_at = tile("u", [P, 2, T], mt_at)
        sg, f_at = tile("sg", [P, 2, T], f_at)
        av, f_at = tile("av", [P, 2, T], f_at)
        xin, s_at = tile("xin", [P, 2, D], arena)
        metain, s_at = tile("metain", [META, D], s_at)
        rows, s_at = tile("rows", [P, 2 * DEPTH, 2, P], s_at)
        outT, _ = tile("outT", [P, 2, D], arena)

        n_tok, KB = SEQ, 4 * SEQ
        c2, _ = tile("c2", [P, n2], x_at)
        assert x_at + 4 * n2 <= y_at
        nT2, top = tile("nT2", [P, DC, SEQ], arena + 78 * KB)
        assert top <= x_at
        raw8, e_at = tile("raw8", [P, 8, SEQ], arena)
        vtk, e_at = tile("vtk", [P, 2, 512], e_at)
        Pe0, e_at = tile("Pe0", [P, 8, P], e_at)
        ght, e_at = tile("ght", [P, 4, SEQ], e_at)
        cvt, e_at = tile("cvt", [P, 4, SEQ], e_at)
        Pe, e_at = tile("Pe", [P, 8, SEQ], e_at)
        PTe, e_at = tile("PTe", [P, 2, 8 * P], e_at)
        sqe, e_at = tile("sqe", [P, 8, SEQ], e_at)
        rne, e_at = tile("rne", [P, 8, SEQ], e_at)
        qk2, o_at = tile("qk2", [P, 2, 4, 2, SEQ], arena)
        vtk2, o_at2 = tile("vtk2", [P, 2, 2048], o_at)
        gH, _ = tile("gH", [P, 16, SEQ], arena, F32R)
        gL, _ = tile("gL", [P, 16, SEQ], o_at, F32R)
        sq16, _ = tile("sq16", [P, 16, SEQ], o_at)
        tsin, o_at3 = tile("tsin", [P, 2, 4, SEQ], o_at2)
        o_at = o_at2 + 4 * 4 * SEQ
        rn4, _ = tile("rn4", [P, 4, SEQ], o_at)
        sgT, o_at = tile("sgT", [P, 16, SEQ], o_at3)
        sc, o_at = tile("sc", [P, 4, 384], o_at)
        oR, o_at4 = tile("oR", [P, 16, SEQ], o_at)
        assert o_at4 <= arena + 78 * KB
        aH2, f_at = tile("aH2", [P, FC, SEQ], arena, F32R)
        aL2, f_at = tile("aL2", [P, FC, SEQ], f_at, F32R)
        u2, f_at = tile("u2", [P, 4, SEQ], f_at)
        sg2, f_at = tile("sg2", [P, 2, SEQ], f_at)
        av2, f_at = tile("av2", [P, 2, SEQ], f_at)
        sqf, f_at = tile("sqf", [P, 8, SEQ], f_at)
        e_at = max(e_at, f_at)
        eH, e_at = tile("eH", [P, 8, SEQ], e_at, F32R)
        eL, e_at = tile("eL", [P, 8, SEQ], e_at, F32R)
        assert e_at <= arena + 78 * KB
        assert f_at <= arena + 78 * KB
        mx8, s_at = tile("mx8", [P, 2, 8], y_at + 4 * 4 * P)
        nmx8, s_at = tile("nmx8", [P, 2, 8], s_at)
        sm8, s_at = tile("sm8", [P, 2, 8], s_at)
        rsm8, s_at = tile("rsm8", [P, 2, 8], s_at)
        KE_QG, KE_KG, KE_SC, KE_FN, KE_T2 = 8, 9, 10, 22, 30
        KO_GN, KO_FN, KO_T2 = 8, 24, 32

        def p2(j, k):
            return par[:, DEPTH + j, k:k + 1]

        def table2(name, n):
            return c2[:, consts_at2[name]:consts_at2[name] + n]

        K_CONV, K_NORM1, K_NORM2, K_ANORM, K_QN, K_KN, K_IN, K_BG, K_FCONV = 0, 48, 56, 64, 65, 66, 67, 68, P
        K_DT, K_NA = 2 * P, 2 * P + 4

        def pc(k, n=1):
            return parL[:, k:k + n]

        def at(name, l, n):
            return l * PER[name] + n

        def tok(b):
            return slice(TB[b][0], TB[b][0] + TB[b][1])

        def cdyn(x, width=1):
            return ds(x, width)

        def full(name, l, it=0):
            b, n, step = PLACE[name]
            return aux_full[b], l * AUX_PER[b] + n + it * step

        def read(name, l, it=0, back=0):
            b, n, step = PLACE[name]
            return aux_read[b], l * AUX_PER[b] + (n - back * step) + it * step

        def bank(name):
            return aux[PLACE[name][0]]

        def emptied(name):
            return aux_read[PLACE[name][0]]

        def filled(name):
            return aux_full[PLACE[name][0]]

        def stand(eng, name):
            eng.sem_inc(sem[name], 1)

        def load(sp, m, s, pieces):
            for h, (k0, k1, src) in enumerate(pieces):
                sp.wait_ge(sem["wlo"], 4 * m + 2 * s + h + 1)
                sp.dma_start(stage[:, s, k0:k1, :], src).then_inc(panel_in[2 * s + h], 16)

        def split_hi(act, m, s):
            act.wait_ge(sem["whi_used"], 2 * m + s + 1)
            for h in range(2):
                ks = slice(4 * h, 4 * h + 4)
                act.wait_ge(panel_in[2 * s + h], 16 * m + 16)
                nc.scalar.activation(wH[:, s, ks], stage[:, s, ks], ACT.Copy).then_inc(sem["whi"], 1)

        def split_lo(dve, m, s, on_pool=False):
            dve.wait_ge(sem["panel_done"], 2 * m + s + 1)
            for h in range(2):
                ks = slice(4 * h, 4 * h + 4)
                dve.wait_ge(sem["whi"], 4 * m + 2 * s + h + 1)
                (nc.gpsimd if on_pool else nc.vector).tensor_tensor(wL[:, s, ks], stage[:, s, ks], wH[:, s, ks].bitcast(F32), ALU.subtract).then_inc(sem["wlo"], 1)

        def multiply(pe, m, s, rnd, groups, width, start=True, stop=True, banks=lin):
            pe.wait_ge(sem["whi"], 4 * m + 2 * s + 2)
            for b, _, _ in groups:
                if start and banks is lin and rnd is not None:
                    pe.wait_ge(lin_read[b], rnd)
            for b, cols, ks in groups:
                for n, (k, xh, xl) in enumerate(ks):
                    nc.tensor.matmul(banks[b][:, 0:width], wH[:, s, k, cols], xh, start=start and n == 0, stop=False)
                    mm = nc.tensor.matmul(banks[b][:, 0:width], wH[:, s, k, cols], xl, start=False, stop=False)
            mm.then_inc(sem["whi_used"], 1)
            pe.wait_ge(sem["wlo"], 4 * m + 2 * s + 6)
            for b, cols, ks in groups:
                for n, (k, xh, _) in enumerate(ks):
                    mm = nc.tensor.matmul(banks[b][:, 0:width], wL[:, s, k, cols], xh, start=False, stop=stop and n == len(ks) - 1)
            mm.then_inc(sem["panel_done"], 1)

        def multiply_first(pe, m, rnd, groups, width, hi_ready, lo_ready, at_once=False):
            pe.wait_ge(sem["whi"], 4 * m + 2)
            pe.wait_ge(sem["wlo"], 4 * m + 6)
            for b, _, _ in groups:
                if rnd is not None:
                    pe.wait_ge(lin_read[b], rnd)

            def product(w, x, pair, first=False, last=False):
                for b, cols, ks in groups:
                    for term in ks[2 * pair:2 * pair + 2]:
                        k = term[0]
                        t = nc.tensor.matmul(lin[b][:, 0:width], w[:, 0, k, cols], term[x], start=first and k == 0, stop=last and k == DC - 1)
                return t

            pairs = range(DC // 2)
            for pair in pairs:
                pe.wait_ge(*hi_ready(pair))
                product(wH, 1, pair, first=True)
                product(wL, 1, pair)
                if at_once:
                    pe.wait_ge(*lo_ready(pair))
                    mm = product(wH, 2, pair, last=True)
            for pair in [] if at_once else pairs:
                pe.wait_ge(*lo_ready(pair))
                mm = product(wH, 2, pair, last=True)
            mm.then_inc(sem["whi_used"], 1)
            pe.wait_ge(sem["whi_used"], 2 * m + 3)
            pe.sem_inc(sem["panel_done"], 1)

        def halves(s, x_hi, x_lo, n=DC, k0=0):
            return [(2 * s + c, slice(c * P, c * P + P), [(k, x_hi[:, k0 + k, :], x_lo[:, k0 + k, :]) for k in range(n)])
                    for c in range(2)]

        block = ctx.enter_context(nc.Block())

        def w_rows(name, k_all):
            return a[name].rearrange("l (k p) n -> p (l k) n", p=P), k_all

        @block.sync
        def _(sp):
            early = consts_at1["half"]
            sp.dma_start(c1[:, 0:early], a["c1"][:, 0:early]).then_inc(sem["start_in"], 16)
            sp.dma_start(xin[:, :, :], a["x"].rearrange("b (j p) d -> p (b j) d", p=P)).then_inc(sem["start_in"], 16)
            sp.dma_start(metain[:, :], a["meta_tokens"]).then_inc(sem["start_in"], 16)

            sp.wait_ge(sem["cleared"], 1)

            def row(t, r, src, n, cols=slice(0, P)):
                sp.dma_start(rows[r:r + n, 0:DEPTH, t, cols], src).then_inc(sem["rows"], 16)

            row(0, K_CONV, a["conv_a"].rearrange("l k (c p) -> (k c) l p", p=P), 48)
            row(0, K_NORM1, a["norm_mix"].rearrange("l (c p) -> c l p", p=P), DC)
            row(0, K_NORM2, a["norm_ffn"].rearrange("l (c p) -> c l p", p=P), DC)
            for r, name in ((K_ANORM, "a_out_norm"), (K_QN, "q_norm"), (K_KN, "k_norm")):
                row(0, r, a[name].unsqueeze(0), 1)
            row(0, K_IN, a["kidx_norm"].unsqueeze(0), 1, slice(0, 64))
            row(0, K_IN, a["kidx_norm"].unsqueeze(0), 1, slice(64, P))
            row(0, K_BG, a["b_gate"].rearrange("l (c p) -> c l p", p=P), 16)
            row(1, 0, a["conv_ffn"].rearrange("l k (c p) -> (k c) l p", p=P), 66)
            for n, name in enumerate(("dt_bias", "a_log")):
                sp.dma_start(rates[:, :, 4 * n:4 * n + 4], a[name].unsqueeze(0).to_broadcast([P, DEPTH, 4])).then_inc(sem["rows"], 16)
            sp.dma_start(c1[:, early:n1], a["c1"][:, early:n1]).then_inc(sem["tables_in"], 16)

            def whole(w, l, kd_, col):
                return [(k0, k0 + 4, w[:, ds(l * kd_ + k0, 4), ds(col, PANEL)]) for k0 in (0, 4)]

            w_in, _ = w_rows("w_in", DC)
            w_gate, _ = w_rows("w_gate", DC)
            w_a, _ = w_rows("w_branch_a", 4)
            w_b, _ = w_rows("w_branch_b", 4)
            w_out, _ = w_rows("w_out", DC)
            w_up, _ = w_rows("w_up", DC)
            w_down, _ = w_rows("w_down", FC)

            def layer(l):
                m0 = l * M_LAYER
                with sp.Fori(0, 4) as i:
                    for s in range(2):
                        load(sp, m0 + i, s, whole(w_in, l, DC, i * 512 + s * PANEL))
                for i, col in ((4, C_BQ), (5, C_IQ)):
                    for s in range(2):
                        load(sp, m0 + i, s, whole(w_in, l, DC, col + s * PANEL))
                with sp.Fori(0, 4) as i:
                    for s in range(2):
                        load(sp, m0 + M_GATE + i, s, whole(w_gate, l, DC, i * 512 + s * PANEL))
                with sp.Fori(0, 2) as i:
                    for s in range(2):
                        cols = ds(i * 512 + s * PANEL, PANEL)
                        load(sp, m0 + M_BRANCH + i, s, [(0, 4, w_a[:, ds(l * 4, 4), cols]), (4, 8, w_b[:, ds(l * 4, 4), cols])])
                with sp.Fori(0, 2) as i:
                    for s in range(2):
                        load(sp, m0 + M_OUT + i, s, whole(w_out, l, DC, i * 512 + s * PANEL))
                with sp.Fori(0, 11) as i:
                    for s in range(2):
                        load(sp, m0 + M_UP + i, s, whole(w_up, l, DC, i * PANEL + s * FF))
                with sp.Fori(0, 2) as i:
                    for p in range(6):
                        k0, n = DOWN_K[p % 3]
                        cols = ds(i * 512 + (p // 3) * PANEL, PANEL)
                        load(sp, m0 + M_DOWN + 3 * i + p // 2, p % 2,
                             [(h, min(h + 4, n), w_down[:, ds(l * FC + k0 + h, min(4, n - h)), cols]) for h in (0, 4)])

            with sp.Fori(0, DEPTH) as l:
                layer(l)

            def mlp2(j, m):
                up = a["ffn_w_up_2"].rearrange("l (k p) n -> p (l k) n", p=P)
                down = a["ffn_w_down_2"].rearrange("l (k p) n -> p (l k) n", p=P)
                with sp.Fori(0, 11) as i:
                    for s in range(2):
                        load(sp, m + i, s, whole(up, j, DC, i * PANEL + s * FF))
                with sp.Fori(0, 2) as i:
                    for p in range(6):
                        k0, n = DOWN_K[p % 3]
                        cols = ds(i * 512 + (p // 3) * PANEL, PANEL)
                        load(sp, m + 11 + 3 * i + p // 2, p % 2,
                             [(h, min(h + 4, n), down[:, j * FC + k0 + h:j * FC + k0 + min(h + 4, n), cols]) for h in (0, 4)])

            def columns(name, m, pairs):
                w = a[name].rearrange("l (k p) n -> p (l k) n", p=P)
                with sp.Fori(0, pairs) as i:
                    for s in range(2):
                        load(sp, m + i, s, whole(w, 0, DC, i * 512 + s * PANEL))

            w = a["even_w_in_2"].rearrange("l (k p) n -> p (l k) n", p=P)
            for i, part in enumerate((0, 1, 5, 4, 2, 3)):
                for s in range(2):
                    load(sp, M_E + i, s, whole(w, 0, DC, part * 512 + s * PANEL))
            columns("even_w_out_2", M_E + E_OUT, 2)
            mlp2(0, M_E + E_UP)
            columns("ret_wq_2", M_O, 2)
            columns("ret_wk_2", M_O + O_K, 2)
            columns("ret_wv_2", M_O + O_V, 4)
            columns("ret_wg_2", M_O + O_G, 4)
            w_o = a["ret_wo_2"].rearrange("l (k p) n -> p (l k) n", p=P)
            with sp.Fori(0, 4) as i:
                for s in range(2):
                    load(sp, M_O + O_OUT + i, s, [(k0, k0 + 4, w_o[:, 8 * s + k0:8 * s + k0 + 4, ds(i * PANEL, PANEL)]) for k0 in (0, 4)])
            mlp2(1, M_O + O_UP)
            sp.wait_ge(sem["out_ready"], 4)
            sp.dma_start(out.rearrange("(j p) d -> p j d", p=P), outT[:, :, :]).then_inc(sem["stored"], 16)
            sp.wait_ge(sem["stored"], 16)

        @block.gpsimd
        def _(pool):
            pool.wait_ge(sem["cleared"], 1)

            def row2(j, t, r, src, n, cols=slice(0, P)):
                pool.dma_start(rows[r:r + n, DEPTH + j, t, cols], src).then_inc(sem["rows2"], 16)

            row2(0, 0, 0, a["even_norm_2"].rearrange("l (c p) -> (l c) p", p=P), DC)
            for r, name in ((KE_QG, "even_q_gain_2"), (KE_KG, "even_k_gain_2")):
                for h in range(2):
                    row2(0, 0, r, a[name], 1, slice(64 * h, 64 * h + 64))
            row2(0, 0, KE_SC, a["even_sconv_w_2"].rearrange("l k (c p) -> (l k c) p", p=P), 12)
            row2(1, 0, 0, a["odd_norm_2"].rearrange("l (c p) -> (l c) p", p=P), DC)
            row2(1, 0, KO_GN, a["ret_gn_gain_2"].rearrange("l h (c p) -> (l h c) p", p=P), 16)
            for j, fn, t2 in ((0, KE_FN, KE_T2), (1, KO_FN, KO_T2)):
                row2(j, 0, fn, a["ffn_norm_2"][j].rearrange("(c p) -> c p", p=P), DC)
                row2(j, 0, t2, a["ffn_conv_w_2"][j, 2:3].rearrange("k (c p) -> (k c) p", p=P), 2 * FC)
                row2(j, 1, 0, a["ffn_conv_w_2"][j, 0:2].rearrange("k (c p) -> (k c) p", p=P), 4 * FC)
            w = a["w_in"].rearrange("l (k p) n -> p (l k) n", p=P)
            for l in range(DEPTH):
                if l:
                    pool.wait_ge(sem["panel_done"], at("panel_done", l - 1, 2 * M_OUT + 2))
                for to, of, n in ((S_IK, C_IK, 64), (S_IK + 64, C_IK, 64), (S_BK, C_BK, 2 * P), (S_AB, C_AB, 8), (S_AB + 8, C_IK + 64, 8)):
                    pool.dma_start(wS[:, :, to:to + n], w[:, l * DC:(l + 1) * DC, of:of + n]).then_inc(sem["small_in"], 16)
                for m in range(M_GATE, M_BRANCH):
                    for s in range(2):
                        pool.wait_ge(sem["wlo"], 4 * (l * M_LAYER + m) + 2 * s + 4)
                        split_lo(pool, l * M_LAYER + m, s, on_pool=True)
            pool.wait_ge(sem["small_in"], DEPTH * 80)
            pool.wait_ge(sem["nl"], DEPTH * PER["nl"])
            pool.dma_start(c2[:, :], a["c2"]).then_inc(sem["c2_in"], 16)
            pool.wait_ge(sem["c2_in"], 16)

        @block.tensor
        def _(pe):
            def begin(name, l, it=0):
                b, n, step = PLACE[name]
                if n > 1:
                    pe.wait_ge(aux_read[b], l * AUX_PER[b] + n - 1 + it * step)
                return aux[b]

            def mm(o_, l_, r_, start=True, stop=True):
                return nc.tensor.matmul(o_, l_, r_, start=start, stop=stop)

            pe.sem_inc(sem["whi_used"], 2)
            pe.sem_inc(sem["panel_done"], 2)
            pe.wait_ge(sem["start_in"], 48)
            for c in range(DC):
                if c >= 4:
                    pe.wait_ge(sem["h0"], c - 3)
                cols = slice(c * P, c * P + P)
                nc.tensor.transpose(lin[c % 4][:, 0:META], metain[:, cols], ident[0:META, 0:META])
                for j in range(2):
                    t = nc.tensor.transpose(lin[c % 4][:, META + j * P:META + (j + 1) * P], xin[:, j, cols], ident)
                t.then_inc(sem["turned"], 1)
            pe.wait_ge(sem["rows"], 12 * 16)
            for l in range(2 * DEPTH):
                if l == DEPTH:
                    pe.wait_ge(sem["rows2"], 14 * 16)
                pe.wait_ge(sem["h0"], 5 + l)
                nc.tensor.transpose(lin[l][:, 0:P], rows[:, l, 0, :], ident)
                nc.tensor.transpose(lin[l][:, P:2 * P], rows[:, l, 1, :], ident).then_inc(sem["turned"], 1)

            pe.wait_ge(sem["tables_in"], 16)

            def mean_square(name, l, which):
                ps = begin(name, l)
                for c in range(DC):
                    if c % 2 == 0:
                        pe.wait_ge(sem["sq"], at("sq", l, 4 * (which - 1) + c // 2 + 1))
                    t = mm(ps[:, 0:T], ones, sq8[:, c, :], c == 0, c == DC - 1)
                t.then_inc(filled(name), 1)

            def behind_norm(l, which):
                return (lambda pair: (sem["nh"], at("nh", l, 4 * (which - 1) + pair + 1)),
                        lambda pair: (sem["nl"], at("nl", l, 4 * (which - 1) + pair + 1)))

            def layer(l):
                m0, r0 = l * M_LAYER, l * R_LAYER
                mean_square("ms1", l, 1)
                multiply_first(pe, m0, None, halves(0, nH, nL), T, *behind_norm(l, 1))
                multiply(pe, m0, 1, None, halves(1, nH, nL), T)
                pe.wait_ge(sem["small_in"], at("small_in", l, 80))
                for name, col in (("ik", S_IK), ("bk", S_BK)):
                    ps = begin(name, l)
                    for k in range(DC):
                        t = mm(ps[:, 0:T], wS[:, k, col:col + P], nT[:, k, :], k == 0, k == DC - 1)
                    t.then_inc(filled(name), 1)
                ps, n = begin("tk", l), S_ALL - S_BV
                for b in range(3):
                    for k in range(DC):
                        t = mm(ps[0:TB[b][1], b * n:(b + 1) * n], nT[:, k, tok(b)], wS[:, k, S_BV:S_ALL], k == 0, k == DC - 1)
                t.then_inc(filled("tk"), 1)
                with pe.Fori(1, 6) as i:
                    for s in range(2):
                        multiply(pe, m0 + i, s, r0 + i, halves(s, nH, nL), T)

                pe.wait_ge(sem["sq_heads"], at("sq_heads", l, 2))
                for h in range(8):
                    name = f"ss{'qk'[h // 4]}{h % 4}"
                    mm(begin(name, l)[:, 0:T], ones, sqh[:, h, :]).then_inc(filled(name), 1)
                pe.wait_ge(sem["sq_att"], at("sq_att", l, 1))
                for h, name in enumerate([f"sbq{h}" for h in range(4)] + ["sbk", "sik"]):
                    mm(begin(name, l)[:, 0:T], ones, sq_att[:, h, :]).then_inc(filled(name), 1)

                def gate(i, slots=(0, 1)):
                    for s in slots:
                        multiply(pe, m0 + M_GATE + i, s, r0 + R_GATE + i, halves(s, nH, nL), T)

                gate(0)
                pe.wait_ge(sem["gt"], at("gt", l, 1))
                ps = begin("gc", l)
                for b in (1, 2, 0):
                    n = TB[b][1]
                    t = mm(ps[0:n, 4 * b:4 * b + 4], const("upto", n, n), gg[0:n, b, :])
                t.then_inc(filled("gc"), 1)
                for b in range(3):
                    n = TB[b][1]
                    for name, src, count in ((f"gb{b}", gtri, 2 + b), (f"bb{b}", bdiag, 5 + b)):
                        pe.wait_ge(sem["gt"], at("gt", l, count))
                        mm(begin(name, l)[:, 0:4 * n], ones[0:n, :], src[b].rearrange("p h c -> p (h c)")).then_inc(filled(name), 1)
                pe.wait_ge(sem["qk_unit"], at("qk_unit", l, 2))
                for b in range(3):
                    n = TB[b][1]
                    for name, off in ((f"kk{b}", 4), (f"qk{b}", 0)):
                        ps = begin(name, l)
                        for h in range(4):
                            t = mm(ps[0:n, h * n:(h + 1) * n], cT[:, 4 + h, tok(b)], cT[:, off + h, tok(b)])
                        t.then_inc(filled(name), 1)
                for b in range(3):
                    n = TB[b][1]
                    for name, off in ((f"kt{b}", 4), (f"vt{b}", 8)):
                        ps = begin(name, l)
                        if off == 8 and b == 0:
                            pe.wait_ge(sem["silu"], at("silu", l, 3))
                        for h in range(4):
                            t = nc.tensor.transpose(ps[0:n, h * P:(h + 1) * P], cT[:, off + h, tok(b)], ident)
                        t.then_inc(filled(name), 1)
                pe.wait_ge(sem["att_unit"], at("att_unit", l, 3))
                for h in range(4):
                    mm(begin(f"rq{h}", l)[:, 0:T], const("turn_a", P), rawT[:, 16 + h, :]).then_inc(filled(f"rq{h}"), 1)
                pe.wait_ge(lin_read[3], r0 + 6)
                for c in range(4):
                    mm(begin(f"ri{c}", l)[:, 0:T], const("turn_i", P), rawT[:, 20 + c, :]).then_inc(filled(f"ri{c}"), 1)
                mm(begin("rk", l)[:, 0:T], const("turn_a", P), bkr[:, :]).then_inc(filled("rk"), 1)
                mm(begin("rik", l)[:, 0:T], const("turn_i", P), ikr[:, :]).then_inc(filled("rik"), 1)
                gate(1)
                pe.wait_ge(sem["rope"], at("rope", l, 4))
                for j in range(2):
                    for e in range(4):
                        name = f"ix{j}{e}"
                        ps = begin(name, l)
                        for n in range(2):
                            h = 4 * (e // 2) + e % 2 + 2 * n
                            r = 64 * (h % 2)
                            t = mm(ps[:, n * SEQ:(n + 1) * SEQ], rawT[r:r + 64, 20 + h // 2, tok(j + 1)], ikr[r:r + 64, META:T])
                        t.then_inc(filled(name), 1)
                with pe.Fori(0, LEVELS) as it:
                    for b in range(3):
                        n = TB[b][1]
                        pe.wait_ge(sem["ml"], at("ml", l, it * 3 + b + 1))
                        pe.wait_ge(*read(f"X{b}" if b else "XA0", l, it, 1))
                        ps = begin(f"Y{b}", l, it)
                        if b == 0:
                            stand(pe, "pe_stood")
                        for h in range(4):
                            t = mm(ps[0:n, h * n:(h + 1) * n], ML[b][:, h, :], X[b][:, h, :])
                        t.then_inc(filled(f"Y{b}"), 1)
                    pe.wait_ge(*read("Y0", l, it))
                    ps = begin("XA0", l, it)
                    stand(pe, "pe_stood")
                    for h in range(4):
                        mm(ps[0:META, h * META:(h + 1) * META], A[0][:, h, :], Y[0][:, h, :])
                        t = mm(ps[0:META, (4 + h) * META:(5 + h) * META], Y[0][:, h, :], A[0][:, h, :])
                    t.then_inc(filled("XA0"), 1)
                    for b in (1, 2):
                        pe.wait_ge(*read(f"Y{b}", l, it))
                        pe.wait_ge(*read(f"A{b}", l, it, 1))
                        for name, lhs, rhs in ((f"X{b}", A, Y), (f"A{b}", Y, A)):
                            ps = begin(name, l, it)
                            for h in range(4):
                                t = mm(ps[:, h * P:(h + 1) * P], lhs[b][:, h, :], rhs[b][:, h, :])
                            t.then_inc(filled(name), 1)

                def state_seen(b):
                    pe.wait_ge(*read(f"dS{b - 1}", l))
                    ps = begin(f"kS{b}", l)
                    for h in range(4):
                        t = mm(ps[:, h * P:(h + 1) * P], cT[:, 4 + h, tok(b)], S[:, h, :])
                    t.then_inc(filled(f"kS{b}"), 1)

                def new_values(b):
                    n = TB[b][1]
                    rhs = R if b else vt[0:n, 0]
                    if b:
                        pe.wait_ge(*read(f"kS{b}", l))
                    pe.wait_ge(sem["ab_ready"], at("ab_ready", l, b + 1))
                    ps = begin(f"vn{b}", l)
                    if b == 0:
                        stand(pe, "pe_stood")
                    for h in range(4):
                        t = mm(ps[0:n, h * P:(h + 1) * P], A[b][:, h, :], rhs[:, h, :])
                    t.then_inc(filled(f"vn{b}"), 1)

                def delta_out(b):
                    n = TB[b][1]
                    pe.wait_ge(*read(f"vn{b}", l))
                    pe.wait_ge(sem["qe"], at("qe", l, 1))
                    ps = begin(f"o{b}", l)
                    for h in range(4):
                        if b:
                            mm(ps[:, h * n:(h + 1) * n], S[:, h, :], cT[:, h, tok(b)], True, False)
                        t = mm(ps[:, h * n:(h + 1) * n], vn[0:n, h, :], QD[b][:, h, :], b == 0, True)
                    t.then_inc(filled(f"o{b}"), 1)
                    if b < 2:
                        ps = begin(f"dS{b}", l)
                        for h in range(4):
                            t = mm(ps[:, h * P:(h + 1) * P], kd[0:n, b, h, :], vn[0:n, h, :])
                        t.then_inc(filled(f"dS{b}"), 1)

                def scores(j):
                    if j == 0:
                        ps = begin("s0", l)
                        for h in range(4):
                            t = mm(ps[0:META, h * META:(h + 1) * META], rawT[:, 16 + h, 0:META], bkr[:, 0:META])
                        t.then_inc(filled("s0"), 1)
                        return
                    for h in range(4):
                        name = f"s{'abcd'[h]}{j}"
                        mm(begin(name, l)[:, 0:T], rawT[:, 16 + h, tok(j)], bkr[:, :]).then_inc(filled(name), 1)

                def weights_turned(j):
                    pe.wait_ge(sem["pn"], at("pn", l, 1 + j))
                    if j == 0:
                        ps = begin("pt0", l)
                        stand(pe, "pe_stood")
                        for h in range(4):
                            t = nc.tensor.transpose(ps[0:META, h * META:(h + 1) * META], P0[:, h, :], ident[0:META, 0:META])
                        t.then_inc(filled("pt0"), 1)
                        return
                    for b in range(3):
                        name = f"pt{b}_{j}"
                        ps = begin(name, l)
                        for h in range(4):
                            t = nc.tensor.transpose(ps[0:TB[b][1], h * P:(h + 1) * P], Pm[:, h, tok(b)], ident)
                        t.then_inc(filled(name), 1)

                def weighted_values(j):
                    ps = begin(f"pv{j}", l)
                    if j == 0:
                        pe.wait_ge(*read("pt0", l))
                        mm(ps[:, 0:4 * META], vtok[0:META, 0, :], PT[0:META, 0, 0:4 * META]).then_inc(filled("pv0"), 1)
                        return
                    for b in range(3):
                        n = TB[b][1]
                        pe.wait_ge(*read(f"pt{b}_{j}", l))
                        t = mm(ps[:, :], vtok[0:n, b, :], PT[0:n, b, :], b == 0, b == 2)
                    t.then_inc(filled(f"pv{j}"), 1)

                new_values(0)
                scores(0)
                scores(1)
                gate(2, [0])
                delta_out(0)
                weights_turned(0)
                gate(2, [1])
                state_seen(1)
                weighted_values(0)
                weights_turned(1)
                gate(3, [0])
                new_values(1)
                scores(2)
                delta_out(1)
                weighted_values(1)
                state_seen(2)
                weights_turned(2)
                new_values(2)
                weighted_values(2)
                delta_out(2)
                pe.wait_ge(sem["sqo"], at("sqo", l, 3))
                for h in range(4):
                    mm(begin(f"so{h}", l)[:, 0:T], ones, sqo[:, h, :]).then_inc(filled(f"so{h}"), 1)
                gate(3, [1])
                pe.wait_ge(sem["oa_l"], at("oa_l", l, 4))
                pe.wait_ge(*read("pv2", l))
                stand(pe, "pe_stood")
                with pe.Fori(0, 2) as i:
                    for s in range(2):
                        if s:
                            for b in range(4):
                                begin(f"br{b}", l, i)
                        multiply(pe, m0 + M_BRANCH + i, s, r0 + R_BRANCH + i,
                                 [(2 * br + c, slice(c * P, c * P + P), [(4 * br + k, oH[:, 4 * br + k, :], oL[:, 4 * br + k, :]) for k in range(4)])
                                  for br in range(2) for c in range(2)], T, banks=[bank(f"br{b}") for b in range(4)] if s else lin)
                    for b in range(4):
                        pe.sem_inc(filled(f"br{b}"), 1)
                multiply_first(pe, m0 + M_OUT, r0 + R_OUT, halves(0, nH, nL), T,
                               lambda pair: (sem["yh"], at("yh", l, pair + 1)), lambda pair: (sem["yl"], at("yl", l, pair + 1)), at_once=True)
                multiply(pe, m0 + M_OUT, 1, r0 + R_OUT, halves(1, nH, nL), T)
                for s in range(2):
                    multiply(pe, m0 + M_OUT + 1, s, r0 + R_OUT + 1, halves(s, nH, nL), T)
                mean_square("ms2", l, 2)
                multiply_first(pe, m0 + M_UP, r0 + R_UP, halves(0, nH, nL), T, *behind_norm(l, 2))
                multiply(pe, m0 + M_UP, 1, r0 + R_UP, halves(1, nH, nL), T)
                with pe.Fori(1, 11) as i:
                    for s in range(2):
                        multiply(pe, m0 + M_UP + i, s, r0 + R_UP + i, halves(s, nH, nL), T)
                with pe.Fori(0, 2) as i:
                    for p in range(6):
                        k0, n = DOWN_K[p % 3]
                        pe.wait_ge(sem["al"], at("al", l, k0 + n))
                        multiply(pe, m0 + M_DOWN + 3 * i + p // 2, p % 2, r0 + R_DOWN + i, 
                                 [(2 * (p // 3) + c, slice(c * P, c * P + P), [(k, aH[:, k0 + k, :], aL[:, k0 + k, :]) for k in range(n)])
                                  for c in range(2)], T, start=p % 3 == 0, stop=p % 3 == 2)

            with pe.Fori(0, DEPTH) as l:
                layer(l)

            L = DEPTH

            def multiply_tok(m, s, rnd):
                pe.wait_ge(sem["whi"], 4 * m + 2 * s + 2)
                for j in range(2):
                    pe.wait_ge(lin_read[2 * s + j], rnd)
                    to, rows_ = lin[2 * s + j][:, 0:PANEL], slice(j * P, j * P + P)
                    for k in range(DC):
                        mm(to, nH[:, k, rows_], wH[:, s, k, :], k == 0, False)
                        t = mm(to, nL[:, k, rows_], wH[:, s, k, :], False, False)
                t.then_inc(sem["whi_used"], 1)
                pe.wait_ge(sem["wlo"], 4 * m + 2 * s + 6)
                for j in range(2):
                    for k in range(DC):
                        t = mm(lin[2 * s + j][:, 0:PANEL], nH[:, k, j * P:j * P + P], wL[:, s, k, :], False, k == DC - 1)
                t.then_inc(sem["panel_done"], 1)

            nH2, nL2 = nH[:, :, 0:SEQ], nL[:, :, 0:SEQ]

            def mean_square2(name, which):
                ps = begin(name, L)
                for c in range(DC):
                    if c % 2 == 0:
                        pe.wait_ge(*((sem["sq"], at("sq", L, c // 2 + 1)) if which == 1 else (sem["sq2"], 4 * (which - 2) + c // 2 + 1)))
                    t = mm(ps[:, 0:SEQ], ones, sq8[:, c, META:T] if which == 1 else sqf[:, c, :], c == 0, c == DC - 1)
                t.then_inc(filled(name), 1)

            def first_pair(which, m, r):
                multiply_first(pe, m, r, halves(0, nH2, nL2), SEQ, lambda pair: (sem["nh2"], 4 * (which - 1) + pair + 1),
                               lambda pair: (sem["nl2"], 4 * (which - 1) + pair + 1))
                multiply(pe, m, 1, r, halves(1, nH2, nL2), SEQ)

            def mlp2(name, which, m, r):
                mean_square2(name, which)
                first_pair(which, m, r)
                with pe.Fori(1, 11) as i:
                    for s in range(2):
                        multiply(pe, m + i, s, r + i, halves(s, nH2, nL2), SEQ)
                with pe.Fori(0, 2) as i:
                    for p in range(6):
                        k0, n = DOWN_K[p % 3]
                        pe.wait_ge(sem["al2"], FC * (which // 2 - 1) + k0 + n)
                        multiply(pe, m + 11 + 3 * i + p // 2, p % 2, r + 11 + i,
                                 [(2 * (p // 3) + c, slice(c * P, c * P + P), [(k, aH2[:, k0 + k, :], aL2[:, k0 + k, :]) for k in range(n)])
                                  for c in range(2)], SEQ, start=p % 3 == 0, stop=p % 3 == 2)

            mean_square2("ems", 1)
            first_pair(1, M_E, R_E)

            def even(i, s):
                multiply(pe, M_E + i, s, R_E + i, halves(s, nH2, nL2), SEQ)

            def even_scores(j):
                keys = (j + 1) * P
                for e, heads in enumerate([(0, 2, 4, 6), (1, 3, 5, 7)] if j == 0 else [(0, 2), (1, 3), (4, 6), (5, 7)]):
                    name = f"e{j}{e}"
                    ps = begin(name, L)
                    for n, h in enumerate(heads):
                        r = 64 * (h % 2)
                        t = mm(ps[:, n * keys:(n + 1) * keys], raw8[r:r + 64, h // 2, j * P:j * P + P], raw8[r:r + 64, 4 + h // 2, 0:keys])
                    t.then_inc(filled(name), 1)

            def even_turned(j):
                pe.wait_ge(sem["epn"], 1 + j)
                src = Pe if j else Pe0
                for g in range(2):
                    for b in range(j + 1):
                        name = f"et{j}{g}" + (str(b) if j else "")
                        ps = begin(name, L)
                        for h in range(4):
                            t = nc.tensor.transpose(ps[:, h * P:(h + 1) * P], src[:, 4 * g + h, b * P:b * P + P], ident)
                        t.then_inc(filled(name), 1)

            def even_values(j):
                for name in ("et100", "et101", "et110", "et111") if j else ("et00", "et01"):
                    pe.wait_ge(*read(name, L))
                for b in range(4):
                    pe.wait_ge(lin_read[b], R_E + 5)
                ps = begin(f"ev{j}", L)
                for h in range(8):
                    r = 64 * (h % 2)
                    for b in range(j + 1):
                        t = mm(ps[r:r + 64, (h // 2) * P:(h // 2 + 1) * P], vtk[:, b, h * 64:h * 64 + 64], PTe[:, b, h * P:(h + 1) * P], b == 0, b == j)
                t.then_inc(filled(f"ev{j}"), 1)

            for s in range(2):
                even(1, s)
            even(2, 0)
            pe.wait_ge(sem["esq"], 2)
            for c in range(4):
                mm(begin(f"eq{c}", L)[:, :], const("half", P), sqe[:, 2 * c:2 * c + 2, :].rearrange("p c t -> p (c t)")).then_inc(filled(f"eq{c}"), 1)
            even(2, 1)
            even(3, 0)
            pe.wait_ge(sem["eunit"], 2)
            even_scores(0)
            even_scores(1)
            even(3, 1)
            even_turned(0)
            for s in range(2):
                multiply_tok(M_E + 4, s, R_E + 4)
            even_values(0)
            even_turned(1)
            even(5, 0)
            even_values(1)
            even(5, 1)
            def branch_ready(pair):
                return read("ev1", L) if pair < 2 else (sem["eb_l"], pair - 1)

            multiply_first(pe, M_E + E_OUT, R_E + E_OUT, halves(0, eH, eL), SEQ, branch_ready, branch_ready, at_once=True)
            multiply(pe, M_E + E_OUT, 1, R_E + E_OUT, halves(1, eH, eL), SEQ)
            for s in range(2):
                multiply(pe, M_E + E_OUT + 1, s, R_E + E_OUT + 1, halves(s, eH, eL), SEQ)
            mlp2("emf", 2, M_E + E_UP, R_E + E_UP)

            mean_square2("oms", 3)
            first_pair(3, M_O, R_O)
            with pe.Fori(1, 4) as i:
                for s in range(2):
                    multiply(pe, M_O + i, s, R_O + i, halves(s, nH2, nL2), SEQ)
            with pe.Fori(O_V, O_G) as i:
                for s in range(2):
                    multiply_tok(M_O + i, s, R_O + i)
            pe.wait_ge(sem["orot"], 4)
            for b in range(4):
                pe.wait_ge(lin_read[b], R_O + O_G)
            for h in range(4):
                ps = begin(f"os{h}", L)
                for b in range(2):
                    to = ps[:, 0:SEQ] if b == 0 else ps[:, SEQ:SEQ + P]
                    for d in range(2):
                        t = mm(to, qk2[:, 1, h, d, b * P:b * P + P], qk2[:, 0, h, d, b * P:SEQ], d == 0, d == 1)
                t.then_inc(filled(f"os{h}"), 1)
            def odd_g(i, s):
                multiply(pe, M_O + O_G + i, s, R_O + O_G + i, halves(s, nH2, nL2), SEQ)

            odd_g(0, 0)
            for h in range(4):
                pe.wait_ge(*read(f"os{h}", L))
                for e in range(2):
                    name = f"oo{h}{e}"
                    ps = begin(name, L)
                    for n in range(2):
                        cols = slice(h * 512 + (2 * e + n) * P, h * 512 + (2 * e + n + 1) * P)
                        mm(ps[:, n * SEQ:(n + 1) * SEQ], vtk2[:, 0, cols], sc[:, h, 0:SEQ], True, False)
                        t = mm(ps[:, n * SEQ + P:(n + 1) * SEQ], vtk2[:, 1, cols], sc[:, h, SEQ:SEQ + P], False, True)
                    t.then_inc(filled(name), 1)
            odd_g(0, 1)
            odd_g(1, 0)
            for h in range(4):
                pe.wait_ge(*read(f"oo{h}0", L))
                pe.wait_ge(*read(f"oo{h}1", L))
                ps = begin(f"om{h}", L)
                for e in range(4):
                    t = mm(ps[:, 0:SEQ], ones, oR[:, 4 * h + e, :], e == 0, e == 3)
                t.then_inc(filled(f"om{h}"), 1)
            odd_g(1, 1)
            odd_g(2, 0)
            for h in range(4):
                pe.wait_ge(sem["osq"], h + 1)
                ps = begin(f"ow{h}", L)
                for e in range(4):
                    t = mm(ps[:, 0:SEQ], ones, sq16[:, 4 * h + e, :], e == 0, e == 3)
                t.then_inc(filled(f"ow{h}"), 1)
            odd_g(2, 1)
            odd_g(3, 0)
            odd_g(3, 1)
            with pe.Fori(0, 2) as i:
                for q in range(2):
                    for s in range(2):
                        pe.wait_ge(sem["og_l"], 2 * s + 2)
                        multiply(pe, M_O + O_OUT + 2 * i + q, s, R_O + RO_OUT + i,
                                 [(2 * q + c, slice(c * P, c * P + P), [(k, gH[:, 8 * s + k, :], gL[:, 8 * s + k, :]) for k in range(DC)])
                                  for c in range(2)], SEQ, start=s == 0, stop=s == 1)
            mlp2("omf", 4, M_O + O_UP, R_O + RO_UP)
            for j in range(2):
                for q in range(2):
                    b = 2 * j + q
                    pe.wait_ge(lin_read[3], R_ALL)
                    for c in range(4):
                        t = nc.tensor.transpose(lin[b][:, c * P:(c + 1) * P], hT[:, 4 * q + c, META + j * P:META + (j + 1) * P], ident)
                    t.then_inc(sem["turned_back"], 1)

        @block.scalar
        def _(act):
            own = Own(act, sem["act_own"])
            Exp, Ln, Copy, Square, Silu, Relu = ACT.Exp, ACT.Ln, ACT.Copy, ACT.Square, ACT.Silu, ACT.Relu
            f = nc.scalar.activation
            EXP_LN, SILU = "natural_log_exp_and_others", "silu_and_others"
            act.preload_act_table_set(EXP_LN)

            def square(pair):
                two = ds(2 * pair, 2)
                return f(sq8[:, two, :], hT[:, two, :], Square)

            for c in range(DC):
                act.wait_ge(sem["turned"], c + 1)
                f(hT[:, c, :], lin[c % 4][:, 0:T], Copy).then_inc(sem["h0"], 1)
            for l in range(2 * DEPTH):
                act.wait_ge(sem["turned"], DC + 1 + l)
                f(par[:, l, :], lin[l][:, 0:2 * P], Copy).then_inc(sem["h0"], 1)
            f(rates[:, :, 4:8], rates[:, :, 4:8], Exp).then_inc(sem["h0"], 1)
            for pair in range(DC // 2):
                act.wait_ge(sem["h0"], 2 * pair + 2)
                square(pair).then_inc(sem["sq"], 1)
            for s in range(2):
                split_hi(act, 0, s)

            def norm(l, which, name):
                act.wait_ge(*full(name, l))
                f(rs[:, :], bank(name)[:, 0:T], Ln, bias=eps_col, scale=1.0 / D).then_inc(emptied(name), 1)
                act.wait_ge(*read(name, l))
                f(rs[:, :], rs[:, :], Exp, scale=-0.5).then_inc(sem["rstd"], 1)
                for pair in range(DC // 2):
                    act.wait_ge(sem["n"], at("n", l, DC * (which - 1) + 2 * pair + 2))
                    f(nH[:, 2 * pair:2 * pair + 2, :], nT[:, 2 * pair:2 * pair + 2, :], Copy).then_inc(sem["nh"], 1)

            def layer(l):
                own.base, own.n = l * PER["act_own"], 0
                m0, r0 = l * M_LAYER, l * R_LAYER
                norm(l, 1, "ms1")
                act.preload_act_table_set(SILU)

                def w_in(i, to, func=Copy):
                    for s in range(2):
                        split_hi(act, m0 + i + 1, s)
                        act.wait_ge(sem["panel_done"], 2 * (m0 + i) + s + 3)
                        for c in range(2):
                            b = 2 * s + c
                            f(to(b), lin[b][:, 0:T].unsqueeze(1), func).then_inc(lin_read[b], 1)

                def group_silu(g):
                    act.wait_ge(sem["conv"], at("conv", l, 4 * g + 4))
                    qkv = cT[:, ds(4 * g, 4), :]
                    f(qkv, qkv, Silu).then_inc(sem["silu"], 1)

                def group_square(g):
                    act.wait_ge(sem["silu"], at("silu", l, g + 1))
                    f(sqh[:, ds(4 * g, 4), :], cT[:, ds(4 * g, 4), :], Square).then_inc(sem["sq_heads"], 1)

                w_in(0, lambda b: rawT[:, b:b + 1, :])
                for name, to in (("ik", ikr), ("bk", bkr)):
                    act.wait_ge(*full(name, l))
                    f(to[:, :], bank(name)[:, 0:T], Copy).then_inc(emptied(name), 1)
                act.wait_ge(*full("tk", l))
                n = S_ALL - S_BV
                for to, of, width in ((vtok, 0, P), (ab, S_AB - S_BV, 16)):
                    own.done(f(to[0:META, 0, :], bank("tk")[0:META, of:of + width], Copy))
                    t = f(to[:, 1:3, :], bank("tk")[:, n:3 * n].rearrange("p (b n) -> p b n", b=2)[:, :, of:of + width], Copy)
                t.then_inc(emptied("tk"), 1)
                with act.Fori(1, 3) as i:
                    w_in(i, lambda b: rawT[:, ds(4 * i + b, 1), :])
                    group_silu(i - 1)
                    group_square(i - 1)
                w_in(3, lambda b: zT[:, b:b + 1, :], Silu)
                group_silu(2)
                w_in(4, lambda b: rawT[:, 16 + b:17 + b, :])
                for b in range(4):
                    act.wait_ge(lin_read[b], r0 + 5)
                f(sq_att[:, 0:4, :], rawT[:, 16:20, :], Square)
                act.wait_ge(*read("bk", l))
                f(sq_att[:, 4, :], bkr[:, :], Square)
                f(sq_att[:, 5, :], ikr[:, :], Square).then_inc(sem["sq_att"], 1)
                w_in(5, lambda b: rawT[:, 20 + b:21 + b, :])
                act.preload_act_table_set(EXP_LN)
                act.wait_ge(sem["sp_in"], at("sp_in", l, 1))
                own.done(f(gl[:, :, :], gm[:, :, :], Exp))
                own.wait()
                f(gl[:, :, :], gl[:, :, :], Ln, bias=one_col)
                f(bt[:, :, :], ab[:, :, 4:8], Exp, scale=-1.0).then_inc(sem["sp_ln"], 1)
                for names, to, scale, bias_ in (
                    ([f"ssq{h}" for h in range(4)], rnq, 1.0, lnq_col),
                    ([f"ssk{h}" for h in range(4)], rnk, 1.0, 0.0),
                    ([f"sbq{h}" for h in range(4)] + ["sbk"], rnb, 1.0 / P, 0.0),
                ):
                    for h, name in enumerate(names):
                        act.wait_ge(*full(name, l))
                        f(to[:, h, :], bank(name)[:, 0:T], Ln, bias=eps_col, scale=scale).then_inc(emptied(name), 1)
                    act.wait_ge(*read(names[-1], l))
                    f(to[:, :, :], to[:, :, :], Exp, scale=-0.5, bias=bias_).then_inc(sem["rn"], 1)
                act.wait_ge(*full("sik", l))
                f(rni[:, :], bank("sik")[:, 0:T], Ln, bias=eps_col, scale=1.0 / P).then_inc(emptied("sik"), 1)
                act.wait_ge(*read("sik", l))
                f(rni[:, :], rni[:, :], Exp, scale=-0.5).then_inc(sem["rn"], 1)

                def gate_hi(i, slots=(0, 1)):
                    for s in slots:
                        split_hi(act, m0 + M_GATE + i + 1, s)

                def gate(i):
                    x = rawT[:, 4 * i:4 * i + 4, :]
                    for b in range(4):
                        act.wait_ge(lin_read[b], r0 + R_GATE + i + 1)
                    f(x, x, Exp, scale=-1.0).then_inc(sem["gates"], 1)
                    act.wait_ge(sem["gates"], at("gates", l, 3 * i + 1))
                    f(x, x, Ln, bias=one_col).then_inc(sem["gates"], 1)
                    act.wait_ge(sem["gates"], at("gates", l, 3 * i + 2))
                    f(x, x, Exp, scale=-1.0).then_inc(sem["gates"], 1)

                gate_hi(0)
                act.wait_ge(*full("gc", l))
                own.done(f(gcs[0:META, 0, :], bank("gc")[0:META, 0:4], Copy))
                f(gcs[:, 1:3, :], bank("gc")[:, 4:12].rearrange("p (b h) -> p b h", b=2), Copy).then_inc(emptied("gc"), 1)
                act.wait_ge(*read("gc", l))
                f(egt[:, :, :], gcs[:, :, :], Exp).then_inc(sem["eg"], 1)
                for b in range(3):
                    n = TB[b][1]
                    act.wait_ge(*full(f"gb{b}", l))
                    f(eg[:, :, tok(b)], bank(f"gb{b}")[:, 0:4 * n].rearrange("p (h c) -> p h c", h=4), Exp).then_inc(sem["eg"], 1)
                    act.wait_ge(*read(f"gb{b}", l))
                    f(decay[b], decay[b], Exp).then_inc(sem["dec"], 1)
                f(kdx[:, :, :], kdx[:, :, :], Exp).then_inc(sem["kdx"], 1)
                for b in range(3):
                    n = TB[b][1]
                    act.wait_ge(*full(f"vt{b}", l))
                    f(vt[0:n, b], bank(f"vt{b}")[0:n, :].rearrange("p (h d) -> p h d", h=4), Copy).then_inc(emptied(f"vt{b}"), 1)
                gate(0)
                gate_hi(1)
                for j in range(2):
                    for e in range(4):
                        name = f"ix{j}{e}"
                        act.wait_ge(*full(name, l))
                        if 4 * j + e >= 2:
                            act.wait_ge(sem["score"], at("score", l, 4 * j + e - 1))
                        f(rl[:, e % 2, :], bank(name)[:, :], Relu).then_inc(emptied(name), 1)
                with act.Fori(0, LEVELS) as it:
                    for b in range(3):
                        n = TB[b][1]
                        act.wait_ge(*full(f"Y{b}", l, it))
                        f(Y[b], bank(f"Y{b}")[0:n, 0:4 * n].rearrange("p (h c) -> p h c", h=4), Copy).then_inc(emptied(f"Y{b}"), 1)
                def new_values(b):
                    n = TB[b][1]
                    act.wait_ge(*full(f"vn{b}", l))
                    f(vn[0:n], bank(f"vn{b}")[0:n, :].rearrange("p (h d) -> p h d", h=4), Copy).then_inc(emptied(f"vn{b}"), 1)

                def delta_out(b):
                    act.wait_ge(sem["qe"], at("qe", l, 1))
                    act.wait_ge(*full(f"o{b}", l))
                    f(oA[:, :, tok(b)], bank(f"o{b}")[:, 0:4 * TB[b][1]].rearrange("p (h c) -> p h c", h=4), Copy).then_inc(emptied(f"o{b}"), 1)
                    act.wait_ge(*read(f"o{b}", l))
                    f(sqo[:, :, tok(b)], oA[:, :, tok(b)], Square).then_inc(sem["sqo"], 1)

                def softmax(j):
                    n = P if j else META
                    act.wait_ge(sem["nmx"], at("nmx", l, 1 + j))
                    for h in range(4):
                        src, to = (Pm[:, h, :], Pm[:, h, :]) if j else (bank("s0")[0:META, h * META:(h + 1) * META], P0[:, h, :])
                        e = f(to, src, Exp, scale=P ** -0.5, bias=nmx[0:n, j, h:h + 1], accum_out=sm[0:n, j, h:h + 1])
                    e.then_inc(sem["soft"] if j else emptied("s0"), 1)

                def weights_turned(j):
                    for b in range(3 if j else 1):
                        n, w = TB[b][1], 4 * TB[j][1]
                        name = f"pt{b}_{j}" if j else "pt0"
                        act.wait_ge(*full(name, l))
                        f(PT[0:n, b, 0:w], bank(name)[0:n, 0:w], Copy).then_inc(emptied(name), 1)

                def weighted_values(j):
                    act.wait_ge(*full(f"pv{j}", l))
                    f(oH[:, 4:8, tok(j)], bank(f"pv{j}")[:, 0:4 * TB[j][1]].rearrange("p (h c) -> p h c", h=4), Copy).then_inc(sem["ob_h"], 1)

                new_values(0)
                softmax(0)
                softmax(1)
                gate_hi(2, [0])
                delta_out(0)
                weights_turned(0)
                gate(1)
                gate_hi(2, [1])
                weighted_values(0)
                weights_turned(1)
                gate_hi(3, [0])
                new_values(1)
                softmax(2)
                delta_out(1)
                weighted_values(1)
                gate(2)
                weights_turned(2)
                new_values(2)
                weighted_values(2)
                delta_out(2)
                for h in range(4):
                    act.wait_ge(*full(f"so{h}", l))
                    f(rno[:, h, :], bank(f"so{h}")[:, 0:T], Ln, bias=eps_col, scale=1.0 / P).then_inc(emptied(f"so{h}"), 1)
                for h in range(4):
                    act.wait_ge(*read(f"so{h}", l))
                    f(rno[:, h, :], rno[:, h, :], Exp, scale=-0.5).then_inc(sem["rno"], 1)
                for h in range(4):
                    act.wait_ge(sem["oa"], at("oa", l, h + 1))
                    f(oH[:, h, :], zT[:, h, :], Copy).then_inc(sem["oa_h"], 1)
                gate_hi(3, [1])
                gate(3)
                with act.Fori(0, 2) as i:
                    for s in range(2):
                        split_hi(act, m0 + M_BRANCH + i + 1, s)
                        act.wait_ge(sem["y"], at("y", l, 4 * i + 2 * s + 2))
                        two = ds(4 * i + 2 * s, 2)
                        f(nH[:, two, :], yT[:, two, :], Copy).then_inc(sem["yh"], 1)
                with act.Fori(0, 2) as i:
                    for s in range(2):
                        split_hi(act, m0 + M_OUT + i + 1, s)
                        for c in range(2):
                            act.wait_ge(lin_read[2 * s + c], r0 + R_OUT + i + 1)
                        square(2 * i + s).then_inc(sem["sq"], 1)
                norm(l, 2, "ms2")
                act.preload_act_table_set(SILU)
                with act.Fori(0, 11) as i:
                    m, r = m0 + M_UP + i, r0 + R_UP + i
                    split_hi(act, m + 1, 0)
                    act.wait_ge(sem["panel_done"], 2 * m + 3)
                    for c in range(2):
                        f(u[:, c, :], lin[c][:, 0:T], Copy, scale=parL[:, ds(K_FCONV + 2 * FC + 2 * i + c, 1)]).then_inc(sem["tap"], 1)
                    split_hi(act, m + 1, 1)
                    for c in range(2):
                        act.wait_ge(lin_read[c], r + 1)
                        f(sg[:, c, :], u[:, c, :], Silu).then_inc(sem["gate_silu"], 1)
                    for c in range(2):
                        act.wait_ge(lin_read[2 + c], r + 1)
                        f(aH[:, ds(2 * i + c, 1), :], av[:, c, :].unsqueeze(1), Copy).then_inc(sem["ah"], 1)
                act.preload_act_table_set(EXP_LN)
                with act.Fori(0, 2) as i:
                    for p in range(6):
                        split_hi(act, m0 + M_DOWN + 3 * i + p // 2 + 1, p % 2)
                        if p % 3 == 2:
                            for c in range(2):
                                act.wait_ge(lin_read[2 * (p // 3) + c], r0 + R_DOWN + i + 1)
                            square(2 * i + p // 3).then_inc(sem["sq"], 1)
                assert own.n == PER["act_own"], own.n

            with act.Fori(0, DEPTH) as l:
                layer(l)

            L = DEPTH
            own.base, own.n = L * PER["act_own"], 0
            def square2(pair):
                two = ds(2 * pair, 2)
                f(sqf[:, two, :], hT[:, two, META:T], Square).then_inc(sem["sq2"], 1)

            def norm2(which, name):
                act.wait_ge(*full(name, L))
                f(rs[:, 0:SEQ], bank(name)[:, 0:SEQ], Ln, bias=eps_col, scale=1.0 / D).then_inc(emptied(name), 1)
                act.wait_ge(*read(name, L))
                f(rs[:, 0:SEQ], rs[:, 0:SEQ], Exp, scale=-0.5).then_inc(sem["rstd2"], 1)
                for pair in range(DC // 2):
                    act.wait_ge(sem["n2"], DC * (which - 1) + 2 * pair + 2)
                    two = slice(2 * pair, 2 * pair + 2)
                    f(nH[:, two, 0:SEQ], nT2[:, two, :], Copy).then_inc(sem["nh2"], 1)

            def take(m, s, to, func=Copy):
                split_hi(act, m + 1, s)
                act.wait_ge(sem["panel_done"], 2 * m + s + 3)
                for c in range(2):
                    f(to(c), lin[2 * s + c][:, 0:SEQ].unsqueeze(1), func).then_inc(lin_read[2 * s + c], 1)

            def mlp2(j, m, r, last):
                which = 2 * j + 2
                norm2(which, ("emf", "omf")[j])
                t2 = (KE_T2, KO_T2)[j]
                act.preload_act_table_set(SILU)

                def rounded(i):
                    for c in range(2):
                        act.wait_ge(sem["conv2"], j * FC + 2 * i + c + 1)
                        f(aH2[:, ds(2 * i + c, 1), :], av2[:, c, :].unsqueeze(1), Copy).then_inc(sem["ah2"], 1)

                def up(i, first):
                    for s in range(2):
                        split_hi(act, m + i + 1, s)
                        act.wait_ge(sem["panel_done"], 2 * (m + i) + s + 3)
                        if s == 0 and not first:
                            act.wait_ge(sem["silu2"], j * FC + 2 * i)
                        for c in range(2):
                            f(u2[:, 2 * s + c, :], lin[2 * s + c][:, 0:SEQ], Copy,
                              scale=par[:, DEPTH + j, ds(t2 + s * FC + 2 * i + c, 1)]).then_inc(sem["tap2"], 1)
                        if s == 0 and not first:
                            rounded(i - 1)
                    for c in range(2):
                        act.wait_ge(lin_read[c], r + i + 1)
                        f(sg2[:, c, :], u2[:, c, :], Silu).then_inc(sem["silu2"], 1)

                up(0, True)
                with act.Fori(1, 11) as i:
                    up(i, False)
                rounded(10)
                act.preload_act_table_set(EXP_LN)
                if last:
                    for p in range(10):
                        split_hi(act, m + 11 + p // 2 + 1, p % 2)
                else:
                    with act.Fori(0, 2) as i:
                        for p in range(6):
                            split_hi(act, m + 11 + 3 * i + p // 2 + 1, p % 2)
                            if p % 3 == 2:
                                for c in range(2):
                                    act.wait_ge(lin_read[2 * (p // 3) + c], r + 11 + i + 1)
                                square2(2 * i + p // 3)

            norm2(1, "ems")
            for i in range(2):
                for s in range(2):
                    take(M_E + i, s, lambda c: raw8[:, 4 * i + 2 * s + c, :].unsqueeze(1))
                for b in range(4):
                    act.wait_ge(lin_read[b], R_E + i + 1)
                f(sqe[:, 4 * i:4 * i + 4, :], raw8[:, 4 * i:4 * i + 4, :], Square).then_inc(sem["esq"], 1)
            take(M_E + 2, 0, lambda c: ght[:, c, :].unsqueeze(1))
            for c in range(4):
                act.wait_ge(*full(f"eq{c}", L))
                f(rne[:, 2 * c:2 * c + 2, :], bank(f"eq{c}")[:, :].rearrange("p (c t) -> p c t", c=2), Ln, bias=eps_col, scale=1.0 / 64).then_inc(emptied(f"eq{c}"), 1)
            for n in range(2):
                act.wait_ge(*read(f"eq{2 * n}", L))
                act.wait_ge(*read(f"eq{2 * n + 1}", L))
                f(rne[:, 4 * n:4 * n + 4, :], rne[:, 4 * n:4 * n + 4, :], Exp, scale=-0.5).then_inc(sem["ern"], 1)
            take(M_E + 2, 1, lambda c: ght[:, 2 + c, :].unsqueeze(1))

            def even_exp(j):
                x = Pe if j else Pe0
                act.wait_ge(sem["enmx"], 1 + j)
                for h in range(8):
                    e = f(x[:, h, :], x[:, h, :], Exp, scale=0.125, bias=nmx8[:, j, h:h + 1])
                e.then_inc(sem["esoft"], 1)

            def even_turned(j):
                for g in range(2):
                    for b in range(j + 1):
                        name = f"et{j}{g}" + (str(b) if j else "")
                        act.wait_ge(*full(name, L))
                        f(PTe[:, b, g * 512:(g + 1) * 512], bank(name)[:, :], Copy).then_inc(emptied(name), 1)

            def even_values(j):
                act.wait_ge(*full(f"ev{j}", L))
                f(eH[:, 0:4, j * P:j * P + P], bank(f"ev{j}")[:, :].rearrange("p (c t) -> p c t", c=4), Copy).then_inc(sem["eob_h"], 1)

            split_hi(act, M_E + 4, 0)
            even_exp(0)
            even_exp(1)
            split_hi(act, M_E + 4, 1)
            even_turned(0)
            for s in range(2):
                take(M_E + 4, s, lambda c: vtk[:, c:c + 1, s * PANEL:(s + 1) * PANEL])
            even_values(0)
            even_turned(1)
            split_hi(act, M_E + 6, 0)
            even_values(1)
            split_hi(act, M_E + 6, 1)
            for s in range(2):
                for c in range(2):
                    act.wait_ge(lin_read[2 * s + c], R_E + 6)
                f(eH[:, 4 + 2 * s:6 + 2 * s, :], cvt[:, 2 * s:2 * s + 2, :], Copy).then_inc(sem["eb_h"], 1)
            with act.Fori(0, 2) as i:
                for s in range(2):
                    split_hi(act, M_E + E_OUT + i + 1, s)
                    for c in range(2):
                        act.wait_ge(lin_read[2 * s + c], R_E + E_OUT + i + 1)
                    square2(2 * i + s)
            mlp2(0, M_E + E_UP, R_E + E_UP, False)

            norm2(3, "oms")
            with act.Fori(0, 2) as i:
                for s in range(2):
                    take(M_O + i, s, lambda c: qk2[:, 0, ds(2 * i + s, 1), c, :])
            with act.Fori(0, 2) as i:
                for s in range(2):
                    take(M_O + O_K + i, s, lambda c: qk2[:, 1, ds(2 * i + s, 1), c, :])
            with act.Fori(0, 4) as i:
                for s in range(2):
                    take(M_O + O_V + i, s, lambda c: vtk2[:, c:c + 1, ds(i * 512 + s * PANEL, PANEL)])
            def odd_g(i, s):
                take(M_O + O_G + i, s, lambda c: sgT[:, 4 * i + 2 * s + c, :].unsqueeze(1), Silu)

            def odd_out(h):
                act.wait_ge(sem["ogate"], h + 1)
                f(gH[:, 4 * h:4 * h + 4, :], oR[:, 4 * h:4 * h + 4, :], Copy).then_inc(sem["og_h"], 1)

            act.preload_act_table_set(SILU)
            odd_g(0, 0)
            for h in range(4):
                for e in range(2):
                    name = f"oo{h}{e}"
                    act.wait_ge(*full(name, L))
                    f(oR[:, 4 * h + 2 * e:4 * h + 2 * e + 2, :], bank(name)[:, :].rearrange("p (c t) -> p c t", c=2), Copy).then_inc(emptied(name), 1)
            odd_g(0, 1)
            odd_g(1, 0)
            for h in range(4):
                act.wait_ge(*read(f"om{h}", L))
                f(sq16[:, 4 * h:4 * h + 4, :], oR[:, 4 * h:4 * h + 4, :], Square).then_inc(sem["osq"], 1)
            odd_g(1, 1)
            odd_g(2, 0)
            act.preload_act_table_set(EXP_LN)
            for h in range(4):
                act.wait_ge(*full(f"ow{h}", L))
                f(rn4[:, h, :], bank(f"ow{h}")[:, 0:SEQ], Ln, bias=eps_col, scale=1.0 / 512).then_inc(emptied(f"ow{h}"), 1)
            for h in range(4):
                act.wait_ge(*read(f"ow{h}", L))
                f(rn4[:, h, :], rn4[:, h, :], Exp, scale=-0.5).then_inc(sem["ovar"], 1)
            act.preload_act_table_set(SILU)
            odd_g(2, 1)
            odd_out(0)
            odd_out(1)
            odd_g(3, 0)
            odd_out(2)
            odd_g(3, 1)
            odd_out(3)
            act.preload_act_table_set(EXP_LN)
            with act.Fori(0, 2) as i:
                for q in range(2):
                    for s in range(2):
                        split_hi(act, M_O + O_OUT + 2 * i + q + 1, s)
                    for c in range(2):
                        act.wait_ge(lin_read[2 * q + c], R_O + RO_OUT + i + 1)
                    square2(2 * i + q)
            mlp2(1, M_O + O_UP, R_O + RO_UP, True)
            for b in range(4):
                act.wait_ge(sem["turned_back"], b + 1)
                f(outT[:, b // 2, (b % 2) * 512:(b % 2) * 512 + 512], lin[b][:, :], Copy).then_inc(sem["out_ready"], 1)

        @block.vector
        def _(dve):
            own = Own(dve, sem["dve_own"])
            v = nc.vector
            dve.sem_inc(sem["wlo"], 4)
            v.memset(rows[:, :, :, :], 0.0).then_inc(sem["cleared"], 1)
            for x in (ab, gcs, kdx):
                v.memset(x[:, 0:1, :], 0.0)
            v.memset(bias[:, :, 0:META], 0.0).then_inc(sem["cleared"], 1)
            dve.wait_ge(sem["h0"], DC + 2 * DEPTH + 1)
            v.tensor_scalar(rates[:, :, 4:8], rates[:, :, 4:8], -1.0, None, ALU.mult).then_inc(sem["cleared"], 1)
            dve.wait_ge(sem["cleared"], 3)
            dve.wait_ge(sem["tables_in"], 16)
            for s in range(2):
                split_lo(dve, 0, s)

            def norm(l, which, gain):
                dve.wait_ge(sem["rstd"], at("rstd", l, which))
                for c in range(DC):
                    v.scalar_tensor_tensor(nT[:, c, :], hT[:, c, :], pc(gain + c), rs[:, :], ALU.mult, ALU.mult).then_inc(sem["n"], 1)
                for pair in range(DC // 2):
                    dve.wait_ge(sem["nh"], at("nh", l, 4 * (which - 1) + pair + 1))
                    gs = slice(2 * pair, 2 * pair + 2)
                    v.tensor_tensor(nL[:, gs, :], nT[:, gs, :], nH[:, gs, :].bitcast(F32), ALU.subtract).then_inc(sem["nl"], 1)

            def layer(l):
                own.base, own.n = l * PER["dve_own"], 0
                m0, r0 = l * M_LAYER, l * R_LAYER
                own.done(v.tensor_copy(parL[:, 0:2 * P].unsqueeze(1), par[:, ds(l, 1), :]))
                own.done(v.tensor_copy(parL[:, K_DT:K_DT + 8].unsqueeze(1), rates[:, ds(l, 1), :]))
                own.wait()
                norm(l, 1, K_NORM1)
                start = own.n
                with dve.Fori(0, 3) as i:
                    own.base, own.n = l * PER["dve_own"] + i * 12, start
                    for s in range(2):
                        split_lo(dve, m0 + i + 1, s)
                    for tap in range(4):
                        for c in range(4):
                            raw, acc = rawT[:, ds(4 * i + c, 1), :], cT[:, ds(4 * i + c, 1), :]
                            w = parL[:, ds(K_CONV + (3 - tap) * 12 + 4 * i + c, 1)]
                            if tap == 0:
                                dve.wait_ge(lin_read[c], r0 + i + 1)
                                own.done(v.tensor_scalar(acc, raw, w, None, ALU.mult))
                                continue
                            own.wait(own.n - 3 if tap < 3 else start + 9 + c)
                            ins = v.scalar_tensor_tensor(acc[:, :, tap:T], raw[:, :, 0:T - tap], w, acc[:, :, tap:T], ALU.mult, ALU.add)
                            if tap < 3:
                                own.done(ins)
                            else:
                                ins.then_inc(sem["conv"], 1)
                own.base, own.n = l * PER["dve_own"], start + 36
                with dve.Fori(3, 5) as i:
                    for s in range(2):
                        split_lo(dve, m0 + i + 1, s)
                dve.wait_ge(*read("tk", l))
                own.done(v.tensor_tensor(gx[:, :, :], ab[:, :, 0:4], bf(pc(K_DT, 4), 1, [P, 3, 4]), ALU.add))
                own.wait()
                v.scalar_tensor_tensor(gm[:, :, :], gx[:, :, :], -1.0, gx[:, :, :], ALU.mult, ALU.min).then_inc(sem["sp_in"], 1)
                own.done(v.tensor_scalar(iw[:, :, :], ab[:, :, 8:16], IDX_HEADS ** -0.5 * IDX_DIM ** -0.5, None, ALU.mult))
                dve.wait_ge(sem["sp_ln"], at("sp_ln", l, 1))
                own.done(v.scalar_tensor_tensor(gm[:, :, :], gx[:, :, :], 0.0, gl[:, :, :], ALU.max, ALU.add))
                own.wait()
                v.tensor_tensor(gg[:, :, :], gm[:, :, :], bf(pc(K_NA, 4), 1, [P, 3, 4]), ALU.mult).then_inc(sem["gt"], 1)
                own.done(v.tensor_scalar(bt[:, :, :], bt[:, :, :], 1.0, None, ALU.add))
                own.wait()
                own.done(v.reciprocal(beta[:, :, :], bt[:, :, :]))
                dve.wait_ge(sem["rn"], at("rn", l, 1))
                v.tensor_tensor(cT[:, 0:4, :], cT[:, 0:4, :], rnq[:, :, :], ALU.mult).then_inc(sem["qk_unit"], 1)
                dve.wait_ge(sem["rn"], at("rn", l, 2))
                v.tensor_tensor(cT[:, 4:8, :], cT[:, 4:8, :], rnk[:, :, :], ALU.mult).then_inc(sem["qk_unit"], 1)
                dve.wait_ge(sem["gt"], at("gt", l, 1))
                own.wait()
                for src, spread in ((gg, gtri), (beta, bdiag)):
                    for b in range(3):
                        n = TB[b][1]
                        mask = const("upto", n, n) if src is gg else ident[0:n, 0:n]
                        v.tensor_tensor(spread[b], bf(mask, 1, [n, 4, n]), bf(src[0:n, b, :], 2, [n, 4, n]), ALU.mult).then_inc(sem["gt"], 1)
                dve.wait_ge(sem["rn"], at("rn", l, 4))
                v.scalar_tensor_tensor(rawT[:, 16:20, :], rawT[:, 16:20, :], pc(K_QN), rnb[:, 0:4, :], ALU.mult, ALU.mult).then_inc(sem["att_unit"], 1)
                v.scalar_tensor_tensor(bkr[:, :], bkr[:, :], pc(K_KN), rnb[:, 4, :], ALU.mult, ALU.mult).then_inc(sem["att_unit"], 1)
                v.scalar_tensor_tensor(ikr[:, :], ikr[:, :], pc(K_IN), rni[:, :], ALU.mult, ALU.mult).then_inc(sem["att_unit"], 1)

                def gate_lo(i, slots=(0, 1)):
                    for s in slots:
                        dve.wait_ge(sem["panel_done"], 2 * (m0 + M_GATE + i) + s + 3)
                        for c in range(2):
                            b = 2 * s + c
                            v.tensor_scalar(rawT[:, 4 * i + b, :], lin[b][:, 0:T], pc(K_BG + 4 * i + b), GATE_LEAST, ALU.add, ALU.max).then_inc(lin_read[b], 1)

                dve.wait_ge(sem["conv"], at("conv", l, 12))
                gate_lo(0)
                dve.wait_ge(sem["eg"], at("eg", l, 1))
                own.done(v.tensor_scalar(egt[:, :, :], egt[:, :, :], -1.0, None, ALU.mult))
                dve.wait_ge(*read("gc", l))
                for b in range(3):
                    n = TB[b][1]
                    ps = bank(f"gb{b}")
                    dve.wait_ge(*full(f"gb{b}", l))
                    dve.wait_ge(sem["eg"], at("eg", l, 2 + b))
                    for h in range(4):
                        v.tensor_scalar(decay[b][:, h, :], ps[0:n, h * n:(h + 1) * n], gcs[0:n, b, h:h + 1], 0.0, ALU.subtract, ALU.min)
                    v.tensor_tensor(kdx[0:n, b, :], ps[0:n, n - 1:4 * n:n], gcs[0:n, b, :], ALU.subtract).then_inc(emptied(f"gb{b}"), 1)
                    dve.wait_ge(sem["dec"], at("dec", l, b + 1))
                    own.done(v.tensor_tensor(decay[b], decay[b], bf(const("upto", n, n), 1, [n, 4, n]), ALU.mult))
                    own.wait()
                    dve.wait_ge(*full(f"bb{b}", l))
                    v.tensor_tensor(MT[b], bank(f"bb{b}")[0:n, 0:4 * n].rearrange("p (h c) -> p h c", h=4), decay[b], ALU.mult).then_inc(emptied(f"bb{b}"), 1)
                for b in range(3):
                    n = TB[b][1]
                    dve.wait_ge(*full(f"kk{b}", l))
                    dve.wait_ge(*read(f"bb{b}", l))
                    v.tensor_tensor(MT[b], bank(f"kk{b}")[0:n, 0:4 * n].rearrange("p (h c) -> p h c", h=4), MT[b], ALU.mult).then_inc(emptied(f"kk{b}"), 1)
                    dve.wait_ge(*full(f"qk{b}", l))
                    v.tensor_tensor(QD[b], bank(f"qk{b}")[0:n, 0:4 * n].rearrange("p (h c) -> p h c", h=4), decay[b], ALU.mult).then_inc(emptied(f"qk{b}"), 1)
                for b in range(3):
                    own.done(v.tensor_copy(sdec[:, b, :], eg[:, :, TB[b][0] + TB[b][1] - 1]))
                v.tensor_tensor(cT[:, 0:4, :], cT[:, 0:4, :], eg[:, :, :], ALU.mult).then_inc(sem["qe"], 1)
                dve.wait_ge(sem["kdx"], at("kdx", l, 1))
                for b in range(3):
                    n = TB[b][1]
                    dve.wait_ge(*full(f"kt{b}", l))
                    v.tensor_tensor(kd[0:n, b], bank(f"kt{b}")[0:n, :].rearrange("p (h d) -> p h d", h=4), bf(kdx[0:n, b, :], 2, [n, 4, P]), ALU.mult).then_inc(emptied(f"kt{b}"), 1)
                for n, (names, kind, x) in enumerate((
                    ([f"rq{h}" for h in range(4)], "a", rawT[:, 16:20, :]), ([f"ri{c}" for c in range(4)], "i", rawT[:, 20:24, :]),
                    (["rk"], "a", bkr[:, :].unsqueeze(1)), (["rik"], "i", ikr[:, :].unsqueeze(1)),
                )):
                    if n:
                        dve.wait_ge(sem["rope"], at("rope", l, n))
                    for c, name in enumerate(names):
                        dve.wait_ge(*full(name, l))
                        v.tensor_tensor(tmp4[:, c, :], bank(name)[:, 0:T], const("sin_" + kind, T), ALU.mult).then_inc(emptied(name), 1)
                    own.done(v.tensor_tensor(x, x, bf(const("cos_" + kind, T), 1, [P, len(names), T]), ALU.mult))
                    own.wait()
                    dve.wait_ge(*read(names[-1], l))
                    v.tensor_tensor(x, x, tmp4[:, 0:len(names), :], ALU.add).then_inc(sem["rope"], 1)
                def masked(b, it):
                    n = TB[b][1]
                    level = c1[0:n, ds(consts_at1["level0"] + it * P, n)]
                    v.tensor_tensor(ML[b], MT[b], bf(level, 1, [n, 4, n]), ALU.mult).then_inc(sem["ml"], 1)

                for b in range(3):
                    n = TB[b][1]
                    for m in (X, A):
                        own.done(v.tensor_copy(m[b], bf(ident[0:n, 0:n], 1, [n, 4, n])))
                for b in range(3):
                    masked(b, 0)
                gate_lo(1)
                for j in range(2):
                    for e in range(4):
                        dve.wait_ge(*read(f"ix{j}{e}", l))
                        for n in range(2):
                            h = 4 * (e // 2) + e % 2 + 2 * n
                            r, w = rl[:, e % 2, n * SEQ:(n + 1) * SEQ], iw[:, j + 1, h:h + 1]
                            if e + n == 0:
                                ins = v.tensor_scalar(score[:, j, :], r, w, None, ALU.mult)
                            else:
                                if n == 0:
                                    dve.wait_ge(sem["score"], at("score", l, 4 * j + e))
                                else:
                                    own.wait()
                                ins = v.scalar_tensor_tensor(score[:, j, :], r, w, score[:, j, :], ALU.mult, ALU.add)
                            if n == 0:
                                own.done(ins)
                            else:
                                ins.then_inc(sem["score"], 1)
                    dve.wait_ge(sem["score"], at("score", l, 4 * j + 4))
                    own.done(v.tensor_tensor(work[:, j, :], score[:, j, :], c1[:, consts_at1["barred"] + j * SEQ:consts_at1["barred"] + (j + 1) * SEQ], ALU.add))

                def take_eight(before):
                    n0 = own.n
                    for j in range(2):
                        own.wait(before + j)
                        stand(dve, "dve_stood")
                        own.done(v.max(m8[:, j, :], work[:, j, :]))
                    for j in range(2):
                        own.wait(n0 + 1 + j)
                        stand(dve, "dve_stood")
                        own.done(v.match_replace(work[:, j, :], m8[:, j, :], work[:, j, :], TAKEN))

                start = own.n

                def level(it, last):
                    take_eight(start - 1)
                    for b in range(3):
                        if not last:
                            dve.wait_ge(*full(f"Y{b}", l, it))
                            masked(b, it + 1)
                    dve.wait_ge(*full("XA0", l, it))
                    v.tensor_tensor(X[0], X[0], bank("XA0")[0:META, 0:4 * META].rearrange("p (h c) -> p h c", h=4), ALU.subtract)
                    v.tensor_tensor(A[0], A[0], bank("XA0")[0:META, 4 * META:8 * META].rearrange("p (h c) -> p h c", h=4), ALU.subtract).then_inc(emptied("XA0"), 1)
                    for b in (1, 2):
                        for name, m in ((f"X{b}", X), (f"A{b}", A)):
                            if name[0] == "X":
                                dve.wait_ge(*full(f"A{b}", l, it))
                            v.tensor_tensor(m[b], m[b], bank(name)[:, :].rearrange("p (h c) -> p h c", h=4), ALU.subtract).then_inc(emptied(name), 1)

                with dve.Fori(0, LEVELS - 1) as it:
                    own.base, own.n = l * PER["dve_own"] + 4 * it, start
                    level(it, False)
                own.base, own.n = l * PER["dve_own"] + 4 * (LEVELS - 1), start
                level(LEVELS - 1, True)
                own.base, own.n = l * PER["dve_own"], start + 4 * LEVELS
                for b, name in enumerate(("XA0", "A1", "A2")):
                    n = TB[b][1]
                    dve.wait_ge(*read(name, l, LEVELS - 1))
                    v.tensor_tensor(A[b], A[b], bf(beta[0:n, b, :], 2, [n, 4, n]), ALU.mult).then_inc(sem["ab_ready"], 1)
                take_eight(own.n - 1)
                own.wait()
                own.done(v.tensor_scalar(bias[:, :, META:T], work[:, :, :], 0.5 * (INVALID + TAKEN), -BIG, ALU.is_gt, ALU.mult))

                def greatest(j):
                    n = P if j else META
                    if j:
                        own.wait()
                        for h in range(4):
                            name = f"s{'abcd'[h]}{j}"
                            dve.wait_ge(*full(name, l))
                            v.tensor_tensor(Pm[:, h, :], bank(name)[:, 0:T], bias[:, j - 1, :], ALU.add).then_inc(emptied(name), 1)
                        dve.wait_ge(*read(f"sd{j}", l))
                        own.done(v.tensor_reduce(mx[:, j, :], Pm[:, :, :], AX, ALU.max))
                    else:
                        dve.wait_ge(*full("s0", l))
                        own.done(v.tensor_reduce(mx[0:META, 0, :], bank("s0")[0:META, 0:4 * META].rearrange("p (h k) -> p h k", h=4), AX, ALU.max))
                    own.wait()
                    v.tensor_scalar(nmx[0:n, j, :], mx[0:n, j, :], -(P ** -0.5), None, ALU.mult).then_inc(sem["nmx"], 1)

                def normed(j):
                    n, x = (P, Pm[:, :, :]) if j else (META, P0[:, :, :])
                    if j:
                        dve.wait_ge(sem["soft"], at("soft", l, j))
                    else:
                        dve.wait_ge(*read("s0", l))
                    own.done(v.reciprocal(rsm[0:n, j, :], sm[0:n, j, :]))
                    own.wait()
                    v.tensor_tensor(x, x, bf(rsm[0:n, j, :], 2, [n, 4, T if j else META]), ALU.mult).then_inc(sem["pn"], 1)

                def out_lo(j):
                    dve.wait_ge(sem["ob_h"], at("ob_h", l, 1 + j))
                    v.tensor_tensor(oL[:, 4:8, tok(j)], bank(f"pv{j}")[:, 0:4 * TB[j][1]].rearrange("p (h c) -> p h c", h=4),
                                    oH[:, 4:8, tok(j)].bitcast(F32), ALU.subtract).then_inc(emptied(f"pv{j}"), 1)

                def state(b):
                    ps = bank(f"dS{b}")
                    dve.wait_ge(*full(f"dS{b}", l))
                    if b == 0:
                        v.tensor_copy(S[:, :, :], ps[:, :].rearrange("p (h d) -> p h d", h=4)).then_inc(emptied("dS0"), 1)
                        return
                    for h in range(4):
                        ins = v.scalar_tensor_tensor(S[:, h, :], S[:, h, :], sdec[:, b, h:h + 1], ps[:, h * P:(h + 1) * P], ALU.mult, ALU.add)
                    ins.then_inc(emptied(f"dS{b}"), 1)

                def unseen_values(b):
                    ps = bank(f"kS{b}")
                    dve.wait_ge(*full(f"kS{b}", l))
                    for h in range(4):
                        ins = v.scalar_tensor_tensor(R[:, h, :], ps[:, h * P:(h + 1) * P], egt[:, b, h:h + 1], vt[:, b, h, :], ALU.mult, ALU.add)
                    ins.then_inc(emptied(f"kS{b}"), 1)

                def gated(b):
                    dve.wait_ge(*read(f"o{b}", l))
                    own.done(v.scalar_tensor_tensor(zT[:, :, tok(b)], oA[:, :, tok(b)], pc(K_ANORM), zT[:, :, tok(b)], ALU.mult, ALU.mult))

                dve.wait_ge(lin_read[3], r0 + 4)
                greatest(0)
                greatest(1)
                normed(0)
                normed(1)
                gate_lo(2, [0])
                state(0)
                gate_lo(2, [1])
                unseen_values(1)
                out_lo(0)
                gate_lo(3, [0])
                greatest(2)
                gated(0)
                state(1)
                normed(2)
                out_lo(1)
                gated(1)
                unseen_values(2)
                out_lo(2)
                gated(2)
                own.wait()
                for h in range(4):
                    dve.wait_ge(sem["rno"], at("rno", l, h + 1))
                    v.tensor_tensor(zT[:, h, :], zT[:, h, :], rno[:, h, :], ALU.mult).then_inc(sem["oa"], 1)
                for h in range(4):
                    dve.wait_ge(sem["oa_h"], at("oa_h", l, h + 1))
                    v.tensor_tensor(oL[:, h, :], zT[:, h, :], oH[:, h, :].bitcast(F32), ALU.subtract).then_inc(sem["oa_l"], 1)
                gate_lo(3, [1])
                dve.wait_ge(sem["wlo"], 4 * (m0 + M_BRANCH) + 4)
                for s in range(2):
                    split_lo(dve, m0 + M_BRANCH, s)
                dve.wait_ge(sem["gates"], at("gates", l, 12))
                stand(dve, "dve_stood")
                with dve.Fori(0, 2) as i:
                    for s in range(2):
                        dve.wait_ge(sem["panel_done"], 2 * (m0 + M_BRANCH + i) + s + 3)
                        banks = [bank(f"br{b}") if s else lin[b] for b in range(4)]
                        free = [emptied(f"br{b}") if s else lin_read[b] for b in range(4)]
                        for c in range(2):
                            q = 4 * i + 2 * s + c
                            v.tensor_tensor(yT[:, ds(q, 1), :], banks[c][:, 0:T].unsqueeze(1), rawT[:, ds(q, 1), :], ALU.mult).then_inc(free[c], 1)
                            v.tensor_tensor(ytmp[:, c, :].unsqueeze(1), banks[2 + c][:, 0:T].unsqueeze(1), rawT[:, ds(8 + q, 1), :], ALU.mult).then_inc(free[2 + c], 1)
                        for c in range(2):
                            q = 4 * i + 2 * s + c
                            dve.wait_ge(*(read(f"br{2 + c}", l, i) if s else (lin_read[2 + c], r0 + R_BRANCH + i + 1)))
                            v.tensor_tensor(yT[:, ds(q, 1), :], yT[:, ds(q, 1), :], ytmp[:, c, :].unsqueeze(1), ALU.add).then_inc(sem["y"], 1)
                        split_lo(dve, m0 + M_BRANCH + i + 1, s)
                        two = ds(4 * i + 2 * s, 2)
                        dve.wait_ge(sem["yh"], at("yh", l, 2 * i + s + 1))
                        v.tensor_tensor(nL[:, two, :], yT[:, two, :], nH[:, two, :].bitcast(F32), ALU.subtract).then_inc(sem["yl"], 1)
                with dve.Fori(0, 2) as i:
                    for s in range(2):
                        dve.wait_ge(sem["panel_done"], 2 * (m0 + M_OUT + i) + s + 3)
                        for c in range(2):
                            x = hT[:, ds(4 * i + 2 * s + c, 1), :]
                            v.tensor_tensor(x, x, lin[2 * s + c][:, 0:T].unsqueeze(1), ALU.add).then_inc(lin_read[2 * s + c], 1)
                        split_lo(dve, m0 + M_OUT + i + 1, s)
                norm(l, 2, K_NORM2)
                with dve.Fori(0, 11) as i:
                    m, r = m0 + M_UP + i, r0 + R_UP + i
                    own.base = l * PER["dve_own"] + i * 2
                    n0 = own.n
                    for c in range(2):
                        dve.wait_ge(sem["tap"], at("tap", l, 2 * i + c + 1))
                        own.done(v.scalar_tensor_tensor(u[:, c, 1:T], lin[c][:, 0:T - 1], parL[:, ds(K_FCONV + FC + 2 * i + c, 1)], u[:, c, 1:T], ALU.mult, ALU.add))
                    for c in range(2):
                        own.wait(n0 + c + 1)
                        v.scalar_tensor_tensor(u[:, c, 2:T], lin[c][:, 0:T - 2], parL[:, ds(K_FCONV + 2 * i + c, 1)], u[:, c, 2:T], ALU.mult, ALU.add).then_inc(lin_read[c], 1)
                    split_lo(dve, m + 1, 0)
                    dve.wait_ge(sem["panel_done"], 2 * m + 4)
                    for c in range(2):
                        dve.wait_ge(sem["gate_silu"], at("gate_silu", l, 2 * i + c + 1))
                        v.tensor_tensor(av[:, c, :], lin[2 + c][:, 0:T], sg[:, c, :], ALU.mult).then_inc(lin_read[2 + c], 1)
                    split_lo(dve, m + 1, 1)
                    for c in range(2):
                        dve.wait_ge(sem["ah"], at("ah", l, 2 * i + c + 1))
                        q = ds(2 * i + c, 1)
                        v.tensor_tensor(aL[:, q, :], av[:, c, :].unsqueeze(1), aH[:, q, :].bitcast(F32), ALU.subtract).then_inc(sem["al"], 1)
                own.base, own.n = l * PER["dve_own"], n0 + 22
                with dve.Fori(0, 2) as i:
                    for p in range(6):
                        m = m0 + M_DOWN + 3 * i + p // 2
                        if p % 3 == 2:
                            dve.wait_ge(sem["panel_done"], 2 * m + p % 2 + 3)
                            for c in range(2):
                                b = 2 * (p // 3) + c
                                x = hT[:, ds(4 * i + b, 1), :]
                                v.tensor_tensor(x, x, lin[b][:, 0:T].unsqueeze(1), ALU.add).then_inc(lin_read[b], 1)
                        split_lo(dve, m + 1, p % 2)
                assert own.n == PER["dve_own"], own.n

            with dve.Fori(0, DEPTH) as l:
                layer(l)

            L = DEPTH
            own.base, own.n = L * PER["dve_own"], 0
            h2 = hT[:, :, META:T]

            def norm2(which, gains):
                dve.wait_ge(sem["rstd2"], which)
                for c in range(DC):
                    v.scalar_tensor_tensor(nT2[:, c, :], h2[:, c, :], gains(c), rs[:, 0:SEQ], ALU.mult, ALU.mult).then_inc(sem["n2"], 1)
                for pair in range(DC // 2):
                    dve.wait_ge(sem["nh2"], 4 * (which - 1) + pair + 1)
                    gs = slice(2 * pair, 2 * pair + 2)
                    v.tensor_tensor(nL[:, gs, 0:SEQ], nT2[:, gs, :], nH[:, gs, 0:SEQ].bitcast(F32), ALU.subtract).then_inc(sem["nl2"], 1)

            def los(m, pairs):
                with dve.Fori(0, pairs) as i:
                    for s in range(2):
                        split_lo(dve, m + i + 1, s)

            def add_h(chunk, b):
                x = hT[:, ds(chunk, 1), META:T]
                v.tensor_tensor(x, x, lin[b][:, 0:SEQ].unsqueeze(1), ALU.add).then_inc(lin_read[b], 1)

            def mlp2(j, m, r, last):
                norm2(2 * j + 2, lambda c: p2(j, (KE_FN, KO_FN)[j] + c))
                n0 = own.n

                def left(i):
                    for c in range(2):
                        dve.wait_ge(sem["ah2"], j * FC + 2 * i + c + 1)
                        q = ds(2 * i + c, 1)
                        v.tensor_tensor(aL2[:, q, :], av2[:, c, :].unsqueeze(1), aH2[:, q, :].bitcast(F32), ALU.subtract).then_inc(sem["al2"], 1)

                def up(i, first):
                    own.base, own.n = L * PER["dve_own"] + i * 4, n0
                    for s in range(2):
                        for c in range(2):
                            q = 2 * s + c
                            w = par[:, DEPTH + j, ds(P + 2 * FC + s * FC + 2 * i + c, 1)]
                            dve.wait_ge(sem["tap2"], j * 2 * FC + 4 * i + q + 1)
                            own.done(v.scalar_tensor_tensor(u2[:, q, 1:SEQ], lin[q][:, 0:SEQ - 1], w, u2[:, q, 1:SEQ], ALU.mult, ALU.add))
                        for c in range(2):
                            q = 2 * s + c
                            w = par[:, DEPTH + j, ds(P + s * FC + 2 * i + c, 1)]
                            own.wait(n0 + q + 1)
                            v.scalar_tensor_tensor(u2[:, q, 2:SEQ], lin[q][:, 0:SEQ - 2], w, u2[:, q, 2:SEQ], ALU.mult, ALU.add).then_inc(lin_read[q], 1)
                        split_lo(dve, m + i + 1, s)
                        if s == 0 and not first:
                            left(i - 1)
                    for c in range(2):
                        dve.wait_ge(sem["silu2"], j * FC + 2 * i + c + 1)
                        dve.wait_ge(lin_read[2 + c], r + i + 1)
                        if not first:
                            dve.wait_ge(sem["al2"], j * FC + 2 * i)
                        v.tensor_tensor(av2[:, c, :], u2[:, 2 + c, :], sg2[:, c, :], ALU.mult).then_inc(sem["conv2"], 1)

                up(0, True)
                with dve.Fori(1, 11) as i:
                    up(i, False)
                left(10)
                own.base, own.n = L * PER["dve_own"], n0 + 44

                def down(i, last):
                    for p in range(6):
                        mp = m + 11 + 3 * i + p // 2
                        if p % 3 == 2:
                            dve.wait_ge(sem["panel_done"], 2 * mp + p % 2 + 3)
                            for c in range(2):
                                add_h(4 * i + 2 * (p // 3) + c, 2 * (p // 3) + c)
                        if not (last and p >= 4):
                            split_lo(dve, mp + 1, p % 2)

                if last:
                    for i in range(2):
                        down(i, i == 1)
                else:
                    with dve.Fori(0, 2) as i:
                        down(i, False)

            norm2(1, lambda c: p2(0, c))
            los(M_E, 2)

            def even_greatest(j):
                keys, x = (j + 1) * P, Pe if j else Pe0
                unseen = c2[:, consts_at2["unseen"] + j * SEQ:consts_at2["unseen"] + j * SEQ + keys]
                for e, heads in enumerate([(0, 2, 4, 6), (1, 3, 5, 7)] if j == 0 else [(0, 2), (1, 3), (4, 6), (5, 7)]):
                    name, n = f"e{j}{e}", len(heads)
                    dve.wait_ge(*full(name, L))
                    v.tensor_tensor(x[:, heads[0]:heads[-1] + 1:2, :], bank(name)[:, 0:n * keys].rearrange("p (h k) -> p h k", h=n),
                                    bf(unseen, 1, [P, n, keys]), ALU.add).then_inc(emptied(name), 1)
                for e in range(2 if j == 0 else 4):
                    dve.wait_ge(*read(f"e{j}{e}", L))
                own.done(v.tensor_reduce(mx8[:, j, :], x[:, :, :], AX, ALU.max))
                own.wait()
                v.tensor_scalar(nmx8[:, j, :], mx8[:, j, :], -0.125, None, ALU.mult).then_inc(sem["enmx"], 1)

            def even_normed(j):
                keys, x = (j + 1) * P, (Pe if j else Pe0)[:, :, :]
                count = c2[:, consts_at2["count"] + j * SEQ:consts_at2["count"] + j * SEQ + keys]
                dve.wait_ge(sem["esoft"], 1 + j)
                own.done(v.tensor_tensor(x, x, bf(count, 1, [P, 8, keys]), ALU.mult))
                own.wait()
                own.done(v.tensor_reduce(sm8[:, j, :], x, AX, ALU.add))
                own.wait()
                own.done(v.reciprocal(rsm8[:, j, :], sm8[:, j, :]))
                own.wait()
                v.tensor_tensor(x, x, bf(rsm8[:, j, :], 2, [P, 8, keys]), ALU.mult).then_inc(sem["epn"], 1)

            def even_out_lo(j):
                ts = slice(j * P, j * P + P)
                dve.wait_ge(sem["eob_h"], 1 + j)
                v.tensor_tensor(eL[:, 0:4, ts], bank(f"ev{j}")[:, :].rearrange("p (c t) -> p c t", c=4), eH[:, 0:4, ts].bitcast(F32),
                                ALU.subtract).then_inc(emptied(f"ev{j}"), 1)

            def times_gate_c(s):
                dve.wait_ge(sem["panel_done"], 2 * (M_E + 3) + s + 3)
                for c in range(2):
                    b = 2 * s + c
                    dve.wait_ge(lin_read[b], R_E + 3)
                    v.tensor_tensor(ght[:, b, :], lin[b][:, 0:SEQ], ght[:, b, :], ALU.mult).then_inc(lin_read[b], 1)

            def times_gate_b(s):
                dve.wait_ge(sem["panel_done"], 2 * (M_E + 5) + s + 3)
                for c in range(2):
                    b = 2 * s + c
                    v.tensor_tensor(cvt[:, b, :], lin[b][:, 0:SEQ], cvt[:, b, :], ALU.mult).then_inc(lin_read[b], 1)

            split_lo(dve, M_E + 3, 0)
            for n, gain in ((0, KE_QG), (1, KE_KG)):
                x = raw8[:, 4 * n:4 * n + 4, :]
                dve.wait_ge(sem["ern"], n + 1)
                v.scalar_tensor_tensor(x, x, p2(0, gain), rne[:, 4 * n:4 * n + 4, :], ALU.mult, ALU.mult).then_inc(sem["eunit"], 1)
            split_lo(dve, M_E + 3, 1)
            times_gate_c(0)
            split_lo(dve, M_E + 4, 0)
            dve.wait_ge(sem["c2_in"], 16)
            even_greatest(0)
            even_greatest(1)
            even_normed(0)
            times_gate_c(1)
            split_lo(dve, M_E + 4, 1)
            even_normed(1)
            split_lo(dve, M_E + 5, 0)
            for tap in range(3):
                for c in range(4):
                    w = p2(0, KE_SC + (2 - tap) * 4 + c)
                    if tap == 0:
                        dve.wait_ge(lin_read[c], R_E + 4)
                        own.done(v.tensor_scalar(cvt[:, c, :], ght[:, c, :], w, None, ALU.mult))
                    else:
                        own.wait(own.n - 3)
                        own.done(v.scalar_tensor_tensor(cvt[:, c, tap:SEQ], ght[:, c, 0:SEQ - tap], w, cvt[:, c, tap:SEQ], ALU.mult, ALU.add))
            split_lo(dve, M_E + 5, 1)
            even_out_lo(0)
            own.wait()
            times_gate_b(0)
            split_lo(dve, M_E + 6, 0)
            even_out_lo(1)
            times_gate_b(1)
            split_lo(dve, M_E + 6, 1)
            for s in range(2):
                dve.wait_ge(sem["eb_h"], s + 1)
                v.tensor_tensor(eL[:, 4 + 2 * s:6 + 2 * s, :], cvt[:, 2 * s:2 * s + 2, :], eH[:, 4 + 2 * s:6 + 2 * s, :].bitcast(F32), ALU.subtract).then_inc(sem["eb_l"], 1)
            with dve.Fori(0, 2) as i:
                for s in range(2):
                    dve.wait_ge(sem["panel_done"], 2 * (M_E + E_OUT + i) + s + 3)
                    for c in range(2):
                        add_h(4 * i + 2 * s + c, 2 * s + c)
                    split_lo(dve, M_E + E_OUT + i + 1, s)
            mlp2(0, M_E + E_UP, R_E + E_UP, False)

            norm2(3, lambda c: p2(1, c))

            def rotate(n, rnd):
                x = [qk2[:, n, :, d, :] for d in range(2)]
                cos, sin = (bf(table2(name, SEQ), 1, [P, 4, SEQ]) for name in ("cos_r", "sin_r"))
                for b in range(4):
                    dve.wait_ge(lin_read[b], rnd)
                if n:
                    dve.wait_ge(sem["orot"], 2)
                for d in range(2):
                    own.done(v.tensor_tensor(tsin[:, d], x[d], sin, ALU.mult))
                own.wait()
                for d in range(2):
                    own.done(v.tensor_tensor(x[d], x[d], cos, ALU.mult))
                own.wait()
                v.tensor_tensor(x[0], x[0], tsin[:, 1], ALU.subtract).then_inc(sem["orot"], 1)
                v.tensor_tensor(x[1], x[1], tsin[:, 0], ALU.add).then_inc(sem["orot"], 1)

            los(M_O, 2)
            los(M_O + O_K, 1)
            rotate(0, R_O + O_K)
            los(M_O + O_K + 1, 2)
            rotate(1, R_O + O_V)
            los(M_O + O_V + 1, 3)
            for h in range(4):
                dve.wait_ge(*full(f"os{h}", L))
                v.tensor_tensor(sc[:, h, :], bank(f"os{h}")[:, 0:384], table2(f"decay{h}", 384), ALU.mult).then_inc(emptied(f"os{h}"), 1)
            for s in range(2):
                split_lo(dve, M_O + O_G + 1, s)
            split_lo(dve, M_O + O_G + 2, 0)
            for h in range(4):
                x = oR[:, 4 * h:4 * h + 4, :]
                dve.wait_ge(*full(f"om{h}", L))
                v.scalar_tensor_tensor(x, bf(bank(f"om{h}")[:, 0:SEQ], 1, [P, 4, SEQ]), -1.0 / 512, x, ALU.mult, ALU.add).then_inc(emptied(f"om{h}"), 1)
            split_lo(dve, M_O + O_G + 2, 1)
            split_lo(dve, M_O + O_G + 3, 0)

            def odd_gate(h):
                dve.wait_ge(sem["ovar"], h + 1)
                for e in range(4):
                    c = 4 * h + e
                    own.done(v.scalar_tensor_tensor(oR[:, c, :], oR[:, c, :], p2(1, KO_GN + c), rn4[:, h, :], ALU.mult, ALU.mult))
                own.wait()
                cs = slice(4 * h, 4 * h + 4)
                for b in range(4):
                    dve.wait_ge(lin_read[b], R_O + O_G + h + 1)
                v.tensor_tensor(oR[:, cs, :], oR[:, cs, :], sgT[:, cs, :], ALU.mult).then_inc(sem["ogate"], 1)

            def odd_lo(h):
                cs = slice(4 * h, 4 * h + 4)
                dve.wait_ge(sem["og_h"], h + 1)
                v.tensor_tensor(gL[:, cs, :], oR[:, cs, :], gH[:, cs, :].bitcast(F32), ALU.subtract).then_inc(sem["og_l"], 1)

            odd_gate(0)
            odd_gate(1)
            split_lo(dve, M_O + O_G + 3, 1)
            odd_lo(0)
            odd_lo(1)
            odd_gate(2)
            split_lo(dve, M_O + O_OUT, 0)
            split_lo(dve, M_O + O_OUT, 1)
            odd_gate(3)
            odd_lo(2)
            odd_lo(3)
            with dve.Fori(0, 2) as i:
                for q in range(2):
                    m = M_O + O_OUT + 2 * i + q
                    split_lo(dve, m + 1, 0)
                    dve.wait_ge(sem["panel_done"], 2 * m + 4)
                    for c in range(2):
                        add_h(4 * i + 2 * q + c, 2 * q + c)
                    split_lo(dve, m + 1, 1)
            mlp2(1, M_O + O_UP, R_O + RO_UP, True)


def kernel(**inputs):
    import numpy as _np
    import concourse.bacc as _bacc
    from concourse import mybir as _mybir
    from concourse.bass_utils import run_bass_kernel_spmd as _run

    nc = _bacc.Bacc("TRN2", target_bir_lowering=False, num_devices=1)
    arrays, a = {}, {}
    tables = constants()
    given = {name: _np.ascontiguousarray(inputs[name]) for name in INPUTS}
    for name, x in (*given.items(), *tables["arrays"].items()):
        arrays[f"in_{name}"] = x
        a[name] = nc.dram_tensor(f"in_{name}", x.shape, _mybir.dt.from_np(x.dtype), kind="ExternalInput").ap()
    out = nc.dram_tensor("out", (1, SEQ, D), _mybir.dt.float32, kind="ExternalOutput").ap()
    build(nc, a, tables["places"], out.rearrange("b t d -> (b t) d"))
    r = _run(nc, [arrays], core_ids=[0])
    return r.results[0]["out"]
```

```python
import math
from contextlib import ExitStack

import numpy as np

import concourse.bass as bass
from concourse import mybir

F32 = mybir.dt.float32
F32R = mybir.dt.float32r
ACT = mybir.ActivationFunctionType
ALU = mybir.AluOpType
AX = mybir.AxisListType.X
ds = bass.ds

P = 128
D = 1024
DC = D // P
DEPTH = 2
SEQ = 256
META = 16
T = META + SEQ
EPS = 1e-6
HEADS = 4
IDX_HEADS, IDX_DIM, TOPK = 8, 64, 64
FF = 2816
FC = FF // P
CHUNK = 64
INPUTS = (
    "x", "meta_tokens", "norm_mix", "w_in", "conv_a", "a_log", "dt_bias", "a_out_norm", "q_norm", "k_norm", "kidx_norm",
    "w_branch_a", "w_branch_b", "w_gate", "b_gate", "w_out", "norm_ffn", "w_up", "conv_ffn", "w_down", "even_norm_2",
    "even_w_in_2", "even_q_gain_2", "even_k_gain_2", "even_sconv_w_2", "even_w_out_2", "odd_norm_2", "ret_wq_2", "ret_wk_2",
    "ret_wv_2", "ret_wg_2", "ret_gn_gain_2", "ret_wo_2", "ffn_norm_2", "ffn_w_up_2", "ffn_conv_w_2", "ffn_w_down_2",
)
TB = [(0, META), (META, P), (META + P, P)]
KEYS = [at + n for at, n in TB]
LEVELS = 7
PANEL = 256
C_AB, C_BQ, C_BK, C_IQ, C_IK = 2048, 2056, 2568, 2824, 3336
IN_COLS = 3408
S_IK, S_BK, S_BV, S_AB, S_ALL = 0, 128, 256, 384, 400

M_IN, M_GATE, M_BRANCH, M_OUT, M_UP, M_DOWN, M_LAYER = 0, 6, 10, 12, 14, 25, 31
R_IN, R_GATE, R_BRANCH, R_OUT, R_UP, R_DOWN, R_LAYER = 0, 6, 10, 12, 14, 25, 27
M_E, R_E = DEPTH * M_LAYER, DEPTH * R_LAYER
E_OUT, E_UP, E_DOWN, M_EVEN, R_EVEN = 6, 8, 19, 25, 21
M_O, R_O = M_E + M_EVEN, R_E + R_EVEN
O_K, O_V, O_G, O_OUT, O_UP, O_DOWN = 2, 4, 8, 12, 16, 27
RO_OUT, RO_UP, RO_DOWN, M_ODD, R_ODD = 12, 14, 25, 33, 27
M_ALL, R_ALL = M_O + M_ODD, R_O + R_ODD
DOWN_K = [(0, 8), (8, 8), (16, FC - 16)]

BIG = 1e30
INVALID = -3.0e38
TAKEN = -3.4e38
GATE_LEAST = -40.0


def constants():
    f = np.float32
    p = np.arange(P)
    parts, at = [], {}

    def put(name, a):
        at[name] = sum(x.shape[1] for x in parts)
        parts.append(np.ascontiguousarray(a, dtype=f).reshape(P, -1))

    put("ident", np.eye(P))
    put("ones", np.ones((P, P)))
    col = np.zeros((P, 4))
    col[:, 0] = EPS
    col[:, 1] = math.log(P ** -0.5)
    col[:, 2] = 1.0
    put("cols", col)
    put("half", (p[:, None] // 64 == p[None, :] // 64))

    def turn(dim):
        r = np.zeros((P, P))
        for i in range(P):
            if i % dim < dim // 2:
                r[i + dim // 2, i] = -1.0
            else:
                r[i - dim // 2, i] = 1.0
        return r

    put("turn_a", turn(P))
    put("turn_i", turn(IDX_DIM))

    def angles(dim, n_tok):
        inv = (1.0 / (f(10000.0) ** (np.arange(0, dim, 2, dtype=f) / f(dim)))).astype(f)
        return (np.arange(n_tok, dtype=f)[:, None] * inv[None, :]).astype(f)

    for name, dim in (("a", P), ("i", IDX_DIM)):
        ang = angles(dim, T)
        rows = p % (dim // 2)
        put("cos_" + name, np.cos(ang).T[rows])
        put("sin_" + name, np.sin(ang).T[rows])
    for l in range(LEVELS):
        s, c = p[:, None], p[None, :]
        put(f"level{l}", (s >> (l + 1) == c >> (l + 1)) & ((c >> l) % 2 == 1) & ((s >> l) % 2 == 0))
    put("upto", p[:, None] <= p[None, :])
    q = np.arange(SEQ).reshape(2, P).T
    limit = (q // CHUNK + 1) * CHUNK
    barred = np.where(np.arange(SEQ)[None, None, :] < limit[:, :, None], 0.0, INVALID)
    put("barred0", barred[:, 0, 0:P])
    put("barred1", barred[:, 1, :])
    first, first_at = np.concatenate(parts, 1), dict(at)
    parts.clear()
    at.clear()
    t, s = np.arange(SEQ)[:, None], np.arange(SEQ)[None, :]
    back = t - s
    count = sum(((back >= 0) & (back % d == 0) & (back // d <= w // d)).astype(f) for w, d in ((128, 1), (512, 4), (2048, 16)))
    put("count", count.reshape(2, P, SEQ).transpose(1, 0, 2))
    put("unseen", np.where(count > 0, 0.0, -BIG).reshape(2, P, SEQ).transpose(1, 0, 2))
    half = P
    inv = (f(10000.0) ** (-np.arange(half, dtype=f) / f(half))).astype(f)
    ang = (np.arange(SEQ, dtype=f)[:, None] * inv[None, :]).astype(f)
    put("cos_r", np.cos(ang).T)
    put("sin_r", np.sin(ang).T)
    for h in range(4):
        log_g = np.log1p(-(2.0 ** (-5.0 - h)))
        dec = np.where(back >= 0, np.exp(log_g * np.maximum(back, 0)), 0.0) * 256 ** -0.5
        dec = dec.T.reshape(2, P, SEQ)
        put(f"decay{h}", np.concatenate([dec[0], dec[1][:, P:]], 1))
    second = np.concatenate(parts, 1)
    return {"arrays": {"c1": first, "c2": second}, "places": (first_at, at, first.shape[1], second.shape[1])}


def plan_aux(jobs):
    place, used, q = {}, [0] * 4, 0
    for job in jobs:
        n, names = job[1:] if isinstance(job, tuple) else (1, [job])
        step = len(names) // 4
        for name in names:
            used[q % 4] += 1
            place[name] = (q % 4, used[q % 4], step)
            q += 1
        for b in range(4):
            used[b] += (n - 1) * step
    return place, used


class Own:

    def __init__(self, eng, sem):
        self.eng, self.sem, self.base, self.n = eng, sem, 0, 0

    def done(self, ins):
        ins.then_inc(self.sem, 1)
        self.n += 1
        return self.n

    def wait(self, n=None):
        self.eng.wait_ge(self.sem, self.base + (self.n if n is None else n))


JOBS = (
    ["ms1", "ik", "bk", "tk"]
    + [f"ssq{h}" for h in range(4)] + [f"ssk{h}" for h in range(4)] + [f"sbq{h}" for h in range(4)] + ["sbk", "sik"]
    + ["gc", "gb0", "bb0", "gb1", "bb1", "kk0", "qk0", "gb2", "bb2", "kk1", "qk1", "kk2", "qk2"] + [x for b in range(3) for x in (f"kt{b}", f"vt{b}")]
    + ["rk", "rik"] + [f"rq{h}" for h in range(4)] + [f"ri{c}" for c in range(4)]
    + ["Y0_0", "Y1_0", "Y2_0"] + [f"ix0{e}" for e in range(2)] + [f"ix1{e}" for e in range(4)]
    + [("loop", LEVELS - 2, ["Y0", "Y1", "T1", "Y2", "T2", "XA0", "X1", "X2"])] + ["Y1_6", "T1_6", "Y2_6", "T2_6", "s0", "A1", "A2"]
    + ["vn0"] + [f"s{h}1" for h in "abcd"] + ["o0", "dS0", "pt0", "kS1", "pv0"] + [f"pt{b}_1" for b in range(2)] + ["vn1"]
    + [f"s{h}2" for h in "abcd"] + ["o1", "dS1", "pv1", "kS2"] + [f"pt{b}_2" for b in range(3)] + ["vn2", "pv2", "o2"]
    + [f"so{h}" for h in range(4)] + [("loop", 2, [f"br{b}" for b in range(4)])] + ["ms2"]
)
PLACE, AUX_PER = plan_aux(JOBS)
IX_HEADS = (
    tuple(tuple(range(e, IDX_HEADS, 2)) for e in range(2)),
    tuple((4 * (e // 2) + e % 2, 4 * (e // 2) + e % 2 + 2) for e in range(4)),
)
JOBS2 = (
    ["ems"] + [f"eq{c}" for c in range(4)] + ["e00", "e01"] + [f"e1{e}" for e in range(4)] + [f"et0{g}" for g in range(2)] + ["ev0"]
    + [f"et1{g}{b}" for g in range(2) for b in range(2)] + ["ev1", "emf", "oms"]
    + [f"os{h}" for h in range(4)] + [f"oo{h}{e}" for h in range(4) for e in range(2)]
    + [f"ow{h}" for h in range(4)] + ["omf"]
)
PLACE.update(plan_aux(JOBS2)[0])

PER = {
    "panel_in": 16 * M_LAYER, "whi": 4 * M_LAYER, "wlo": 4 * M_LAYER, "whi_used": 2 * M_LAYER, "panel_done": 2 * M_LAYER,
    "lin_read": R_LAYER, "small_in": 5 * 16,
    "sq": DC, "rstd": 2, "n": 2 * DC, "nh": DC, "nl": DC,
    "conv": 12, "silu": 3, "sq_heads": 2, "sq_att": 1, "rn": 4, "qk_unit": 2, "att_unit": 3,
    "sp_in": 1, "sp_ln": 1, "gt": 7, "eg": 4, "dec": 3, "kdx": 1, "qe": 1,
    "beta": 1, "rope_cos": 4, "rope": 4, "score": 6, "ml": 3 * LEVELS, "ab_ready": 3,
    "nmx": 3, "soft": 2, "pn": 3, "ob_h": 3, "sqo": 3, "rno": 4, "oa": 4, "oa_h": 4, "oa_l": 4,
    "gates": 12, "y": 8, "yh": 4, "yl": 4,
    "tap": 2 * 11, "gate_silu": 2 * 11, "ah": 2 * 11, "al": 2 * 11,
    "act_own": 0, "dve_own": 0,
}
PER["act_own"] = 4
PER["dve_own"] = 127


SECOND = ("c2_in", "sq2", "rstd2", "n2", "nh2", "nl2", "raw2", "esq", "ern", "eunit", "enmx", "esoft", "epn", "eob_h", "egh", "econv",
          "eb_h", "eb_l", "oraw", "orot", "osc", "osq", "ovar", "ogate", "og_h", "og_l", "tap2", "silu2", "conv2", "ah2", "al2")


def bf(ap, axis, shape):
    return ap.unsqueeze(axis).to_broadcast(shape)


def build(nc, a, places, out):
    ctx = ExitStack()
    consts_at1, consts_at2, n1, n2 = places
    with ctx:
        sem = {name: ctx.enter_context(nc.semaphore(name)) for name in PER if name not in ("panel_in", "lin_read")}
        for name in ("start_in", "tables_in", "h0", "rows", "rows2_0", "rows2_1", "par_in", "stored", "turned", "turned_back", "out_ready", "cleared", "pe_stood", "dve_stood", *SECOND):
            sem[name] = ctx.enter_context(nc.semaphore(name))
        panel_in = [ctx.enter_context(nc.semaphore(f"panel_in{i}")) for i in range(4)]
        lin_read = [ctx.enter_context(nc.semaphore(f"lin_read{i}")) for i in range(4)]
        aux_full = [ctx.enter_context(nc.semaphore(f"aux_full{i}")) for i in range(4)]
        aux_read = [ctx.enter_context(nc.semaphore(f"aux_read{i}")) for i in range(4)]
        lin = [ctx.enter_context(nc.psum_tensor(f"lin{i}", [P, 512], F32)) for i in range(4)]
        aux = [ctx.enter_context(nc.psum_tensor(f"aux{i}", [P, 512], F32)) for i in range(4)]

        base = nc.sbuf_usable_end - nc.sbuf_bytes_remaining
        base = (base + 63) // 64 * 64

        def tile(name, shape, at, dt=F32):
            size = 4 * int(np.prod(shape[1:]))
            assert at % 32 == 0 and at + size <= nc.sbuf_usable_end, (name, at + size - nc.sbuf_usable_end)
            return nc.alloc_sbuf_tensor_at(name, shape, dt, offset=at), (at + size + 31) // 32 * 32

        hT, o = tile("hT", [P, DC, T], base)
        nH, o = tile("nH", [P, DC, T], o, F32R)
        nL, o = tile("nL", [P, DC, T], o, F32R)
        stage, o = tile("stage", [P, 2, DC, PANEL], o)
        wH, o = tile("wH", [P, 2, DC, PANEL], o, F32R)
        wL, o = tile("wL", [P, 2, DC, PANEL], o, F32R)
        c1, o = tile("c1", [P, n1], o)
        par, o = tile("par", [P, 2 * DEPTH, 2 * P], o)
        rates, o = tile("rates", [P, DEPTH, 8], o)
        parL, o = tile("parL", [P, 2 * P + 8], o)
        o = (o + 63) // 64 * 64
        arena = o

        def const(name, n, parts=P):
            return c1[0:parts, consts_at1[name]:consts_at1[name] + n]

        ident, ones = const("ident", P), const("ones", P)
        eps_col, lnq_col = const("cols", 1), c1[:, consts_at1["cols"] + 1:consts_at1["cols"] + 2]
        one_col = c1[:, consts_at1["cols"] + 2:consts_at1["cols"] + 3]

        rawT, o = tile("rawT", [P, 24, T], arena)
        cT, o = tile("cT", [P, 12, T], o)
        zT, o = tile("zT", [P, 4, T], o)
        kd_at = o
        kd, o = tile("kd", [P, 3, 4, P], o)
        vt, o = tile("vt", [P, 3, 4, P], o)
        mixer_tail = o
        nT, o = tile("nT", [P, DC, T], o)
        oH, o = tile("oH", [P, DC, T], o, F32R)
        oL, o2 = tile("oL", [P, DC, T], o, F32R)
        wS, _ = tile("wS", [P, DC, S_ALL], o - 4 * DC * T)
        o = o2

        def blocks(name, at):
            big, at = tile(name, [P, 2, 4, P], at)
            small, at = tile(name + "0", [META, 4, META], at)
            return [small[:, :, :], big[:, 0], big[:, 1]], at

        MT, q_at = blocks("MT", o)
        QD, x_at = blocks("QD", q_at)
        X, a_at = blocks("X", x_at)
        A, ml_at = blocks("A", a_at)
        ML, y_at = blocks("ML", ml_at)
        Y, o2 = blocks("Y", y_at)
        mt_at, o = o, o2
        sqh, _ = tile("sqh", [P, DC, T], x_at)
        gtri, _ = blocks("gtri", x_at)
        bdiag, _ = blocks("bdiag", a_at)
        decay, _ = blocks("decay", ml_at)
        sq_att, _ = tile("sq_att", [P, 6, T], ml_at)
        rnq, _ = tile("rnq", [P, 4, T], mt_at)
        rnk, _ = tile("rnk", [P, 4, T], q_at)
        rnb, _ = tile("rnb", [P, 5, T], kd_at)
        rni, _ = tile("rni", [P, 1, T], kd_at + 4 * 3 * 4 * P)
        tmp4, _ = tile("tmp4", [P, 4, T], y_at)
        R, vn_at = tile("R", [P, 4, P], ml_at)
        vn, _ = tile("vn", [P, 4, P], vn_at)
        S, _ = tile("S", [P, 4, P], y_at)
        Pm, _ = tile("Pm", [P, 4, T], mt_at)
        sqo, _ = tile("sqo", [P, 4, T], x_at)
        rno, _ = tile("rno", [P, 4, T], a_at)
        yT, _ = tile("yT", [P, DC, T], mixer_tail)
        sq8, _ = tile("sq8", [P, DC, T], mixer_tail)
        ytmp, _ = tile("ytmp", [P, 2, T], x_at)
        rl, r_at = tile("rl", [P, 2, 2 * SEQ], mixer_tail)
        score, r_at = tile("score", [P, 2, SEQ], r_at)
        PT, pt_end = tile("PT", [P, 3, 4 * P], mixer_tail)
        assert pt_end <= r_at
        work, r_at = tile("work", [P, 2, SEQ], r_at)
        assert r_at <= mixer_tail + 4 * DC * T
        eg, o2 = tile("eg", [P, 4, T], o)
        oA, _ = tile("oA", [P, 4, T], o)
        o = o2
        bkr, o = tile("bkr", [P, T], o)
        ikr, o = tile("ikr", [P, T], o)
        vtok, o = tile("vtok", [P, 3, P], o)
        bias, o = tile("bias", [P, 2, T], o)
        rs, _ = tile("rs", [P, T], y_at)
        P0, o = tile("P0", [META, 4, META], o)
        ab, o = tile("ab", [P, 3, 16], o)
        iw, o = tile("iw", [P, 3, 8], o)
        gx, o = tile("gx", [P, 3, 4], o)
        gm, o = tile("gm", [P, 3, 4], o)
        gl, o = tile("gl", [P, 3, 4], o)
        gg, o = tile("gg", [P, 3, 4], o)
        bt, o = tile("bt", [P, 3, 4], o)
        beta, o = tile("beta", [P, 3, 4], o)
        gcs, o = tile("gcs", [P, 3, 4], o)
        egt, o = tile("egt", [P, 3, 4], o)
        kdx, o = tile("kdx", [P, 3, 4], o)
        sdec, o = tile("sdec", [P, 3, 4], o)
        m8, o = tile("m8", [P, 2, 8], o)
        mx, o = tile("mx", [P, 3, 4], o)
        nmx, o = tile("nmx", [P, 3, 4], o)
        sm, o = tile("sm", [P, 3, 4], o)
        rsm, o = tile("rsm", [P, 3, 4], o)
        aH, f_at = tile("aH", [P, FC, T], arena, F32R)
        aL, f_at = tile("aL", [P, FC, T], f_at, F32R)
        assert f_at <= mixer_tail
        u, f_at = tile("u", [P, 2, T], mt_at)
        sg, f_at = tile("sg", [P, 2, T], f_at)
        av, f_at = tile("av", [P, 2, T], f_at)
        xin, s_at = tile("xin", [P, 2, D], arena)
        metain, s_at = tile("metain", [META, D], s_at)
        rows, s_at = tile("rows", [P, 2 * DEPTH, 2, P], s_at)
        outT, _ = tile("outT", [P, 2, D], arena)

        n_tok, KB = SEQ, 4 * SEQ
        c2, _ = tile("c2", [P, n2], x_at)
        assert x_at + 4 * n2 <= y_at
        nT2, top = tile("nT2", [P, DC, SEQ], arena + 78 * KB)
        assert top <= x_at
        raw8, e_at = tile("raw8", [P, 8, SEQ], arena)
        vtk, e_at = tile("vtk", [P, 2, 512], e_at)
        Pe0, e_at = tile("Pe0", [P, 8, P], e_at)
        ght, e_at = tile("ght", [P, 4, SEQ], e_at)
        cvt, e_at = tile("cvt", [P, 4, SEQ], e_at)
        Pe, e_at = tile("Pe", [P, 8, SEQ], e_at)
        PTe, e_at = tile("PTe", [P, 2, 8 * P], e_at)
        sqe, e_at = tile("sqe", [P, 8, SEQ], e_at)
        rne, e_at = tile("rne", [P, 8, SEQ], e_at)
        qk2, o_at = tile("qk2", [P, 2, 4, 2, SEQ], arena)
        vtk2, o_at2 = tile("vtk2", [P, 2, 2048], o_at)
        gH, _ = tile("gH", [P, 16, SEQ], arena, F32R)
        gL, _ = tile("gL", [P, 16, SEQ], o_at, F32R)
        sq16, _ = tile("sq16", [P, 16, SEQ], o_at)
        tsin, o_at3 = tile("tsin", [P, 2, 4, SEQ], o_at2)
        o_at = o_at2 + 4 * 4 * SEQ
        rn4, _ = tile("rn4", [P, 4, SEQ], o_at)
        sgT, o_at = tile("sgT", [P, 16, SEQ], o_at3)
        sc, o_at = tile("sc", [P, 4, 384], o_at)
        oR, o_at4 = tile("oR", [P, 16, SEQ], o_at)
        assert o_at4 <= arena + 78 * KB
        aH2, f_at = tile("aH2", [P, FC, SEQ], arena, F32R)
        aL2, f_at = tile("aL2", [P, FC, SEQ], f_at, F32R)
        u2, f_at = tile("u2", [P, 4, SEQ], f_at)
        sg2, f_at = tile("sg2", [P, 2, SEQ], f_at)
        av2, f_at = tile("av2", [P, 2, SEQ], f_at)
        sqf, f_at = tile("sqf", [P, 8, SEQ], f_at)
        e_at = max(e_at, f_at)
        eH, e_at = tile("eH", [P, 8, SEQ], e_at, F32R)
        eL, e_at = tile("eL", [P, 8, SEQ], e_at, F32R)
        assert e_at <= arena + 78 * KB
        assert f_at <= arena + 78 * KB
        mx8, s_at = tile("mx8", [P, 2, 8], y_at + 4 * 4 * P)
        nmx8, s_at = tile("nmx8", [P, 2, 8], s_at)
        sm8, s_at = tile("sm8", [P, 2, 8], s_at)
        rsm8, s_at = tile("rsm8", [P, 2, 8], s_at)
        vmean, s_at = tile("vmean", [P, 2], s_at)
        KE_QG, KE_KG, KE_SC, KE_FN, KE_T2 = 8, 9, 10, 22, 30
        KO_GN, KO_FN, KO_T2 = 8, 24, 32

        def p2(j, k):
            return par[:, DEPTH + j, k:k + 1]

        def table2(name, n):
            return c2[:, consts_at2[name]:consts_at2[name] + n]

        K_CONV, K_NORM1, K_NORM2, K_ANORM, K_QN, K_KN, K_IN, K_BG, K_FCONV = 0, 48, 56, 64, 65, 66, 67, 68, P
        K_DT, K_NA = 2 * P, 2 * P + 4

        def pc(k, n=1):
            return parL[:, k:k + n]

        def at(name, l, n):
            return l * PER[name] + n

        def tok(b):
            return slice(TB[b][0], TB[b][0] + TB[b][1])

        def cdyn(x, width=1):
            return ds(x, width)

        def full(name, l, it=0):
            b, n, step = PLACE[name]
            return aux_full[b], l * AUX_PER[b] + n + it * step

        def read(name, l, it=0, back=0):
            b, n, step = PLACE[name]
            return aux_read[b], l * AUX_PER[b] + (n - back * step) + it * step

        def bank(name):
            return aux[PLACE[name][0]]

        def emptied(name):
            return aux_read[PLACE[name][0]]

        def filled(name):
            return aux_full[PLACE[name][0]]

        def stand(eng, name):
            eng.sem_inc(sem[name], 1)

        def load(sp, m, s, pieces):
            for h, (k0, k1, src) in enumerate(pieces):
                sp.wait_ge(sem["wlo"], 4 * m + 2 * s + h + 1)
                sp.dma_start(stage[:, s, k0:k1, :], src).then_inc(panel_in[2 * s + h], 16)

        def split_hi(act, m, s):
            act.wait_ge(sem["whi_used"], 2 * m + s + 1)
            for h in range(2):
                ks = slice(4 * h, 4 * h + 4)
                act.wait_ge(panel_in[2 * s + h], 16 * m + 16)
                nc.scalar.activation(wH[:, s, ks], stage[:, s, ks], ACT.Copy).then_inc(sem["whi"], 1)

        def split_lo(dve, m, s, on_pool=False):
            dve.wait_ge(sem["panel_done"], 2 * m + s + 1)
            for h in range(2):
                ks = slice(4 * h, 4 * h + 4)
                dve.wait_ge(sem["whi"], 4 * m + 2 * s + h + 1)
                (nc.gpsimd if on_pool else nc.vector).tensor_tensor(wL[:, s, ks], stage[:, s, ks], wH[:, s, ks].bitcast(F32), ALU.subtract).then_inc(sem["wlo"], 1)

        def multiply(pe, m, s, rnd, groups, width, start=True, stop=True, banks=lin, late=None, behind_first=False):
            pe.wait_ge(sem["whi"], 4 * m + 2 * s + 2)
            for g, (b, cols, ks) in enumerate(groups):
                if start and banks is lin and rnd is not None:
                    pe.wait_ge(lin_read[b], rnd)
                if late and g == late[0]:
                    pe.wait_ge(*late[1])
                for n, (k, xh, xl) in enumerate(ks):
                    mm = nc.tensor.matmul(banks[b][:, 0:width], wH[:, s, k, cols], xh, start=start and n == 0, stop=False)
                    if behind_first and g + n == 0:
                        mm.then_inc(sem["panel_done"], 1)
                    mm = nc.tensor.matmul(banks[b][:, 0:width], wH[:, s, k, cols], xl, start=False, stop=False)
            mm.then_inc(sem["whi_used"], 1)
            pe.wait_ge(sem["wlo"], 4 * m + 2 * s + 6)
            for b, cols, ks in groups:
                for n, (k, xh, _) in enumerate(ks):
                    mm = nc.tensor.matmul(banks[b][:, 0:width], wL[:, s, k, cols], xh, start=False, stop=stop and n == len(ks) - 1)
            mm.then_inc(sem["panel_done"], 1)

        def multiply_first(pe, m, rnd, groups, width, hi_ready, lo_ready, at_once=False):
            pe.wait_ge(sem["whi"], 4 * m + 2)
            pe.wait_ge(sem["wlo"], 4 * m + 6)
            for b, _, _ in groups:
                if rnd is not None:
                    pe.wait_ge(lin_read[b], rnd)

            def product(w, x, pair, first=False, last=False):
                for b, cols, ks in groups:
                    for term in ks[2 * pair:2 * pair + 2]:
                        k = term[0]
                        t = nc.tensor.matmul(lin[b][:, 0:width], w[:, 0, k, cols], term[x], start=first and k == 0, stop=last and k == DC - 1)
                return t

            pairs = range(DC // 2)
            for pair in pairs:
                pe.wait_ge(*hi_ready(pair))
                product(wH, 1, pair, first=True)
                product(wL, 1, pair)
                if at_once:
                    pe.wait_ge(*lo_ready(pair))
                    mm = product(wH, 2, pair, last=True)
            for pair in [] if at_once else pairs:
                pe.wait_ge(*lo_ready(pair))
                mm = product(wH, 2, pair, last=True)
            mm.then_inc(sem["whi_used"], 1)

        def halves(s, x_hi, x_lo, n=DC, k0=0):
            return [(2 * s + c, slice(c * P, c * P + P), [(k, x_hi[:, k0 + k, :], x_lo[:, k0 + k, :]) for k in range(n)])
                    for c in range(2)]

        block = ctx.enter_context(nc.Block())

        def w_rows(name, k_all):
            return a[name].rearrange("l (k p) n -> p (l k) n", p=P), k_all

        def parameter_rows2(eng, j):
            def row(t, r, src, n, cols=slice(0, P)):
                eng.dma_start(rows[r:r + n, DEPTH + j, t, cols], src).then_inc(sem[f"rows2_{j}"], 16)

            if j == 0:
                row(0, 0, a["even_norm_2"].rearrange("l (c p) -> (l c) p", p=P), DC)
                for r, name in ((KE_QG, "even_q_gain_2"), (KE_KG, "even_k_gain_2")):
                    for h in range(2):
                        row(0, r, a[name], 1, slice(64 * h, 64 * h + 64))
                row(0, KE_SC, a["even_sconv_w_2"].rearrange("l k (c p) -> (l k c) p", p=P), 12)
            else:
                row(0, 0, a["odd_norm_2"].rearrange("l (c p) -> (l c) p", p=P), DC)
                row(0, KO_GN, a["ret_gn_gain_2"].rearrange("l h (c p) -> (l h c) p", p=P), 16)
            fn, t2 = ((KE_FN, KE_T2), (KO_FN, KO_T2))[j]
            row(0, fn, a["ffn_norm_2"][j].rearrange("(c p) -> c p", p=P), DC)
            row(0, t2, a["ffn_conv_w_2"][j, 2:3].rearrange("k (c p) -> (k c) p", p=P), 2 * FC)
            row(1, 0, a["ffn_conv_w_2"][j, 0:2].rearrange("k (c p) -> (k c) p", p=P), 4 * FC)

        early = consts_at1["half"]

        @block.sync
        def _(sp):
            sp.dma_start(c1[:, 0:early], a["c1"][:, 0:early]).then_inc(sem["start_in"], 16)
            sp.dma_start(xin[:, :, :], a["x"].rearrange("b (j p) d -> p (b j) d", p=P)).then_inc(sem["start_in"], 16)
            sp.dma_start(metain[:, :], a["meta_tokens"]).then_inc(sem["start_in"], 16)

            def whole(w, l, kd_, col):
                return [(k0, k0 + 4, w[:, ds(l * kd_ + k0, 4), ds(col, PANEL)]) for k0 in (0, 4)]

            w_in, _ = w_rows("w_in", DC)
            w_gate, _ = w_rows("w_gate", DC)
            w_a, _ = w_rows("w_branch_a", 4)
            w_b, _ = w_rows("w_branch_b", 4)
            w_out, _ = w_rows("w_out", DC)
            w_up, _ = w_rows("w_up", DC)
            w_down, _ = w_rows("w_down", FC)

            def layer(l):
                m0 = l * M_LAYER
                with sp.Fori(0, 4) as i:
                    for s in range(2):
                        load(sp, m0 + i, s, whole(w_in, l, DC, i * 512 + s * PANEL))
                for i, col in ((4, C_BQ), (5, C_IQ)):
                    for s in range(2):
                        load(sp, m0 + i, s, whole(w_in, l, DC, col + s * PANEL))
                with sp.Fori(0, 4) as i:
                    for s in range(2):
                        load(sp, m0 + M_GATE + i, s, whole(w_gate, l, DC, i * 512 + s * PANEL))
                with sp.Fori(0, 2) as i:
                    for s in range(2):
                        cols = ds(i * 512 + s * PANEL, PANEL)
                        load(sp, m0 + M_BRANCH + i, s, [(0, 4, w_a[:, ds(l * 4, 4), cols]), (4, 8, w_b[:, ds(l * 4, 4), cols])])
                with sp.Fori(0, 2) as i:
                    for s in range(2):
                        load(sp, m0 + M_OUT + i, s, whole(w_out, l, DC, i * 512 + s * PANEL))
                with sp.Fori(0, 11) as i:
                    for s in range(2):
                        load(sp, m0 + M_UP + i, s, whole(w_up, l, DC, i * PANEL + s * FF))
                with sp.Fori(0, 2) as i:
                    for p in range(6):
                        k0, n = DOWN_K[p % 3]
                        cols = ds(i * 512 + (p // 3) * PANEL, PANEL)
                        load(sp, m0 + M_DOWN + 3 * i + p // 2, p % 2,
                             [(h, min(h + 4, n), w_down[:, ds(l * FC + k0 + h, min(4, n - h)), cols]) for h in (0, 4)])

            with sp.Fori(0, DEPTH) as l:
                layer(l)

            def mlp2(j, m):
                up = a["ffn_w_up_2"].rearrange("l (k p) n -> p (l k) n", p=P)
                down = a["ffn_w_down_2"].rearrange("l (k p) n -> p (l k) n", p=P)
                with sp.Fori(0, 11) as i:
                    for s in range(2):
                        load(sp, m + i, s, whole(up, j, DC, i * PANEL + s * FF))
                with sp.Fori(0, 2) as i:
                    for p in range(6):
                        k0, n = DOWN_K[p % 3]
                        cols = ds(i * 512 + (p // 3) * PANEL, PANEL)
                        load(sp, m + 11 + 3 * i + p // 2, p % 2,
                             [(h, min(h + 4, n), down[:, j * FC + k0 + h:j * FC + k0 + min(h + 4, n), cols]) for h in (0, 4)])

            def columns(name, m, pairs):
                w = a[name].rearrange("l (k p) n -> p (l k) n", p=P)
                with sp.Fori(0, pairs) as i:
                    for s in range(2):
                        load(sp, m + i, s, whole(w, 0, DC, i * 512 + s * PANEL))

            w = a["even_w_in_2"].rearrange("l (k p) n -> p (l k) n", p=P)
            for i, part in enumerate((0, 1, 5, 4, 2, 3)):
                for s in range(2):
                    load(sp, M_E + i, s, whole(w, 0, DC, part * 512 + s * PANEL))
            columns("even_w_out_2", M_E + E_OUT, 2)
            mlp2(0, M_E + E_UP)
            columns("ret_wq_2", M_O, 2)
            columns("ret_wk_2", M_O + O_K, 2)
            columns("ret_wv_2", M_O + O_V, 4)
            columns("ret_wg_2", M_O + O_G, 4)
            w_o = a["ret_wo_2"].rearrange("l (k p) n -> p (l k) n", p=P)
            with sp.Fori(0, 4) as i:
                for s in range(2):
                    load(sp, M_O + O_OUT + i, s, [(k0, k0 + 4, w_o[:, 8 * s + k0:8 * s + k0 + 4, ds(i * PANEL, PANEL)]) for k0 in (0, 4)])
            mlp2(1, M_O + O_UP)
            sp.wait_ge(sem["out_ready"], 4)
            sp.dma_start(out.rearrange("(j p) d -> p j d", p=P), outT[:, :, :]).then_inc(sem["stored"], 16)
            sp.wait_ge(sem["stored"], 16)

        @block.gpsimd
        def _(pool):
            pool.wait_ge(sem["cleared"], 1)
            parameter_rows2(pool, 0)
            w = a["w_in"].rearrange("l (k p) n -> p (l k) n", p=P)
            for l in range(DEPTH):
                if l:
                    pool.wait_ge(sem["panel_done"], at("panel_done", l - 1, 2 * M_OUT + 2))
                for to, of, n in ((S_IK, C_IK, 64), (S_IK + 64, C_IK, 64), (S_BK, C_BK, 2 * P), (S_AB, C_AB, 8), (S_AB + 8, C_IK + 64, 8)):
                    pool.dma_start(wS[:, :, to:to + n], w[:, l * DC:(l + 1) * DC, of:of + n]).then_inc(sem["small_in"], 16)
                if l == 0:
                    pool.wait_ge(sem["wlo"], 6)
                    split_lo(pool, 0, 1, on_pool=True)
                def gate_lo(i):
                    m = l * M_LAYER + M_GATE + i
                    for s in range(2):
                        pool.wait_ge(sem["wlo"], 4 * m + 2 * s + 4)
                        split_lo(pool, m, s, on_pool=True)

                gate_lo(0)
                pool.wait_ge(*full("ssk3", l))
                for src, spread in ((gg, gtri), (beta, bdiag)):
                    pool.wait_ge(*((sem["gt"], at("gt", l, 1)) if src is gg else (sem["beta"], at("beta", l, 1))))
                    for b in range(3):
                        n = TB[b][1]
                        mask = const("upto", n, n) if src is gg else ident[0:n, 0:n]
                        nc.gpsimd.tensor_tensor(spread[b], bf(mask, 1, [n, 4, n]), bf(src[0:n, b, :], 2, [n, 4, n]), ALU.mult).then_inc(sem["gt"], 1)
                gate_lo(1)
                pool.wait_ge(sem["eg"], at("eg", l, 4))
                pool.wait_ge(*full("qk2", l))
                nc.gpsimd.tensor_tensor(cT[:, 0:4, :], cT[:, 0:4, :], eg[:, :, :], ALU.mult).then_inc(sem["qe"], 1)
                for name, kind, x in (("rk", "a", bkr[:, :].unsqueeze(1)), ("rik", "i", ikr[:, :].unsqueeze(1)),
                                      ("rq3", "a", rawT[:, 16:20, :]), ("ri3", "i", rawT[:, 20:24, :])):
                    pool.wait_ge(*full(name, l))
                    nc.gpsimd.tensor_tensor(x, x, bf(const("cos_" + kind, T), 1, [P, x.shape[1], T]), ALU.mult).then_inc(sem["rope_cos"], 1)
                gate_lo(2)
                gate_lo(3)
            pool.wait_ge(sem["small_in"], DEPTH * 80)
            pool.wait_ge(sem["nl"], DEPTH * PER["nl"])
            pool.dma_start(c2[:, :], a["c2"]).then_inc(sem["c2_in"], 16)
            pool.wait_ge(sem["c2_in"], 16)

        @block.tensor
        def _(pe):
            def begin(name, l, it=0):
                b, n, step = PLACE[name]
                if n > 1:
                    pe.wait_ge(aux_read[b], l * AUX_PER[b] + n - 1 + it * step)
                return aux[b]

            def mm(o_, l_, r_, start=True, stop=True):
                return nc.tensor.matmul(o_, l_, r_, start=start, stop=stop)

            pe.sem_inc(sem["whi_used"], 2)
            pe.sem_inc(sem["panel_done"], 2)
            pe.wait_ge(sem["start_in"], 48)
            for c in range(DC):
                if c >= 4:
                    pe.wait_ge(sem["h0"], c - 3)
                cols = slice(c * P, c * P + P)
                nc.tensor.transpose(lin[c % 4][:, 0:META], metain[:, cols], ident[0:META, 0:META])
                for j in range(2):
                    t = nc.tensor.transpose(lin[c % 4][:, META + j * P:META + (j + 1) * P], xin[:, j, cols], ident)
                t.then_inc(sem["turned"], 1)
            pe.wait_ge(sem["rows"], 12 * 16)
            for l in range(2 * DEPTH):
                if l >= DEPTH:
                    pe.wait_ge(sem[f"rows2_{l - DEPTH}"], (9, 5)[l - DEPTH] * 16)
                pe.wait_ge(sem["h0"], 5 + l)
                nc.tensor.transpose(lin[l][:, 0:P], rows[:, l, 0, :], ident)
                nc.tensor.transpose(lin[l][:, P:2 * P], rows[:, l, 1, :], ident).then_inc(sem["turned"], 1)

            def mean_square(name, l, which):
                ps = begin(name, l)
                for c in range(DC):
                    if c % 2 == 0:
                        pe.wait_ge(sem["sq"], at("sq", l, 4 * (which - 1) + c // 2 + 1))
                    t = mm(ps[:, 0:T], ones, sq8[:, c, :], c == 0, c == DC - 1)
                t.then_inc(filled(name), 1)

            def behind_norm(l, which):
                return (lambda pair: (sem["nh"], at("nh", l, 4 * (which - 1) + pair + 1)),
                        lambda pair: (sem["nl"], at("nl", l, 4 * (which - 1) + pair + 1)))

            def layer(l):
                m0, r0 = l * M_LAYER, l * R_LAYER
                mean_square("ms1", l, 1)
                multiply_first(pe, m0, None, halves(0, nH, nL), T, *behind_norm(l, 1))
                multiply(pe, m0, 1, None, halves(1, nH, nL), T, behind_first=True)
                pe.wait_ge(sem["small_in"], at("small_in", l, 80))
                for name, col in (("ik", S_IK), ("bk", S_BK)):
                    ps = begin(name, l)
                    for k in range(DC):
                        t = mm(ps[:, 0:T], wS[:, k, col:col + P], nT[:, k, :], k == 0, k == DC - 1)
                    t.then_inc(filled(name), 1)
                ps, n = begin("tk", l), S_ALL - S_BV
                for b in range(3):
                    for k in range(DC):
                        t = mm(ps[0:TB[b][1], b * n:(b + 1) * n], nT[:, k, tok(b)], wS[:, k, S_BV:S_ALL], k == 0, k == DC - 1)
                t.then_inc(filled("tk"), 1)
                with pe.Fori(1, 6) as i:
                    for s in range(2):
                        multiply(pe, m0 + i, s, r0 + i, halves(s, nH, nL), T)

                pe.wait_ge(sem["sq_heads"], at("sq_heads", l, 2))
                for h in range(8):
                    name = f"ss{'qk'[h // 4]}{h % 4}"
                    mm(begin(name, l)[:, 0:T], ones, sqh[:, h, :]).then_inc(filled(name), 1)
                pe.wait_ge(sem["sq_att"], at("sq_att", l, 1))
                for h, name in enumerate([f"sbq{h}" for h in range(4)] + ["sbk", "sik"]):
                    mm(begin(name, l)[:, 0:T], ones, sq_att[:, h, :]).then_inc(filled(name), 1)

                def gate(i, slots=(0, 1)):
                    for s in slots:
                        multiply(pe, m0 + M_GATE + i, s, r0 + R_GATE + i, halves(s, nH, nL), T)

                gate(0, [0])
                pe.wait_ge(sem["tables_in"], 16)
                pe.wait_ge(sem["gt"], at("gt", l, 1))
                ps = begin("gc", l)
                for b in (1, 2, 0):
                    n = TB[b][1]
                    t = mm(ps[0:n, 4 * b:4 * b + 4], const("upto", n, n), gg[0:n, b, :])
                t.then_inc(filled("gc"), 1)
                def decays(b):
                    n = TB[b][1]
                    for name, src, count in ((f"gb{b}", gtri, 2 + b), (f"bb{b}", bdiag, 5 + b)):
                        pe.wait_ge(sem["gt"], at("gt", l, count))
                        mm(begin(name, l)[:, 0:4 * n], ones[0:n, :], src[b].rearrange("p h c -> p (h c)")).then_inc(filled(name), 1)

                def keys_and_queries(b):
                    n = TB[b][1]
                    pe.wait_ge(sem["qk_unit"], at("qk_unit", l, 2))
                    for name, off in ((f"kk{b}", 4), (f"qk{b}", 0)):
                        ps = begin(name, l)
                        for h in range(4):
                            t = mm(ps[0:n, h * n:(h + 1) * n], cT[:, 4 + h, tok(b)], cT[:, off + h, tok(b)])
                        t.then_inc(filled(name), 1)

                decays(0)
                decays(1)
                keys_and_queries(0)
                gate(0, [1])
                decays(2)
                keys_and_queries(1)
                keys_and_queries(2)
                for b in range(3):
                    n = TB[b][1]
                    for name, off in ((f"kt{b}", 4), (f"vt{b}", 8)):
                        ps = begin(name, l)
                        if off == 8 and b == 0:
                            pe.wait_ge(sem["silu"], at("silu", l, 3))
                        for h in range(4):
                            t = nc.tensor.transpose(ps[0:n, h * P:(h + 1) * P], cT[:, off + h, tok(b)], ident)
                        t.then_inc(filled(name), 1)
                pe.wait_ge(sem["att_unit"], at("att_unit", l, 3))
                mm(begin("rk", l)[:, 0:T], const("turn_a", P), bkr[:, :]).then_inc(filled("rk"), 1)
                mm(begin("rik", l)[:, 0:T], const("turn_i", P), ikr[:, :]).then_inc(filled("rik"), 1)
                for h in range(4):
                    mm(begin(f"rq{h}", l)[:, 0:T], const("turn_a", P), rawT[:, 16 + h, :]).then_inc(filled(f"rq{h}"), 1)
                pe.wait_ge(lin_read[3], r0 + 6)
                for c in range(4):
                    mm(begin(f"ri{c}", l)[:, 0:T], const("turn_i", P), rawT[:, 20 + c, :]).then_inc(filled(f"ri{c}"), 1)
                gate(1, [0])
                for b in range(3):
                    n = TB[b][1]
                    pe.wait_ge(sem["ml"], at("ml", l, b + 1))
                    ps = begin(f"Y{b}_0", l)
                    if b == 0:
                        stand(pe, "pe_stood")
                    for h in range(4):
                        t = nc.tensor.transpose(ps[0:n, h * n:(h + 1) * n], ML[b][:, h, :], ident[0:n, 0:n])
                    t.then_inc(filled(f"Y{b}_0"), 1)
                pe.wait_ge(sem["rope"], at("rope", l, 4))
                for j in range(2):
                    if j:
                        gate(1, [1])
                    w = (j + 1) * P
                    for e, heads in enumerate(IX_HEADS[j]):
                        name = f"ix{j}{e}"
                        ps = begin(name, l)
                        for n, h in enumerate(heads):
                            r = 64 * (h % 2)
                            t = mm(ps[:, n * w:(n + 1) * w], rawT[r:r + 64, 20 + h // 2, tok(j + 1)], ikr[r:r + 64, META:META + w])
                        t.then_inc(filled(name), 1)
                def times_inverse(b, it, suffix, round_):
                    n = TB[b][1]
                    y, x_t = f"Y{b}{suffix}", f"T{b}{suffix}"
                    pe.wait_ge(sem["ml"], at("ml", l, round_ * 3 + b + 4))
                    ps = begin(y, l, it)
                    if b == 0:
                        stand(pe, "pe_stood")
                    for h in range(4):
                        t = mm(ps[0:n, h * n:(h + 1) * n], ML[b][:, h, :], X[b][:, h, :])
                    t.then_inc(filled(y), 1)
                    if b:
                        ps = begin(x_t, l, it)
                        for h in range(4):
                            t = nc.tensor.transpose(ps[:, h * P:(h + 1) * P], X[b][:, h, :], ident)
                        t.then_inc(filled(x_t), 1)

                with pe.Fori(0, LEVELS - 2) as it:
                    for b in range(3):
                        pe.wait_ge(*read(f"X{b}" if b else "XA0", l, it, 1))
                        times_inverse(b, it, "", it)
                    pe.wait_ge(*read("Y0", l, it))
                    ps = begin("XA0", l, it)
                    stand(pe, "pe_stood")
                    for h in range(4):
                        mm(ps[0:META, h * META:(h + 1) * META], A[0][:, h, :], Y[0][:, h, :])
                        t = mm(ps[0:META, (4 + h) * META:(5 + h) * META], Y[0][:, h, :], A[0][:, h, :])
                    t.then_inc(filled("XA0"), 1)
                    for b in (1, 2):
                        pe.wait_ge(*read(f"Y{b}", l, it))
                        pe.wait_ge(*read(f"T{b}", l, it))
                        ps = begin(f"X{b}", l, it)
                        for h in range(4):
                            t = mm(ps[:, h * P:(h + 1) * P], A[b][:, h, :], Y[b][:, h, :])
                        t.then_inc(filled(f"X{b}"), 1)
                for b in (1, 2):
                    pe.wait_ge(*read(f"X{b}", l, LEVELS - 3))
                    times_inverse(b, 0, "_6", LEVELS - 2)
                def scores(j):
                    if j == 0:
                        ps = begin("s0", l)
                        for h in range(4):
                            t = mm(ps[0:META, h * META:(h + 1) * META], rawT[:, 16 + h, 0:META], bkr[:, 0:META])
                        t.then_inc(filled("s0"), 1)
                        return
                    for h in range(4):
                        name = f"s{'abcd'[h]}{j}"
                        mm(begin(name, l)[:, 0:KEYS[j]], rawT[:, 16 + h, tok(j)], bkr[:, 0:KEYS[j]]).then_inc(filled(name), 1)

                scores(0)
                for b in (1, 2):
                    pe.wait_ge(*read(f"Y{b}_6", l))
                    pe.wait_ge(*read(f"T{b}_6", l))
                    ps = begin(f"A{b}", l)
                    for h in range(4):
                        t = mm(ps[:, h * P:(h + 1) * P], Y[b][:, h, :], A[b][:, h, :])
                    t.then_inc(filled(f"A{b}"), 1)

                def state_seen(b):
                    pe.wait_ge(*read(f"dS{b - 1}", l))
                    ps = begin(f"kS{b}", l)
                    for h in range(4):
                        t = mm(ps[:, h * P:(h + 1) * P], cT[:, 4 + h, tok(b)], S[:, h, :])
                    t.then_inc(filled(f"kS{b}"), 1)

                def new_values(b):
                    n = TB[b][1]
                    rhs = R if b else vt[0:n, 0]
                    if b:
                        pe.wait_ge(*read(f"kS{b}", l))
                    pe.wait_ge(sem["ab_ready"], at("ab_ready", l, b + 1))
                    ps = begin(f"vn{b}", l)
                    if b == 0:
                        stand(pe, "pe_stood")
                    for h in range(4):
                        t = mm(ps[0:n, h * P:(h + 1) * P], A[b][:, h, :], rhs[:, h, :])
                    t.then_inc(filled(f"vn{b}"), 1)

                def delta_out(b):
                    n = TB[b][1]
                    pe.wait_ge(*read(f"vn{b}", l))
                    pe.wait_ge(sem["qe"], at("qe", l, 1))
                    ps = begin(f"o{b}", l)
                    for h in range(4):
                        if b:
                            mm(ps[:, h * n:(h + 1) * n], S[:, h, :], cT[:, h, tok(b)], True, False)
                        t = mm(ps[:, h * n:(h + 1) * n], vn[0:n, h, :], QD[b][:, h, :], b == 0, True)
                    t.then_inc(filled(f"o{b}"), 1)
                    if b < 2:
                        ps = begin(f"dS{b}", l)
                        for h in range(4):
                            t = mm(ps[:, h * P:(h + 1) * P], kd[0:n, b, h, :], vn[0:n, h, :])
                        t.then_inc(filled(f"dS{b}"), 1)

                def weights_turned(j):
                    pe.wait_ge(sem["pn"], at("pn", l, 1 + j))
                    if j == 0:
                        ps = begin("pt0", l)
                        stand(pe, "pe_stood")
                        for h in range(4):
                            t = nc.tensor.transpose(ps[0:META, h * META:(h + 1) * META], P0[:, h, :], ident[0:META, 0:META])
                        t.then_inc(filled("pt0"), 1)
                        return
                    for b in range(j + 1):
                        name = f"pt{b}_{j}"
                        ps = begin(name, l)
                        for h in range(4):
                            t = nc.tensor.transpose(ps[0:TB[b][1], h * P:(h + 1) * P], Pm[:, h, tok(b)], ident)
                        t.then_inc(filled(name), 1)

                def weighted_values(j, parts=None):
                    parts = parts or tuple(range(j + 1))
                    ps = bank(f"pv{j}") if parts[0] else begin(f"pv{j}", l)
                    if j == 0:
                        pe.wait_ge(*read("pt0", l))
                        mm(ps[:, 0:4 * META], vtok[0:META, 0, :], PT[0:META, 0, 0:4 * META]).then_inc(filled("pv0"), 1)
                        return
                    for b in parts:
                        n = TB[b][1]
                        pe.wait_ge(*read(f"pt{b}_{j}", l))
                        t = mm(ps[:, :], vtok[0:n, b, :], PT[0:n, b, :], b == 0, b == j)
                    if parts[-1] == j:
                        t.then_inc(filled(f"pv{j}"), 1)

                new_values(0)
                scores(1)
                gate(2, [0])
                delta_out(0)
                weights_turned(0)
                gate(2, [1])
                state_seen(1)
                weighted_values(0)
                weights_turned(1)
                gate(3, [0])
                new_values(1)
                scores(2)
                delta_out(1)
                weighted_values(1)
                state_seen(2)
                weights_turned(2)
                new_values(2)
                weighted_values(2, (0,))
                delta_out(2)
                weighted_values(2, (1, 2))
                pe.wait_ge(sem["sqo"], at("sqo", l, 3))
                for h in range(4):
                    mm(begin(f"so{h}", l)[:, 0:T], ones, sqo[:, h, :]).then_inc(filled(f"so{h}"), 1)
                gate(3, [1])
                pe.wait_ge(*read("pv2", l))
                stand(pe, "pe_stood")
                with pe.Fori(0, 2) as i:
                    for s in range(2):
                        if s:
                            for b in range(4):
                                begin(f"br{b}", l, i)
                        multiply(pe, m0 + M_BRANCH + i, s, r0 + R_BRANCH + i,
                                 [(2 - 2 * br + c, slice(c * P, c * P + P), [(4 * br + k, oH[:, 4 * br + k, :], oL[:, 4 * br + k, :]) for k in range(4)])
                                  for br in (1, 0) for c in range(2)], T, banks=[bank(f"br{b}") for b in range(4)] if s else lin,
                                 late=(2, (sem["oa_l"], at("oa_l", l, 4))))
                    for b in range(4):
                        pe.sem_inc(filled(f"br{b}"), 1)
                multiply_first(pe, m0 + M_OUT, r0 + R_OUT, halves(0, nH, nL), T,
                               lambda pair: (sem["yh"], at("yh", l, pair + 1)), lambda pair: (sem["yl"], at("yl", l, pair + 1)), at_once=True)
                multiply(pe, m0 + M_OUT, 1, r0 + R_OUT, halves(1, nH, nL), T, behind_first=True)
                for s in range(2):
                    multiply(pe, m0 + M_OUT + 1, s, r0 + R_OUT + 1, halves(s, nH, nL), T)
                mean_square("ms2", l, 2)
                multiply_first(pe, m0 + M_UP, r0 + R_UP, halves(0, nH, nL), T, *behind_norm(l, 2))
                multiply(pe, m0 + M_UP, 1, r0 + R_UP, halves(1, nH, nL), T, behind_first=True)
                with pe.Fori(1, 11) as i:
                    for s in range(2):
                        multiply(pe, m0 + M_UP + i, s, r0 + R_UP + i, halves(s, nH, nL), T)
                with pe.Fori(0, 2) as i:
                    for p in range(6):
                        k0, n = DOWN_K[p % 3]
                        pe.wait_ge(sem["al"], at("al", l, k0 + n))
                        multiply(pe, m0 + M_DOWN + 3 * i + p // 2, p % 2, r0 + R_DOWN + i, 
                                 [(2 * (p // 3) + c, slice(c * P, c * P + P), [(k, aH[:, k0 + k, :], aL[:, k0 + k, :]) for k in range(n)])
                                  for c in range(2)], T, start=p % 3 == 0, stop=p % 3 == 2)

            with pe.Fori(0, DEPTH) as l:
                layer(l)

            L = DEPTH

            def multiply_tok(m, s, rnd):
                pe.wait_ge(sem["whi"], 4 * m + 2 * s + 2)
                for j in range(2):
                    pe.wait_ge(lin_read[2 * s + j], rnd)
                    to, rows_ = lin[2 * s + j][:, 0:PANEL], slice(j * P, j * P + P)
                    for k in range(DC):
                        mm(to, nH[:, k, rows_], wH[:, s, k, :], k == 0, False)
                        t = mm(to, nL[:, k, rows_], wH[:, s, k, :], False, False)
                t.then_inc(sem["whi_used"], 1)
                pe.wait_ge(sem["wlo"], 4 * m + 2 * s + 6)
                for j in range(2):
                    for k in range(DC):
                        t = mm(lin[2 * s + j][:, 0:PANEL], nH[:, k, j * P:j * P + P], wL[:, s, k, :], False, k == DC - 1)
                t.then_inc(sem["panel_done"], 1)

            nH2, nL2 = nH[:, :, 0:SEQ], nL[:, :, 0:SEQ]

            def mean_square2(name, which):
                ps = begin(name, L)
                for c in range(DC):
                    if c % 2 == 0:
                        pe.wait_ge(*((sem["sq"], at("sq", L, c // 2 + 1)) if which == 1 else (sem["sq2"], 4 * (which - 2) + c // 2 + 1)))
                    t = mm(ps[:, 0:SEQ], ones, sq8[:, c, META:T] if which == 1 else sqf[:, c, :], c == 0, c == DC - 1)
                t.then_inc(filled(name), 1)

            def first_pair(which, m, r):
                multiply_first(pe, m, r, halves(0, nH2, nL2), SEQ, lambda pair: (sem["nh2"], 4 * (which - 1) + pair + 1),
                               lambda pair: (sem["nl2"], 4 * (which - 1) + pair + 1))
                multiply(pe, m, 1, r, halves(1, nH2, nL2), SEQ, behind_first=True)

            def mlp2(name, which, m, r):
                mean_square2(name, which)
                first_pair(which, m, r)
                with pe.Fori(1, 11) as i:
                    for s in range(2):
                        multiply(pe, m + i, s, r + i, halves(s, nH2, nL2), SEQ)
                with pe.Fori(0, 2) as i:
                    for p in range(6):
                        k0, n = DOWN_K[p % 3]
                        pe.wait_ge(sem["al2"], FC * (which // 2 - 1) + k0 + n)
                        multiply(pe, m + 11 + 3 * i + p // 2, p % 2, r + 11 + i,
                                 [(2 * (p // 3) + c, slice(c * P, c * P + P), [(k, aH2[:, k0 + k, :], aL2[:, k0 + k, :]) for k in range(n)])
                                  for c in range(2)], SEQ, start=p % 3 == 0, stop=p % 3 == 2)

            mean_square2("ems", 1)
            first_pair(1, M_E, R_E)

            def even(i, s):
                multiply(pe, M_E + i, s, R_E + i, halves(s, nH2, nL2), SEQ)

            def even_scores(j):
                keys = (j + 1) * P
                for e, heads in enumerate([(0, 2, 4, 6), (1, 3, 5, 7)] if j == 0 else [(0, 2), (1, 3), (4, 6), (5, 7)]):
                    name = f"e{j}{e}"
                    ps = begin(name, L)
                    for n, h in enumerate(heads):
                        r = 64 * (h % 2)
                        t = mm(ps[:, n * keys:(n + 1) * keys], raw8[r:r + 64, h // 2, j * P:j * P + P], raw8[r:r + 64, 4 + h // 2, 0:keys])
                    t.then_inc(filled(name), 1)

            def even_turned(j):
                pe.wait_ge(sem["epn"], 1 + j)
                src = Pe if j else Pe0
                for g in range(2):
                    for b in range(j + 1):
                        name = f"et{j}{g}" + (str(b) if j else "")
                        ps = begin(name, L)
                        for h in range(4):
                            t = nc.tensor.transpose(ps[:, h * P:(h + 1) * P], src[:, 4 * g + h, b * P:b * P + P], ident)
                        t.then_inc(filled(name), 1)

            def even_values(j):
                for name in ("et100", "et101", "et110", "et111") if j else ("et00", "et01"):
                    pe.wait_ge(*read(name, L))
                for b in range(4):
                    pe.wait_ge(lin_read[b], R_E + 5)
                ps = begin(f"ev{j}", L)
                for h in range(8):
                    r = 64 * (h % 2)
                    for b in range(j + 1):
                        t = mm(ps[r:r + 64, (h // 2) * P:(h // 2 + 1) * P], vtk[:, b, h * 64:h * 64 + 64], PTe[:, b, h * P:(h + 1) * P], b == 0, b == j)
                t.then_inc(filled(f"ev{j}"), 1)

            for s in range(2):
                even(1, s)
            even(2, 0)
            pe.wait_ge(sem["esq"], 2)
            for c in range(4):
                mm(begin(f"eq{c}", L)[:, :], const("half", P), sqe[:, 2 * c:2 * c + 2, :].rearrange("p c t -> p (c t)")).then_inc(filled(f"eq{c}"), 1)
            even(2, 1)
            even(3, 0)
            pe.wait_ge(sem["eunit"], 2)
            even_scores(0)
            even_scores(1)
            even(3, 1)
            multiply_tok(M_E + 4, 0, R_E + 4)
            even_turned(0)
            multiply_tok(M_E + 4, 1, R_E + 4)
            even_values(0)
            even(5, 0)
            even_turned(1)
            even_values(1)
            even(5, 1)
            def branch_ready(pair):
                return read("ev1", L) if pair < 2 else (sem["eb_l"], pair - 1)

            multiply_first(pe, M_E + E_OUT, R_E + E_OUT, halves(0, eH, eL), SEQ, branch_ready, branch_ready, at_once=True)
            multiply(pe, M_E + E_OUT, 1, R_E + E_OUT, halves(1, eH, eL), SEQ, behind_first=True)
            for s in range(2):
                multiply(pe, M_E + E_OUT + 1, s, R_E + E_OUT + 1, halves(s, eH, eL), SEQ)
            mlp2("emf", 2, M_E + E_UP, R_E + E_UP)

            mean_square2("oms", 3)
            first_pair(3, M_O, R_O)
            with pe.Fori(1, 4) as i:
                for s in range(2):
                    multiply(pe, M_O + i, s, R_O + i, halves(s, nH2, nL2), SEQ)
            with pe.Fori(O_V, O_G) as i:
                for s in range(2):
                    multiply_tok(M_O + i, s, R_O + i)
            pe.wait_ge(sem["orot"], 4)
            for b in range(4):
                pe.wait_ge(lin_read[b], R_O + O_G)
            for h in range(4):
                ps = begin(f"os{h}", L)
                for b in range(2):
                    to = ps[:, 0:SEQ] if b == 0 else ps[:, SEQ:SEQ + P]
                    for d in range(2):
                        t = mm(to, qk2[:, 1, h, d, b * P:b * P + P], qk2[:, 0, h, d, b * P:SEQ], d == 0, d == 1)
                t.then_inc(filled(f"os{h}"), 1)
            def odd_g(i, s):
                multiply(pe, M_O + O_G + i, s, R_O + O_G + i, halves(s, nH2, nL2), SEQ)

            odd_g(0, 0)
            for h in range(4):
                pe.wait_ge(*read(f"os{h}", L))
                for e in range(2):
                    name = f"oo{h}{e}"
                    ps = begin(name, L)
                    for n in range(2):
                        cols = slice(h * 512 + (2 * e + n) * P, h * 512 + (2 * e + n + 1) * P)
                        mm(ps[:, n * SEQ:(n + 1) * SEQ], vtk2[:, 0, cols], sc[:, h, 0:SEQ], True, False)
                        t = mm(ps[:, n * SEQ + P:(n + 1) * SEQ], vtk2[:, 1, cols], sc[:, h, SEQ:SEQ + P], False, True)
                    t.then_inc(filled(name), 1)
            odd_g(0, 1)
            for h in range(4):
                pe.wait_ge(sem["osq"], h + 1)
                ps = begin(f"ow{h}", L)
                for e in range(4):
                    t = mm(ps[:, 0:SEQ], ones, sq16[:, 4 * h + e, :], e == 0, e == 3)
                t.then_inc(filled(f"ow{h}"), 1)
            for i in range(1, 4):
                for s in range(2):
                    odd_g(i, s)
            with pe.Fori(0, 2) as i:
                for q in range(2):
                    for s in range(2):
                        pe.wait_ge(sem["og_l"], 2 * s + 2)
                        multiply(pe, M_O + O_OUT + 2 * i + q, s, R_O + RO_OUT + i,
                                 [(2 * q + c, slice(c * P, c * P + P), [(k, gH[:, 8 * s + k, :], gL[:, 8 * s + k, :]) for k in range(DC)])
                                  for c in range(2)], SEQ, start=s == 0, stop=s == 1)
            mlp2("omf", 4, M_O + O_UP, R_O + RO_UP)
            for j in range(2):
                for q in range(2):
                    b = 2 * j + q
                    pe.wait_ge(lin_read[3], R_ALL)
                    for c in range(4):
                        t = nc.tensor.transpose(lin[b][:, c * P:(c + 1) * P], hT[:, 4 * q + c, META + j * P:META + (j + 1) * P], ident)
                    t.then_inc(sem["turned_back"], 1)

        @block.scalar
        def _(act):
            own = Own(act, sem["act_own"])
            Exp, Ln, Copy, Square, Silu, Relu = ACT.Exp, ACT.Ln, ACT.Copy, ACT.Square, ACT.Silu, ACT.Relu
            f = nc.scalar.activation
            EXP_LN, SILU = "natural_log_exp_and_others", "silu_and_others"
            act.preload_act_table_set(EXP_LN)
            act.wait_ge(sem["cleared"], 1)

            def row(t, r, src, n, cols=slice(0, P)):
                act.dma_start(rows[r:r + n, 0:DEPTH, t, cols], src).then_inc(sem["rows"], 16)

            row(0, K_CONV, a["conv_a"].rearrange("l k (c p) -> (k c) l p", p=P), 48)
            row(0, K_NORM1, a["norm_mix"].rearrange("l (c p) -> c l p", p=P), DC)
            row(0, K_NORM2, a["norm_ffn"].rearrange("l (c p) -> c l p", p=P), DC)
            for r, name in ((K_ANORM, "a_out_norm"), (K_QN, "q_norm"), (K_KN, "k_norm")):
                row(0, r, a[name].unsqueeze(0), 1)
            for half in range(2):
                row(0, K_IN, a["kidx_norm"].unsqueeze(0), 1, slice(64 * half, 64 * half + 64))
            row(0, K_BG, a["b_gate"].rearrange("l (c p) -> c l p", p=P), 16)
            row(1, 0, a["conv_ffn"].rearrange("l k (c p) -> (k c) l p", p=P), 66)
            for n, name in enumerate(("dt_bias", "a_log")):
                act.dma_start(rates[:, :, 4 * n:4 * n + 4], a[name].unsqueeze(0).to_broadcast([P, DEPTH, 4])).then_inc(sem["rows"], 16)
            parameter_rows2(act, 1)
            act.dma_start(c1[:, early:n1], a["c1"][:, early:n1]).then_inc(sem["tables_in"], 16)

            def square(pair):
                two = ds(2 * pair, 2)
                return f(sq8[:, two, :], hT[:, two, :], Square)

            def parameters(l):
                act.wait_ge(sem["turned"], DC + 1 + l)
                f(par[:, l, :], lin[l][:, 0:2 * P], Copy).then_inc(sem["par_in"], 1)

            for l in range(DEPTH):
                parameters(l)
            f(rates[:, :, 4:8], rates[:, :, 4:8], Exp).then_inc(sem["par_in"], 1)
            split_hi(act, 0, 0)
            for l in range(DEPTH, 2 * DEPTH):
                parameters(l)
            split_hi(act, 0, 1)

            def norm(l, which, name):
                act.wait_ge(*full(name, l))
                f(rs[:, :], bank(name)[:, 0:T], Ln, bias=eps_col, scale=1.0 / D).then_inc(emptied(name), 1)
                act.wait_ge(*read(name, l))
                f(rs[:, :], rs[:, :], Exp, scale=-0.5).then_inc(sem["rstd"], 1)
                for pair in range(1, DC // 2):
                    act.wait_ge(sem["n"], at("n", l, DC * (which - 1) + 2 * pair))
                    f(nH[:, 2 * pair:2 * pair + 2, :], nT[:, 2 * pair:2 * pair + 2, :], Copy).then_inc(sem["nh"], 1)

            def layer(l):
                own.base, own.n = l * PER["act_own"], 0
                m0, r0 = l * M_LAYER, l * R_LAYER
                norm(l, 1, "ms1")
                act.preload_act_table_set(SILU)

                def w_in(i, to, func=Copy):
                    for s in range(2):
                        split_hi(act, m0 + i + 1, s)
                        act.wait_ge(sem["panel_done"], 2 * (m0 + i) + s + 3)
                        for c in range(2):
                            b = 2 * s + c
                            f(to(b), lin[b][:, 0:T].unsqueeze(1), func).then_inc(lin_read[b], 1)

                def group_silu(g):
                    act.wait_ge(sem["conv"], at("conv", l, 4 * g + 4))
                    qkv = cT[:, ds(4 * g, 4), :]
                    f(qkv, qkv, Silu).then_inc(sem["silu"], 1)

                def group_square(g):
                    act.wait_ge(sem["silu"], at("silu", l, g + 1))
                    f(sqh[:, ds(4 * g, 4), :], cT[:, ds(4 * g, 4), :], Square).then_inc(sem["sq_heads"], 1)

                w_in(0, lambda b: rawT[:, b:b + 1, :])
                for name, to in (("ik", ikr), ("bk", bkr)):
                    act.wait_ge(*full(name, l))
                    f(to[:, :], bank(name)[:, 0:T], Copy).then_inc(emptied(name), 1)
                act.wait_ge(*full("tk", l))
                n = S_ALL - S_BV
                for to, of, width in ((vtok, 0, P), (ab, S_AB - S_BV, 16)):
                    own.done(f(to[0:META, 0, :], bank("tk")[0:META, of:of + width], Copy))
                    t = f(to[:, 1:3, :], bank("tk")[:, n:3 * n].rearrange("p (b n) -> p b n", b=2)[:, :, of:of + width], Copy)
                t.then_inc(emptied("tk"), 1)
                with act.Fori(1, 3) as i:
                    w_in(i, lambda b: rawT[:, ds(4 * i + b, 1), :])
                    group_silu(i - 1)
                    group_square(i - 1)
                w_in(3, lambda b: zT[:, b:b + 1, :], Silu)
                group_silu(2)
                act.preload_act_table_set(EXP_LN)
                w_in(4, lambda b: rawT[:, 16 + b:17 + b, :])
                for b in range(4):
                    act.wait_ge(lin_read[b], r0 + 5)
                f(sq_att[:, 0:4, :], rawT[:, 16:20, :], Square)
                act.wait_ge(*read("bk", l))
                f(sq_att[:, 4, :], bkr[:, :], Square)
                f(sq_att[:, 5, :], ikr[:, :], Square).then_inc(sem["sq_att"], 1)
                w_in(5, lambda b: rawT[:, 20 + b:21 + b, :])
                act.wait_ge(sem["sp_in"], at("sp_in", l, 1))
                own.done(f(gl[:, :, :], gm[:, :, :], Exp))
                own.wait()
                f(gl[:, :, :], gl[:, :, :], Ln, bias=one_col)
                f(bt[:, :, :], ab[:, :, 4:8], Exp, scale=-1.0).then_inc(sem["sp_ln"], 1)
                roots = (
                    ([f"ssq{h}" for h in range(4)], rnq, 1.0, lnq_col),
                    ([f"ssk{h}" for h in range(4)], rnk, 1.0, 0.0),
                    ([f"sbq{h}" for h in range(4)] + ["sbk"], rnb, 1.0 / P, 0.0),
                    (["sik"], rni, 1.0 / P, 0.0),
                )
                for names, to, scale, bias_ in roots:
                    for h, name in enumerate(names):
                        act.wait_ge(*full(name, l))
                        f(to[:, h, :], bank(name)[:, 0:T], Ln, bias=eps_col, scale=scale).then_inc(emptied(name), 1)
                for names, to, scale, bias_ in roots:
                    act.wait_ge(*read(names[-1], l))
                    f(to[:, :, :], to[:, :, :], Exp, scale=-0.5, bias=bias_).then_inc(sem["rn"], 1)

                def gate_hi(i, slots=(0, 1)):
                    for s in slots:
                        split_hi(act, m0 + M_GATE + i + 1, s)

                def gate(i):
                    x = rawT[:, 4 * i:4 * i + 4, :]
                    for b in range(4):
                        act.wait_ge(lin_read[b], r0 + R_GATE + i + 1)
                    f(x, x, Exp, scale=-1.0).then_inc(sem["gates"], 1)
                    act.wait_ge(sem["gates"], at("gates", l, 3 * i + 1))
                    f(x, x, Ln, bias=one_col).then_inc(sem["gates"], 1)
                    act.wait_ge(sem["gates"], at("gates", l, 3 * i + 2))
                    f(x, x, Exp, scale=-1.0).then_inc(sem["gates"], 1)

                gate_hi(0, [0])
                act.wait_ge(*full("gc", l))
                own.done(f(gcs[0:META, 0, :], bank("gc")[0:META, 0:4], Copy))
                f(gcs[:, 1:3, :], bank("gc")[:, 4:12].rearrange("p (b h) -> p b h", b=2), Copy).then_inc(emptied("gc"), 1)
                act.wait_ge(*read("gc", l))
                f(egt[:, :, :], gcs[:, :, :], Exp).then_inc(sem["eg"], 1)
                for b in range(3):
                    n = TB[b][1]
                    if b == 2:
                        gate_hi(0, [1])
                    act.wait_ge(*full(f"gb{b}", l))
                    f(eg[:, :, tok(b)], bank(f"gb{b}")[:, 0:4 * n].rearrange("p (h c) -> p h c", h=4), Exp).then_inc(sem["eg"], 1)
                    act.wait_ge(*read(f"gb{b}", l))
                    f(decay[b], decay[b], Exp).then_inc(sem["dec"], 1)
                f(kdx[:, :, :], kdx[:, :, :], Exp).then_inc(sem["kdx"], 1)
                for b in range(3):
                    n = TB[b][1]
                    act.wait_ge(*full(f"vt{b}", l))
                    f(vt[0:n, b], bank(f"vt{b}")[0:n, :].rearrange("p (h d) -> p h d", h=4), Copy).then_inc(emptied(f"vt{b}"), 1)
                gate(0)
                gate_hi(1, [0])
                for j in range(2):
                    if j:
                        gate_hi(1, [1])
                    for e in range(len(IX_HEADS[j])):
                        name = f"ix{j}{e}"
                        act.wait_ge(*full(name, l))
                        if 2 * j + e >= 2:
                            act.wait_ge(sem["score"], at("score", l, 2 * j + e - 1))
                        f(rl[:, e % 2, :], bank(name)[:, :], Relu).then_inc(emptied(name), 1)
                def inverse_read(name, to, n, it=0):
                    act.wait_ge(*full(name, l, it))
                    f(to, bank(name)[0:n, 0:4 * n].rearrange("p (h c) -> p h c", h=4), Copy).then_inc(emptied(name), 1)

                with act.Fori(0, LEVELS - 2) as it:
                    inverse_read("Y0", Y[0], META, it)
                    for b in (1, 2):
                        inverse_read(f"Y{b}", Y[b], P, it)
                        inverse_read(f"T{b}", A[b], P, it)
                for b in (1, 2):
                    inverse_read(f"Y{b}_6", Y[b], P)
                    inverse_read(f"T{b}_6", A[b], P)
                def new_values(b):
                    n = TB[b][1]
                    act.wait_ge(*full(f"vn{b}", l))
                    f(vn[0:n], bank(f"vn{b}")[0:n, :].rearrange("p (h d) -> p h d", h=4), Copy).then_inc(emptied(f"vn{b}"), 1)

                def delta_out(b):
                    act.wait_ge(sem["qe"], at("qe", l, 1))
                    act.wait_ge(*full(f"o{b}", l))
                    ps = bank(f"o{b}")[:, 0:4 * TB[b][1]].rearrange("p (h c) -> p h c", h=4)
                    f(sqo[:, :, tok(b)], ps, Square).then_inc(sem["sqo"], 1)
                    f(oA[:, :, tok(b)], ps, Copy).then_inc(emptied(f"o{b}"), 1)

                def softmax(j):
                    n = P if j else META
                    act.wait_ge(sem["nmx"], at("nmx", l, 1 + j))
                    for h in range(4):
                        src, to = (Pm[:, h, 0:KEYS[j]], Pm[:, h, 0:KEYS[j]]) if j else (bank("s0")[0:META, h * META:(h + 1) * META], P0[:, h, :])
                        e = f(to, src, Exp, scale=P ** -0.5, bias=nmx[0:n, j, h:h + 1], accum_out=sm[0:n, j, h:h + 1])
                    e.then_inc(sem["soft"] if j else emptied("s0"), 1)

                def weights_turned(j):
                    for b in range(j + 1):
                        n, w = TB[b][1], 4 * TB[j][1]
                        name = f"pt{b}_{j}" if j else "pt0"
                        act.wait_ge(*full(name, l))
                        f(PT[0:n, b, 0:w], bank(name)[0:n, 0:w], Copy).then_inc(emptied(name), 1)

                def weighted_values(j):
                    act.wait_ge(*full(f"pv{j}", l))
                    f(oH[:, 4:8, tok(j)], bank(f"pv{j}")[:, 0:4 * TB[j][1]].rearrange("p (h c) -> p h c", h=4), Copy).then_inc(sem["ob_h"], 1)

                softmax(0)
                new_values(0)
                softmax(1)
                gate_hi(2, [0])
                delta_out(0)
                weights_turned(0)
                gate(1)
                gate_hi(2, [1])
                weighted_values(0)
                weights_turned(1)
                gate_hi(3, [0])
                new_values(1)
                gate(2)
                softmax(2)
                delta_out(1)
                weighted_values(1)
                weights_turned(2)
                new_values(2)
                delta_out(2)
                weighted_values(2)
                for h in range(4):
                    act.wait_ge(*full(f"so{h}", l))
                    f(rno[:, h, :], bank(f"so{h}")[:, 0:T], Ln, bias=eps_col, scale=1.0 / P).then_inc(emptied(f"so{h}"), 1)
                for h in range(4):
                    act.wait_ge(*read(f"so{h}", l))
                    f(rno[:, h, :], rno[:, h, :], Exp, scale=-0.5).then_inc(sem["rno"], 1)
                for h in range(4):
                    act.wait_ge(sem["oa"], at("oa", l, h + 1))
                    f(oH[:, h, :], zT[:, h, :], Copy).then_inc(sem["oa_h"], 1)
                gate_hi(3, [1])
                gate(3)
                with act.Fori(0, 2) as i:
                    for s in range(2):
                        split_hi(act, m0 + M_BRANCH + i + 1, s)
                        act.wait_ge(sem["y"], at("y", l, 4 * i + 2 * s + 2))
                        two = ds(4 * i + 2 * s, 2)
                        f(nH[:, two, :], yT[:, two, :], Copy).then_inc(sem["yh"], 1)
                with act.Fori(0, 2) as i:
                    for s in range(2):
                        split_hi(act, m0 + M_OUT + i + 1, s)
                        for c in range(2):
                            act.wait_ge(lin_read[2 * s + c], r0 + R_OUT + i + 1)
                        square(2 * i + s).then_inc(sem["sq"], 1)
                norm(l, 2, "ms2")
                act.preload_act_table_set(SILU)
                with act.Fori(0, 11) as i:
                    m, r = m0 + M_UP + i, r0 + R_UP + i
                    split_hi(act, m + 1, 0)
                    act.wait_ge(sem["panel_done"], 2 * m + 3)
                    for c in range(2):
                        f(u[:, c, :], lin[c][:, 0:T], Copy, scale=parL[:, ds(K_FCONV + 2 * FC + 2 * i + c, 1)]).then_inc(sem["tap"], 1)
                    split_hi(act, m + 1, 1)
                    for c in range(2):
                        act.wait_ge(lin_read[c], r + 1)
                        f(sg[:, c, :], u[:, c, :], Silu).then_inc(sem["gate_silu"], 1)
                    for c in range(2):
                        act.wait_ge(lin_read[2 + c], r + 1)
                        f(aH[:, ds(2 * i + c, 1), :], av[:, c, :].unsqueeze(1), Copy).then_inc(sem["ah"], 1)
                act.preload_act_table_set(EXP_LN)
                with act.Fori(0, 2) as i:
                    for p in range(6):
                        split_hi(act, m0 + M_DOWN + 3 * i + p // 2 + 1, p % 2)
                        if p % 3 == 2:
                            for c in range(2):
                                act.wait_ge(lin_read[2 * (p // 3) + c], r0 + R_DOWN + i + 1)
                            square(2 * i + p // 3).then_inc(sem["sq"], 1)
                assert own.n == PER["act_own"], own.n

            with act.Fori(0, DEPTH) as l:
                layer(l)

            L = DEPTH
            own.base, own.n = L * PER["act_own"], 0
            def square2(pair):
                two = ds(2 * pair, 2)
                f(sqf[:, two, :], hT[:, two, META:T], Square).then_inc(sem["sq2"], 1)

            def norm2(which, name):
                act.wait_ge(*full(name, L))
                f(rs[:, 0:SEQ], bank(name)[:, 0:SEQ], Ln, bias=eps_col, scale=1.0 / D).then_inc(emptied(name), 1)
                act.wait_ge(*read(name, L))
                f(rs[:, 0:SEQ], rs[:, 0:SEQ], Exp, scale=-0.5).then_inc(sem["rstd2"], 1)
                for pair in range(1, DC // 2):
                    act.wait_ge(sem["n2"], DC * (which - 1) + 2 * pair)
                    two = slice(2 * pair, 2 * pair + 2)
                    f(nH[:, two, 0:SEQ], nT2[:, two, :], Copy).then_inc(sem["nh2"], 1)

            def take(m, s, to, func=Copy, at_once=False):
                if not at_once:
                    split_hi(act, m + 1, s)
                act.wait_ge(sem["panel_done"], 2 * m + s + 3)
                for c in range(2):
                    f(to(c), lin[2 * s + c][:, 0:SEQ].unsqueeze(1), func).then_inc(lin_read[2 * s + c], 1)
                if at_once:
                    split_hi(act, m + 1, s)

            def mlp2(j, m, r, last):
                which = 2 * j + 2
                norm2(which, ("emf", "omf")[j])
                t2 = (KE_T2, KO_T2)[j]
                act.preload_act_table_set(SILU)

                def rounded(i):
                    for c in range(2):
                        act.wait_ge(sem["conv2"], j * FC + 2 * i + c + 1)
                        f(aH2[:, ds(2 * i + c, 1), :], av2[:, c, :].unsqueeze(1), Copy).then_inc(sem["ah2"], 1)

                def up(i, first):
                    for s in range(2):
                        split_hi(act, m + i + 1, s)
                        act.wait_ge(sem["panel_done"], 2 * (m + i) + s + 3)
                        if s == 0 and not first:
                            act.wait_ge(sem["silu2"], j * FC + 2 * i)
                        for c in range(2):
                            f(u2[:, 2 * s + c, :], lin[2 * s + c][:, 0:SEQ], Copy,
                              scale=par[:, DEPTH + j, ds(t2 + s * FC + 2 * i + c, 1)]).then_inc(sem["tap2"], 1)
                        if s == 0 and not first:
                            rounded(i - 1)
                    for c in range(2):
                        act.wait_ge(lin_read[c], r + i + 1)
                        f(sg2[:, c, :], u2[:, c, :], Silu).then_inc(sem["silu2"], 1)

                up(0, True)
                with act.Fori(1, 11) as i:
                    up(i, False)
                rounded(10)
                act.preload_act_table_set(EXP_LN)
                if last:
                    for p in range(10):
                        split_hi(act, m + 11 + p // 2 + 1, p % 2)
                else:
                    with act.Fori(0, 2) as i:
                        for p in range(6):
                            split_hi(act, m + 11 + 3 * i + p // 2 + 1, p % 2)
                            if p % 3 == 2:
                                for c in range(2):
                                    act.wait_ge(lin_read[2 * (p // 3) + c], r + 11 + i + 1)
                                square2(2 * i + p // 3)

            norm2(1, "ems")
            for i in range(2):
                for s in range(2):
                    take(M_E + i, s, lambda c: raw8[:, 4 * i + 2 * s + c, :].unsqueeze(1))
                for b in range(4):
                    act.wait_ge(lin_read[b], R_E + i + 1)
                f(sqe[:, 4 * i:4 * i + 4, :], raw8[:, 4 * i:4 * i + 4, :], Square).then_inc(sem["esq"], 1)
            take(M_E + 2, 0, lambda c: ght[:, c, :].unsqueeze(1))
            for c in range(4):
                act.wait_ge(*full(f"eq{c}", L))
                f(rne[:, 2 * c:2 * c + 2, :], bank(f"eq{c}")[:, :].rearrange("p (c t) -> p c t", c=2), Ln, bias=eps_col, scale=1.0 / 64).then_inc(emptied(f"eq{c}"), 1)
            for n in range(2):
                act.wait_ge(*read(f"eq{2 * n}", L))
                act.wait_ge(*read(f"eq{2 * n + 1}", L))
                f(rne[:, 4 * n:4 * n + 4, :], rne[:, 4 * n:4 * n + 4, :], Exp, scale=-0.5).then_inc(sem["ern"], 1)
            take(M_E + 2, 1, lambda c: ght[:, 2 + c, :].unsqueeze(1))

            def even_exp(j):
                x = Pe if j else Pe0
                act.wait_ge(sem["enmx"], 1 + j)
                for h in range(8):
                    e = f(x[:, h, :], x[:, h, :], Exp, scale=0.125, bias=nmx8[:, j, h:h + 1])
                e.then_inc(sem["esoft"], 1)

            def even_turned(j):
                for g in range(2):
                    for b in range(j + 1):
                        name = f"et{j}{g}" + (str(b) if j else "")
                        act.wait_ge(*full(name, L))
                        f(PTe[:, b, g * 512:(g + 1) * 512], bank(name)[:, :], Copy).then_inc(emptied(name), 1)

            def even_values(j):
                act.wait_ge(*full(f"ev{j}", L))
                f(eH[:, 0:4, j * P:j * P + P], bank(f"ev{j}")[:, :].rearrange("p (c t) -> p c t", c=4), Copy).then_inc(sem["eob_h"], 1)

            split_hi(act, M_E + 4, 0)
            even_exp(0)
            even_exp(1)
            split_hi(act, M_E + 4, 1)
            even_turned(0)
            for s in range(2):
                take(M_E + 4, s, lambda c: vtk[:, c:c + 1, s * PANEL:(s + 1) * PANEL], at_once=s == 1)
            even_values(0)
            even_turned(1)
            split_hi(act, M_E + 6, 0)
            even_values(1)
            for s in range(2):
                if s:
                    split_hi(act, M_E + 6, 1)
                for c in range(2):
                    act.wait_ge(lin_read[2 * s + c], R_E + 6)
                f(eH[:, 4 + 2 * s:6 + 2 * s, :], cvt[:, 2 * s:2 * s + 2, :], Copy).then_inc(sem["eb_h"], 1)
            with act.Fori(0, 2) as i:
                for s in range(2):
                    split_hi(act, M_E + E_OUT + i + 1, s)
                    for c in range(2):
                        act.wait_ge(lin_read[2 * s + c], R_E + E_OUT + i + 1)
                    square2(2 * i + s)
            mlp2(0, M_E + E_UP, R_E + E_UP, False)

            norm2(3, "oms")
            with act.Fori(0, 2) as i:
                for s in range(2):
                    take(M_O + i, s, lambda c: qk2[:, 0, ds(2 * i + s, 1), c, :])
            with act.Fori(0, 2) as i:
                for s in range(2):
                    take(M_O + O_K + i, s, lambda c: qk2[:, 1, ds(2 * i + s, 1), c, :])
            with act.Fori(0, 4) as i:
                for s in range(2):
                    take(M_O + O_V + i, s, lambda c: vtk2[:, c:c + 1, ds(i * 512 + s * PANEL, PANEL)], at_once=s == 1)
            def odd_g(i, s):
                take(M_O + O_G + i, s, lambda c: sgT[:, 4 * i + 2 * s + c, :].unsqueeze(1), Silu)

            def odd_out(h):
                act.wait_ge(sem["ogate"], h + 1)
                f(gH[:, 4 * h:4 * h + 4, :], oR[:, 4 * h:4 * h + 4, :], Copy).then_inc(sem["og_h"], 1)

            act.preload_act_table_set(SILU)
            odd_g(0, 0)
            for h in range(4):
                for e in range(2):
                    name = f"oo{h}{e}"
                    act.wait_ge(*full(name, L))
                    f(oR[:, 4 * h + 2 * e:4 * h + 2 * e + 2, :], bank(name)[:, :].rearrange("p (c t) -> p c t", c=2), Copy).then_inc(emptied(name), 1)
            for h in range(4):
                for e in range(2):
                    act.wait_ge(*read(f"oo{h}{e}", L))
                f(sq16[:, 4 * h:4 * h + 4, :], oR[:, 4 * h:4 * h + 4, :], Square).then_inc(sem["osq"], 1)
            odd_g(0, 1)
            act.preload_act_table_set(EXP_LN)
            for h in range(4):
                act.wait_ge(*full(f"ow{h}", L))
                f(rn4[:, h, :], bank(f"ow{h}")[:, 0:SEQ], Ln, bias=eps_col, scale=1.0 / 512).then_inc(emptied(f"ow{h}"), 1)
            for h in range(4):
                act.wait_ge(*read(f"ow{h}", L))
                f(rn4[:, h, :], rn4[:, h, :], Exp, scale=-0.5).then_inc(sem["ovar"], 1)
            act.preload_act_table_set(SILU)
            odd_g(1, 0)
            odd_g(1, 1)
            odd_out(0)
            odd_g(2, 0)
            odd_out(1)
            odd_g(2, 1)
            odd_g(3, 0)
            odd_out(2)
            odd_g(3, 1)
            odd_out(3)
            act.preload_act_table_set(EXP_LN)
            with act.Fori(0, 2) as i:
                for q in range(2):
                    for s in range(2):
                        split_hi(act, M_O + O_OUT + 2 * i + q + 1, s)
                    for c in range(2):
                        act.wait_ge(lin_read[2 * q + c], R_O + RO_OUT + i + 1)
                    square2(2 * i + q)
            mlp2(1, M_O + O_UP, R_O + RO_UP, True)
            for b in range(4):
                act.wait_ge(sem["turned_back"], b + 1)
                f(outT[:, b // 2, (b % 2) * 512:(b % 2) * 512 + 512], lin[b][:, :], Copy).then_inc(sem["out_ready"], 1)

        @block.vector
        def _(dve):
            own = Own(dve, sem["dve_own"])
            v = nc.vector
            dve.sem_inc(sem["wlo"], 4)
            v.memset(rows[:, :, :, :], 0.0).then_inc(sem["cleared"], 1)
            for x in (ab, gcs, kdx):
                v.memset(x[:, 0:1, :], 0.0)
            v.memset(bias[:, :, 0:META], 0.0).then_inc(sem["cleared"], 1)
            for c in range(DC):
                dve.wait_ge(sem["turned"], c + 1)
                v.tensor_copy(hT[:, c, :], lin[c % 4][:, 0:T]).then_inc(sem["h0"], 1)
            for pair in range(DC // 2):
                two = slice(2 * pair, 2 * pair + 2)
                dve.wait_ge(sem["h0"], 2 * pair + 2)
                v.tensor_tensor(sq8[:, two, :], hT[:, two, :], hT[:, two, :], ALU.mult).then_inc(sem["sq"], 1)
            split_lo(dve, 0, 0)
            dve.wait_ge(sem["par_in"], DEPTH + 1)
            v.tensor_scalar(rates[:, :, 4:8], rates[:, :, 4:8], -1.0, None, ALU.mult).then_inc(sem["cleared"], 1)
            dve.wait_ge(sem["cleared"], 3)

            def norm(l, which, gain):
                dve.wait_ge(sem["rstd"], at("rstd", l, which))
                for c in range(2):
                    ins = v.scalar_tensor_tensor(nH[:, c, :], hT[:, c, :], pc(gain + c), rs[:, :], ALU.mult, ALU.mult)
                ins.then_inc(sem["nh"], 1)
                for c in (*range(2, DC), 0, 1):
                    v.scalar_tensor_tensor(nT[:, c, :], hT[:, c, :], pc(gain + c), rs[:, :], ALU.mult, ALU.mult).then_inc(sem["n"], 1)
                dve.wait_ge(sem["n"], at("n", l, DC * which))
                for pair in range(DC // 2):
                    dve.wait_ge(sem["nh"], at("nh", l, 4 * (which - 1) + pair + 1))
                    gs = slice(2 * pair, 2 * pair + 2)
                    v.tensor_tensor(nL[:, gs, :], nT[:, gs, :], nH[:, gs, :].bitcast(F32), ALU.subtract).then_inc(sem["nl"], 1)

            def layer(l):
                own.base, own.n = l * PER["dve_own"], 0
                m0, r0 = l * M_LAYER, l * R_LAYER
                own.done(v.tensor_copy(parL[:, 0:2 * P].unsqueeze(1), par[:, ds(l, 1), :]))
                own.done(v.tensor_copy(parL[:, K_DT:K_DT + 8].unsqueeze(1), rates[:, ds(l, 1), :]))
                own.wait()
                norm(l, 1, K_NORM1)
                dve.wait_ge(sem["wlo"], 4 * m0 + 8)
                dve.wait_ge(sem["tables_in"], 16)
                stand(dve, "dve_stood")
                start = own.n
                with dve.Fori(0, 3) as i:
                    own.base, own.n = l * PER["dve_own"] + i * 12, start
                    for s in range(2):
                        split_lo(dve, m0 + i + 1, s)
                    for tap in range(4):
                        for c in range(4):
                            raw, acc = rawT[:, ds(4 * i + c, 1), :], cT[:, ds(4 * i + c, 1), :]
                            w = parL[:, ds(K_CONV + (3 - tap) * 12 + 4 * i + c, 1)]
                            if tap == 0:
                                dve.wait_ge(lin_read[c], r0 + i + 1)
                                own.done(v.tensor_scalar(acc, raw, w, None, ALU.mult))
                                continue
                            own.wait(own.n - 3 if tap < 3 else start + 9 + c)
                            ins = v.scalar_tensor_tensor(acc[:, :, tap:T], raw[:, :, 0:T - tap], w, acc[:, :, tap:T], ALU.mult, ALU.add)
                            if tap < 3:
                                own.done(ins)
                            else:
                                ins.then_inc(sem["conv"], 1)
                own.base, own.n = l * PER["dve_own"], start + 36
                with dve.Fori(3, 5) as i:
                    for s in range(2):
                        split_lo(dve, m0 + i + 1, s)
                dve.wait_ge(*read("tk", l))
                own.done(v.tensor_tensor(gx[:, :, :], ab[:, :, 0:4], bf(pc(K_DT, 4), 1, [P, 3, 4]), ALU.add))
                own.wait()
                v.scalar_tensor_tensor(gm[:, :, :], gx[:, :, :], -1.0, gx[:, :, :], ALU.mult, ALU.min).then_inc(sem["sp_in"], 1)
                own.done(v.tensor_scalar(iw[:, :, :], ab[:, :, 8:16], IDX_HEADS ** -0.5 * IDX_DIM ** -0.5, None, ALU.mult))
                dve.wait_ge(sem["sp_ln"], at("sp_ln", l, 1))
                own.done(v.scalar_tensor_tensor(gm[:, :, :], gx[:, :, :], 0.0, gl[:, :, :], ALU.max, ALU.add))
                own.wait()
                v.tensor_tensor(gg[:, :, :], gm[:, :, :], bf(pc(K_NA, 4), 1, [P, 3, 4]), ALU.mult).then_inc(sem["gt"], 1)
                own.done(v.tensor_scalar(bt[:, :, :], bt[:, :, :], 1.0, None, ALU.add))
                own.wait()
                v.reciprocal(beta[:, :, :], bt[:, :, :]).then_inc(sem["beta"], 1)
                dve.wait_ge(sem["rn"], at("rn", l, 1))
                v.tensor_tensor(cT[:, 0:4, :], cT[:, 0:4, :], rnq[:, :, :], ALU.mult).then_inc(sem["qk_unit"], 1)
                dve.wait_ge(sem["rn"], at("rn", l, 2))
                v.tensor_tensor(cT[:, 4:8, :], cT[:, 4:8, :], rnk[:, :, :], ALU.mult).then_inc(sem["qk_unit"], 1)
                own.wait()
                dve.wait_ge(sem["rn"], at("rn", l, 4))
                v.scalar_tensor_tensor(rawT[:, 16:20, :], rawT[:, 16:20, :], pc(K_QN), rnb[:, 0:4, :], ALU.mult, ALU.mult).then_inc(sem["att_unit"], 1)
                v.scalar_tensor_tensor(bkr[:, :], bkr[:, :], pc(K_KN), rnb[:, 4, :], ALU.mult, ALU.mult).then_inc(sem["att_unit"], 1)
                v.scalar_tensor_tensor(ikr[:, :], ikr[:, :], pc(K_IN), rni[:, 0, :], ALU.mult, ALU.mult).then_inc(sem["att_unit"], 1)

                def gate_lo(i, slots=(0, 1)):
                    for s in slots:
                        dve.wait_ge(sem["panel_done"], 2 * (m0 + M_GATE + i) + s + 3)
                        for c in range(2):
                            b = 2 * s + c
                            v.tensor_scalar(rawT[:, 4 * i + b, :], lin[b][:, 0:T], pc(K_BG + 4 * i + b), GATE_LEAST, ALU.add, ALU.max).then_inc(lin_read[b], 1)

                dve.wait_ge(sem["conv"], at("conv", l, 12))
                gate_lo(0, [0])
                dve.wait_ge(sem["eg"], at("eg", l, 1))
                own.done(v.tensor_scalar(egt[:, :, :], egt[:, :, :], -1.0, None, ALU.mult))
                dve.wait_ge(*read("gc", l))
                def decays(b):
                    n = TB[b][1]
                    ps = bank(f"gb{b}")
                    dve.wait_ge(*full(f"gb{b}", l))
                    dve.wait_ge(sem["eg"], at("eg", l, 2 + b))
                    for h in range(4):
                        v.tensor_scalar(decay[b][:, h, :], ps[0:n, h * n:(h + 1) * n], gcs[0:n, b, h:h + 1], 0.0, ALU.subtract, ALU.min)
                    v.tensor_tensor(kdx[0:n, b, :], ps[0:n, n - 1:4 * n:n], gcs[0:n, b, :], ALU.subtract).then_inc(emptied(f"gb{b}"), 1)
                    dve.wait_ge(sem["dec"], at("dec", l, b + 1))
                    own.done(v.tensor_tensor(decay[b], decay[b], bf(const("upto", n, n), 1, [n, 4, n]), ALU.mult))
                    own.wait()
                    dve.wait_ge(*full(f"bb{b}", l))
                    v.tensor_tensor(MT[b], bank(f"bb{b}")[0:n, 0:4 * n].rearrange("p (h c) -> p h c", h=4), decay[b], ALU.mult).then_inc(emptied(f"bb{b}"), 1)

                def keys_and_queries(b):
                    n = TB[b][1]
                    dve.wait_ge(*full(f"kk{b}", l))
                    dve.wait_ge(*read(f"bb{b}", l))
                    v.tensor_tensor(MT[b], bank(f"kk{b}")[0:n, 0:4 * n].rearrange("p (h c) -> p h c", h=4), MT[b], ALU.mult).then_inc(emptied(f"kk{b}"), 1)
                    dve.wait_ge(*full(f"qk{b}", l))
                    v.tensor_tensor(QD[b], bank(f"qk{b}")[0:n, 0:4 * n].rearrange("p (h c) -> p h c", h=4), decay[b], ALU.mult).then_inc(emptied(f"qk{b}"), 1)

                decays(0)
                decays(1)
                keys_and_queries(0)
                gate_lo(0, [1])
                decays(2)
                keys_and_queries(1)
                keys_and_queries(2)
                for b in range(3):
                    own.done(v.tensor_copy(sdec[:, b, :], eg[:, :, TB[b][0] + TB[b][1] - 1]))
                dve.wait_ge(sem["kdx"], at("kdx", l, 1))
                for b in range(3):
                    n = TB[b][1]
                    dve.wait_ge(*full(f"kt{b}", l))
                    v.tensor_tensor(kd[0:n, b], bank(f"kt{b}")[0:n, :].rearrange("p (h d) -> p h d", h=4), bf(kdx[0:n, b, :], 2, [n, 4, P]), ALU.mult).then_inc(emptied(f"kt{b}"), 1)
                def masked(b, it):
                    n = TB[b][1]
                    level = c1[0:n, ds(consts_at1["level0"] + it * P, n)]
                    v.tensor_tensor(ML[b], MT[b], bf(level, 1, [n, 4, n]), ALU.mult).then_inc(sem["ml"], 1)

                for n, (names, kind, x) in enumerate((
                    (["rk"], "a", bkr[:, :].unsqueeze(1)), (["rik"], "i", ikr[:, :].unsqueeze(1)),
                    ([f"rq{h}" for h in range(4)], "a", rawT[:, 16:20, :]), ([f"ri{c}" for c in range(4)], "i", rawT[:, 20:24, :]),
                )):
                    if n:
                        dve.wait_ge(sem["rope"], at("rope", l, n))
                    if n == 3:
                        for b in range(3):
                            masked(b, 0)
                    for c, name in enumerate(names):
                        dve.wait_ge(*full(name, l))
                        v.tensor_tensor(tmp4[:, c, :], bank(name)[:, 0:T], const("sin_" + kind, T), ALU.mult).then_inc(emptied(name), 1)
                    dve.wait_ge(*read(names[-1], l))
                    dve.wait_ge(sem["rope_cos"], at("rope_cos", l, n + 1))
                    v.tensor_tensor(x, x, tmp4[:, 0:len(names), :], ALU.add).then_inc(sem["rope"], 1)
                gate_lo(1, [0])
                dve.wait_ge(sem["ml"], at("ml", l, 1))
                own.done(v.tensor_tensor(A[0], bf(ident[0:META, 0:META], 1, [META, 4, META]), ML[0], ALU.subtract))
                for b in range(3):
                    n, name = TB[b][1], f"Y{b}_0"
                    dve.wait_ge(*full(name, l))
                    v.tensor_tensor(X[b], bf(ident[0:n, 0:n], 1, [n, 4, n]), bank(name)[0:n, 0:4 * n].rearrange("p (h c) -> p h c", h=4), ALU.subtract).then_inc(emptied(name), 1)
                    own.wait()
                    masked(b, 1)
                for j in range(2):
                    wide = (j + 1) * P
                    if j:
                        gate_lo(1, [1])
                    for e, heads in enumerate(IX_HEADS[j]):
                        dve.wait_ge(*read(f"ix{j}{e}", l))
                        for n, h in enumerate(heads):
                            r, w = rl[:, e % 2, n * wide:(n + 1) * wide], iw[:, j + 1, h:h + 1]
                            if e + n == 0:
                                ins = v.tensor_scalar(score[:, j, 0:wide], r, w, None, ALU.mult)
                            else:
                                if n == 0:
                                    dve.wait_ge(sem["score"], at("score", l, 2 * j + e))
                                else:
                                    own.wait()
                                ins = v.scalar_tensor_tensor(score[:, j, 0:wide], r, w, score[:, j, 0:wide], ALU.mult, ALU.add)
                            if h != heads[-1]:
                                own.done(ins)
                            else:
                                ins.then_inc(sem["score"], 1)
                    dve.wait_ge(sem["score"], at("score", l, 2 + 4 * j))
                    barred = consts_at1[f"barred{j}"]
                    own.done(v.tensor_tensor(work[:, j, 0:wide], score[:, j, 0:wide], c1[:, barred:barred + wide], ALU.add))

                def take_eight(before):
                    n0 = own.n
                    for j in range(2):
                        own.wait(before + j)
                        stand(dve, "dve_stood")
                        own.done(v.max(m8[:, j, :], work[:, j, 0:(j + 1) * P]))
                    for j in range(2):
                        own.wait(n0 + 1 + j)
                        stand(dve, "dve_stood")
                        x = work[:, j, 0:(j + 1) * P]
                        own.done(v.match_replace(x, m8[:, j, :], x, TAKEN))

                def less(m, ps, name):
                    v.tensor_tensor(m, m, ps.rearrange("p (h c) -> p h c", h=4), ALU.subtract).then_inc(emptied(name), 1)

                start = own.n
                with dve.Fori(0, LEVELS - 2) as it:
                    own.base, own.n = l * PER["dve_own"] + 4 * it, start
                    for b in range(3):
                        dve.wait_ge(*full(f"Y{b}", l, it))
                        masked(b, it + 2)
                    dve.wait_ge(*full("XA0", l, it))
                    v.tensor_tensor(X[0], X[0], bank("XA0")[0:META, 0:4 * META].rearrange("p (h c) -> p h c", h=4), ALU.subtract)
                    less(A[0], bank("XA0")[0:META, 4 * META:8 * META], "XA0")
                    for b in (1, 2):
                        dve.wait_ge(*full(f"X{b}", l, it))
                        less(X[b], bank(f"X{b}")[:, :], f"X{b}")
                    take_eight(start - 1)
                own.base, own.n = l * PER["dve_own"], start + 4 * (LEVELS - 2)
                for _ in range(2):
                    take_eight(own.n - 1)
                dve.wait_ge(*read("XA0", l, LEVELS - 3))
                v.tensor_tensor(A[0], A[0], bf(beta[0:META, 0, :], 2, [META, 4, META]), ALU.mult).then_inc(sem["ab_ready"], 1)
                def greatest(j):
                    n = P if j else META
                    if j:
                        own.wait()
                        for h in range(4):
                            name = f"s{'abcd'[h]}{j}"
                            dve.wait_ge(*full(name, l))
                            v.tensor_tensor(Pm[:, h, 0:KEYS[j]], bank(name)[:, 0:KEYS[j]], bias[:, j - 1, 0:KEYS[j]], ALU.add).then_inc(emptied(name), 1)
                        dve.wait_ge(*read(f"sd{j}", l))
                        own.done(v.tensor_reduce(mx[:, j, :], Pm[:, :, 0:KEYS[j]], AX, ALU.max))
                    else:
                        dve.wait_ge(*full("s0", l))
                        own.done(v.tensor_reduce(mx[0:META, 0, :], bank("s0")[0:META, 0:4 * META].rearrange("p (h k) -> p h k", h=4), AX, ALU.max))
                    own.wait()
                    v.tensor_scalar(nmx[0:n, j, :], mx[0:n, j, :], -(P ** -0.5), None, ALU.mult).then_inc(sem["nmx"], 1)

                greatest(0)
                for b in (1, 2):
                    dve.wait_ge(*full(f"A{b}", l))
                    less(A[b], bank(f"A{b}")[:, :], f"A{b}")
                    dve.wait_ge(*read(f"A{b}", l))
                    v.tensor_tensor(A[b], A[b], bf(beta[:, b, :], 2, [P, 4, P]), ALU.mult).then_inc(sem["ab_ready"], 1)
                take_eight(own.n - 1)
                own.wait()
                for j in range(2):
                    own.done(v.tensor_scalar(bias[:, j, META:KEYS[j + 1]], work[:, j, 0:(j + 1) * P], 0.5 * (INVALID + TAKEN), -BIG, ALU.is_gt, ALU.mult))

                def normed(j):
                    n, x = (P, Pm[:, :, 0:KEYS[j]]) if j else (META, P0[:, :, :])
                    if j:
                        dve.wait_ge(sem["soft"], at("soft", l, j))
                    else:
                        dve.wait_ge(*read("s0", l))
                    own.done(v.reciprocal(rsm[0:n, j, :], sm[0:n, j, :]))
                    own.wait()
                    v.tensor_tensor(x, x, bf(rsm[0:n, j, :], 2, [n, 4, KEYS[j]]), ALU.mult).then_inc(sem["pn"], 1)

                def out_lo(j):
                    dve.wait_ge(sem["ob_h"], at("ob_h", l, 1 + j))
                    v.tensor_tensor(oL[:, 4:8, tok(j)], bank(f"pv{j}")[:, 0:4 * TB[j][1]].rearrange("p (h c) -> p h c", h=4),
                                    oH[:, 4:8, tok(j)].bitcast(F32), ALU.subtract).then_inc(emptied(f"pv{j}"), 1)

                def state(b):
                    ps = bank(f"dS{b}")
                    dve.wait_ge(*full(f"dS{b}", l))
                    if b == 0:
                        v.tensor_copy(S[:, :, :], ps[:, :].rearrange("p (h d) -> p h d", h=4)).then_inc(emptied("dS0"), 1)
                        return
                    for h in range(4):
                        ins = v.scalar_tensor_tensor(S[:, h, :], S[:, h, :], sdec[:, b, h:h + 1], ps[:, h * P:(h + 1) * P], ALU.mult, ALU.add)
                    ins.then_inc(emptied(f"dS{b}"), 1)

                def unseen_values(b):
                    ps = bank(f"kS{b}")
                    dve.wait_ge(*full(f"kS{b}", l))
                    for h in range(4):
                        ins = v.scalar_tensor_tensor(R[:, h, :], ps[:, h * P:(h + 1) * P], egt[:, b, h:h + 1], vt[:, b, h, :], ALU.mult, ALU.add)
                    ins.then_inc(emptied(f"kS{b}"), 1)

                def gated(b):
                    dve.wait_ge(*read(f"o{b}", l))
                    own.done(v.scalar_tensor_tensor(zT[:, :, tok(b)], oA[:, :, tok(b)], pc(K_ANORM), zT[:, :, tok(b)], ALU.mult, ALU.mult))

                dve.wait_ge(lin_read[3], r0 + 4)
                greatest(1)
                normed(0)
                normed(1)
                gate_lo(2, [0])
                state(0)
                gate_lo(2, [1])
                unseen_values(1)
                out_lo(0)
                gate_lo(3, [0])
                greatest(2)
                gated(0)
                state(1)
                normed(2)
                out_lo(1)
                unseen_values(2)
                gated(1)
                gated(2)
                out_lo(2)
                own.wait()
                for h in range(4):
                    dve.wait_ge(sem["rno"], at("rno", l, h + 1))
                    v.tensor_tensor(zT[:, h, :], zT[:, h, :], rno[:, h, :], ALU.mult).then_inc(sem["oa"], 1)
                for h in range(4):
                    dve.wait_ge(sem["oa_h"], at("oa_h", l, h + 1))
                    v.tensor_tensor(oL[:, h, :], zT[:, h, :], oH[:, h, :].bitcast(F32), ALU.subtract).then_inc(sem["oa_l"], 1)
                gate_lo(3, [1])
                dve.wait_ge(sem["wlo"], 4 * (m0 + M_BRANCH) + 4)
                for s in range(2):
                    split_lo(dve, m0 + M_BRANCH, s)
                dve.wait_ge(sem["gates"], at("gates", l, 12))
                stand(dve, "dve_stood")
                with dve.Fori(0, 2) as i:
                    for s in range(2):
                        dve.wait_ge(sem["panel_done"], 2 * (m0 + M_BRANCH + i) + s + 3)
                        banks = [bank(f"br{b}") if s else lin[b] for b in range(4)]
                        free = [emptied(f"br{b}") if s else lin_read[b] for b in range(4)]
                        for c in range(2):
                            q = 4 * i + 2 * s + c
                            v.tensor_tensor(yT[:, ds(q, 1), :], banks[2 + c][:, 0:T].unsqueeze(1), rawT[:, ds(q, 1), :], ALU.mult).then_inc(free[2 + c], 1)
                            v.tensor_tensor(ytmp[:, c, :].unsqueeze(1), banks[c][:, 0:T].unsqueeze(1), rawT[:, ds(8 + q, 1), :], ALU.mult).then_inc(free[c], 1)
                        for c in range(2):
                            q = 4 * i + 2 * s + c
                            dve.wait_ge(*(read(f"br{c}", l, i) if s else (lin_read[c], r0 + R_BRANCH + i + 1)))
                            v.tensor_tensor(yT[:, ds(q, 1), :], yT[:, ds(q, 1), :], ytmp[:, c, :].unsqueeze(1), ALU.add).then_inc(sem["y"], 1)
                        split_lo(dve, m0 + M_BRANCH + i + 1, s)
                        two = ds(4 * i + 2 * s, 2)
                        dve.wait_ge(sem["yh"], at("yh", l, 2 * i + s + 1))
                        v.tensor_tensor(nL[:, two, :], yT[:, two, :], nH[:, two, :].bitcast(F32), ALU.subtract).then_inc(sem["yl"], 1)
                with dve.Fori(0, 2) as i:
                    for s in range(2):
                        dve.wait_ge(sem["panel_done"], 2 * (m0 + M_OUT + i) + s + 3)
                        for c in range(2):
                            x = hT[:, ds(4 * i + 2 * s + c, 1), :]
                            v.tensor_tensor(x, x, lin[2 * s + c][:, 0:T].unsqueeze(1), ALU.add).then_inc(lin_read[2 * s + c], 1)
                        split_lo(dve, m0 + M_OUT + i + 1, s)
                norm(l, 2, K_NORM2)
                with dve.Fori(0, 11) as i:
                    m, r = m0 + M_UP + i, r0 + R_UP + i
                    own.base = l * PER["dve_own"] + i * 2
                    n0 = own.n
                    for c in range(2):
                        dve.wait_ge(sem["tap"], at("tap", l, 2 * i + c + 1))
                        own.done(v.scalar_tensor_tensor(u[:, c, 1:T], lin[c][:, 0:T - 1], parL[:, ds(K_FCONV + FC + 2 * i + c, 1)], u[:, c, 1:T], ALU.mult, ALU.add))
                    for c in range(2):
                        own.wait(n0 + c + 1)
                        v.scalar_tensor_tensor(u[:, c, 2:T], lin[c][:, 0:T - 2], parL[:, ds(K_FCONV + 2 * i + c, 1)], u[:, c, 2:T], ALU.mult, ALU.add).then_inc(lin_read[c], 1)
                    split_lo(dve, m + 1, 0)
                    dve.wait_ge(sem["panel_done"], 2 * m + 4)
                    for c in range(2):
                        dve.wait_ge(sem["gate_silu"], at("gate_silu", l, 2 * i + c + 1))
                        v.tensor_tensor(av[:, c, :], lin[2 + c][:, 0:T], sg[:, c, :], ALU.mult).then_inc(lin_read[2 + c], 1)
                    split_lo(dve, m + 1, 1)
                    for c in range(2):
                        dve.wait_ge(sem["ah"], at("ah", l, 2 * i + c + 1))
                        q = ds(2 * i + c, 1)
                        v.tensor_tensor(aL[:, q, :], av[:, c, :].unsqueeze(1), aH[:, q, :].bitcast(F32), ALU.subtract).then_inc(sem["al"], 1)
                own.base, own.n = l * PER["dve_own"], n0 + 22
                with dve.Fori(0, 2) as i:
                    for p in range(6):
                        m = m0 + M_DOWN + 3 * i + p // 2
                        if p % 3 == 2:
                            dve.wait_ge(sem["panel_done"], 2 * m + p % 2 + 3)
                            for c in range(2):
                                b = 2 * (p // 3) + c
                                x = hT[:, ds(4 * i + b, 1), :]
                                v.tensor_tensor(x, x, lin[b][:, 0:T].unsqueeze(1), ALU.add).then_inc(lin_read[b], 1)
                        split_lo(dve, m + 1, p % 2)
                assert own.n == PER["dve_own"], own.n

            with dve.Fori(0, DEPTH) as l:
                layer(l)

            L = DEPTH
            own.base, own.n = L * PER["dve_own"], 0
            h2 = hT[:, :, META:T]

            def norm2(which, gains):
                dve.wait_ge(sem["rstd2"], which)
                for c in range(2):
                    ins = v.scalar_tensor_tensor(nH[:, c, 0:SEQ], h2[:, c, :], gains(c), rs[:, 0:SEQ], ALU.mult, ALU.mult)
                ins.then_inc(sem["nh2"], 1)
                for c in (*range(2, DC), 0, 1):
                    v.scalar_tensor_tensor(nT2[:, c, :], h2[:, c, :], gains(c), rs[:, 0:SEQ], ALU.mult, ALU.mult).then_inc(sem["n2"], 1)
                dve.wait_ge(sem["n2"], DC * which)
                for pair in range(DC // 2):
                    dve.wait_ge(sem["nh2"], 4 * (which - 1) + pair + 1)
                    gs = slice(2 * pair, 2 * pair + 2)
                    v.tensor_tensor(nL[:, gs, 0:SEQ], nT2[:, gs, :], nH[:, gs, 0:SEQ].bitcast(F32), ALU.subtract).then_inc(sem["nl2"], 1)

            def los(m, pairs):
                with dve.Fori(0, pairs) as i:
                    for s in range(2):
                        split_lo(dve, m + i + 1, s)

            def add_h(chunk, b):
                x = hT[:, ds(chunk, 1), META:T]
                v.tensor_tensor(x, x, lin[b][:, 0:SEQ].unsqueeze(1), ALU.add).then_inc(lin_read[b], 1)

            def mlp2(j, m, r, last):
                norm2(2 * j + 2, lambda c: p2(j, (KE_FN, KO_FN)[j] + c))
                n0 = own.n

                def left(i):
                    for c in range(2):
                        dve.wait_ge(sem["ah2"], j * FC + 2 * i + c + 1)
                        q = ds(2 * i + c, 1)
                        v.tensor_tensor(aL2[:, q, :], av2[:, c, :].unsqueeze(1), aH2[:, q, :].bitcast(F32), ALU.subtract).then_inc(sem["al2"], 1)

                def up(i, first):
                    own.base, own.n = L * PER["dve_own"] + i * 4, n0
                    for s in range(2):
                        for c in range(2):
                            q = 2 * s + c
                            w = par[:, DEPTH + j, ds(P + 2 * FC + s * FC + 2 * i + c, 1)]
                            dve.wait_ge(sem["tap2"], j * 2 * FC + 4 * i + q + 1)
                            own.done(v.scalar_tensor_tensor(u2[:, q, 1:SEQ], lin[q][:, 0:SEQ - 1], w, u2[:, q, 1:SEQ], ALU.mult, ALU.add))
                        for c in range(2):
                            q = 2 * s + c
                            w = par[:, DEPTH + j, ds(P + s * FC + 2 * i + c, 1)]
                            own.wait(n0 + q + 1)
                            v.scalar_tensor_tensor(u2[:, q, 2:SEQ], lin[q][:, 0:SEQ - 2], w, u2[:, q, 2:SEQ], ALU.mult, ALU.add).then_inc(lin_read[q], 1)
                        split_lo(dve, m + i + 1, s)
                        if s == 0 and not first:
                            left(i - 1)
                    for c in range(2):
                        dve.wait_ge(sem["silu2"], j * FC + 2 * i + c + 1)
                        dve.wait_ge(lin_read[2 + c], r + i + 1)
                        if not first:
                            dve.wait_ge(sem["al2"], j * FC + 2 * i)
                        v.tensor_tensor(av2[:, c, :], u2[:, 2 + c, :], sg2[:, c, :], ALU.mult).then_inc(sem["conv2"], 1)

                up(0, True)
                with dve.Fori(1, 11) as i:
                    up(i, False)
                left(10)
                own.base, own.n = L * PER["dve_own"], n0 + 44

                def down(i, last):
                    for p in range(6):
                        mp = m + 11 + 3 * i + p // 2
                        if p % 3 == 2:
                            dve.wait_ge(sem["panel_done"], 2 * mp + p % 2 + 3)
                            for c in range(2):
                                add_h(4 * i + 2 * (p // 3) + c, 2 * (p // 3) + c)
                        if not (last and p >= 4):
                            split_lo(dve, mp + 1, p % 2)

                if last:
                    for i in range(2):
                        down(i, i == 1)
                else:
                    with dve.Fori(0, 2) as i:
                        down(i, False)

            norm2(1, lambda c: p2(0, c))
            los(M_E, 2)

            def even_greatest(j):
                keys, x = (j + 1) * P, Pe if j else Pe0
                unseen = c2[:, consts_at2["unseen"] + j * SEQ:consts_at2["unseen"] + j * SEQ + keys]
                for e, heads in enumerate([(0, 2, 4, 6), (1, 3, 5, 7)] if j == 0 else [(0, 2), (1, 3), (4, 6), (5, 7)]):
                    name, n = f"e{j}{e}", len(heads)
                    dve.wait_ge(*full(name, L))
                    v.tensor_tensor(x[:, heads[0]:heads[-1] + 1:2, :], bank(name)[:, 0:n * keys].rearrange("p (h k) -> p h k", h=n),
                                    bf(unseen, 1, [P, n, keys]), ALU.add).then_inc(emptied(name), 1)
                for e in range(2 if j == 0 else 4):
                    dve.wait_ge(*read(f"e{j}{e}", L))
                own.done(v.tensor_reduce(mx8[:, j, :], x[:, :, :], AX, ALU.max))
                own.wait()
                v.tensor_scalar(nmx8[:, j, :], mx8[:, j, :], -0.125, None, ALU.mult).then_inc(sem["enmx"], 1)

            def even_normed(j):
                keys, x = (j + 1) * P, (Pe if j else Pe0)[:, :, :]
                count = c2[:, consts_at2["count"] + j * SEQ:consts_at2["count"] + j * SEQ + keys]
                dve.wait_ge(sem["esoft"], 1 + j)
                own.done(v.tensor_tensor(x, x, bf(count, 1, [P, 8, keys]), ALU.mult))
                own.wait()
                own.done(v.tensor_reduce(sm8[:, j, :], x, AX, ALU.add))
                own.wait()
                own.done(v.reciprocal(rsm8[:, j, :], sm8[:, j, :]))
                own.wait()
                v.tensor_tensor(x, x, bf(rsm8[:, j, :], 2, [P, 8, keys]), ALU.mult).then_inc(sem["epn"], 1)

            def even_out_lo(j):
                ts = slice(j * P, j * P + P)
                dve.wait_ge(sem["eob_h"], 1 + j)
                v.tensor_tensor(eL[:, 0:4, ts], bank(f"ev{j}")[:, :].rearrange("p (c t) -> p c t", c=4), eH[:, 0:4, ts].bitcast(F32),
                                ALU.subtract).then_inc(emptied(f"ev{j}"), 1)

            def times_gate_c(s):
                dve.wait_ge(sem["panel_done"], 2 * (M_E + 3) + s + 3)
                for c in range(2):
                    b = 2 * s + c
                    dve.wait_ge(lin_read[b], R_E + 3)
                    v.tensor_tensor(ght[:, b, :], lin[b][:, 0:SEQ], ght[:, b, :], ALU.mult).then_inc(lin_read[b], 1)

            def times_gate_b(s):
                dve.wait_ge(sem["panel_done"], 2 * (M_E + 5) + s + 3)
                for c in range(2):
                    b = 2 * s + c
                    v.tensor_tensor(cvt[:, b, :], lin[b][:, 0:SEQ], cvt[:, b, :], ALU.mult).then_inc(lin_read[b], 1)

            split_lo(dve, M_E + 3, 0)
            for n, gain in ((0, KE_QG), (1, KE_KG)):
                x = raw8[:, 4 * n:4 * n + 4, :]
                dve.wait_ge(sem["ern"], n + 1)
                v.scalar_tensor_tensor(x, x, p2(0, gain), rne[:, 4 * n:4 * n + 4, :], ALU.mult, ALU.mult).then_inc(sem["eunit"], 1)
            split_lo(dve, M_E + 3, 1)
            times_gate_c(0)
            split_lo(dve, M_E + 4, 0)
            dve.wait_ge(sem["c2_in"], 16)
            even_greatest(0)
            even_greatest(1)
            even_normed(0)
            times_gate_c(1)
            split_lo(dve, M_E + 4, 1)
            even_normed(1)
            split_lo(dve, M_E + 5, 0)
            even_out_lo(0)
            for tap in range(3):
                for c in range(4):
                    w = p2(0, KE_SC + (2 - tap) * 4 + c)
                    if tap == 0:
                        dve.wait_ge(lin_read[c], R_E + 4)
                        own.done(v.tensor_scalar(cvt[:, c, :], ght[:, c, :], w, None, ALU.mult))
                    else:
                        own.wait(own.n - 3)
                        own.done(v.scalar_tensor_tensor(cvt[:, c, tap:SEQ], ght[:, c, 0:SEQ - tap], w, cvt[:, c, tap:SEQ], ALU.mult, ALU.add))
            split_lo(dve, M_E + 5, 1)
            own.wait()
            times_gate_b(0)
            split_lo(dve, M_E + 6, 0)
            even_out_lo(1)
            for s in range(2):
                if s:
                    times_gate_b(1)
                dve.wait_ge(sem["eb_h"], s + 1)
                v.tensor_tensor(eL[:, 4 + 2 * s:6 + 2 * s, :], cvt[:, 2 * s:2 * s + 2, :], eH[:, 4 + 2 * s:6 + 2 * s, :].bitcast(F32), ALU.subtract).then_inc(sem["eb_l"], 1)
            split_lo(dve, M_E + 6, 1)
            with dve.Fori(0, 2) as i:
                for s in range(2):
                    dve.wait_ge(sem["panel_done"], 2 * (M_E + E_OUT + i) + s + 3)
                    for c in range(2):
                        add_h(4 * i + 2 * s + c, 2 * s + c)
                    split_lo(dve, M_E + E_OUT + i + 1, s)
            mlp2(0, M_E + E_UP, R_E + E_UP, False)

            norm2(3, lambda c: p2(1, c))

            def rotate(n, rnd):
                x = [qk2[:, n, :, d, :] for d in range(2)]
                cos, sin = (bf(table2(name, SEQ), 1, [P, 4, SEQ]) for name in ("cos_r", "sin_r"))
                for b in range(4):
                    dve.wait_ge(lin_read[b], rnd)
                if n:
                    dve.wait_ge(sem["orot"], 2)
                for d in range(2):
                    own.done(v.tensor_tensor(tsin[:, d], x[d], sin, ALU.mult))
                own.wait()
                for d in range(2):
                    own.done(v.tensor_tensor(x[d], x[d], cos, ALU.mult))
                own.wait()
                v.tensor_tensor(x[0], x[0], tsin[:, 1], ALU.subtract).then_inc(sem["orot"], 1)
                v.tensor_tensor(x[1], x[1], tsin[:, 0], ALU.add).then_inc(sem["orot"], 1)

            los(M_O, 2)
            los(M_O + O_K, 1)
            rotate(0, R_O + O_K)
            los(M_O + O_K + 1, 2)
            rotate(1, R_O + O_V)
            def centre(h):
                x = vtk2[:, :, ds(h * 512, 512)]
                own.wait()
                for b in range(4):
                    dve.wait_ge(lin_read[b], R_O + O_V + h + 1)
                own.done(v.tensor_reduce(vmean[:, :], x, AX, ALU.add))
                own.wait()
                own.done(v.tensor_scalar(vmean[:, :], vmean[:, :], 1.0 / 512, None, ALU.mult))
                own.wait()
                own.done(v.tensor_tensor(x, x, bf(vmean[:, :], 2, [P, 2, 512]), ALU.subtract))

            n0 = own.n
            with dve.Fori(0, 3) as i:
                own.base, own.n = L * PER["dve_own"] + 3 * i, n0
                split_lo(dve, M_O + O_V + i + 2, 0)
                centre(i)
                split_lo(dve, M_O + O_V + i + 2, 1)
            own.base, own.n = L * PER["dve_own"], n0 + 9
            centre(3)
            for h in range(4):
                dve.wait_ge(*full(f"os{h}", L))
                v.tensor_tensor(sc[:, h, :], bank(f"os{h}")[:, 0:384], table2(f"decay{h}", 384), ALU.mult).then_inc(emptied(f"os{h}"), 1)
            for s in range(2):
                split_lo(dve, M_O + O_G + 1, s)

            def odd_normed(h):
                dve.wait_ge(sem["ovar"], h + 1)
                for e in range(4):
                    c = 4 * h + e
                    own.done(v.scalar_tensor_tensor(oR[:, c, :], oR[:, c, :], p2(1, KO_GN + c), rn4[:, h, :], ALU.mult, ALU.mult))

            def odd_gate(h):
                own.wait()
                cs = slice(4 * h, 4 * h + 4)
                for b in range(4):
                    dve.wait_ge(lin_read[b], R_O + O_G + h + 1)
                v.tensor_tensor(oR[:, cs, :], oR[:, cs, :], sgT[:, cs, :], ALU.mult).then_inc(sem["ogate"], 1)

            def odd_lo(h):
                cs = slice(4 * h, 4 * h + 4)
                dve.wait_ge(sem["og_h"], h + 1)
                v.tensor_tensor(gL[:, cs, :], oR[:, cs, :], gH[:, cs, :].bitcast(F32), ALU.subtract).then_inc(sem["og_l"], 1)

            odd_normed(0)
            odd_normed(1)
            split_lo(dve, M_O + O_G + 2, 0)
            odd_normed(2)
            odd_normed(3)
            odd_gate(0)
            split_lo(dve, M_O + O_G + 2, 1)
            odd_gate(1)
            odd_lo(0)
            split_lo(dve, M_O + O_G + 3, 0)
            odd_lo(1)
            split_lo(dve, M_O + O_G + 3, 1)
            odd_gate(2)
            split_lo(dve, M_O + O_OUT, 0)
            odd_lo(2)
            odd_gate(3)
            split_lo(dve, M_O + O_OUT, 1)
            odd_lo(3)
            with dve.Fori(0, 2) as i:
                for q in range(2):
                    m = M_O + O_OUT + 2 * i + q
                    split_lo(dve, m + 1, 0)
                    dve.wait_ge(sem["panel_done"], 2 * m + 4)
                    for c in range(2):
                        add_h(4 * i + 2 * q + c, 2 * q + c)
                    split_lo(dve, m + 1, 1)
            mlp2(1, M_O + O_UP, R_O + RO_UP, True)


def kernel(**inputs):
    import numpy as _np
    import concourse.bacc as _bacc
    from concourse import mybir as _mybir
    from concourse.bass_utils import run_bass_kernel_spmd as _run

    nc = _bacc.Bacc("TRN2", target_bir_lowering=False, num_devices=1)
    arrays, a = {}, {}
    tables = constants()
    given = {name: _np.ascontiguousarray(inputs[name]) for name in INPUTS}
    for name, x in (*given.items(), *tables["arrays"].items()):
        arrays[f"in_{name}"] = x
        a[name] = nc.dram_tensor(f"in_{name}", x.shape, _mybir.dt.from_np(x.dtype), kind="ExternalInput").ap()
    out = nc.dram_tensor("out", (1, SEQ, D), _mybir.dt.float32, kind="ExternalOutput").ap()
    build(nc, a, tables["places"], out.rearrange("b t d -> (b t) d"))
    r = _run(nc, [arrays], core_ids=[0])
    return r.results[0]["out"]
```
